# Optimizing a Trainium2 kernel written in Bass

```python
import jax, jax.numpy as jnp
from jax import lax
import numpy as np

D_MODEL = 1024
BATCH = 1
SEQ = 2048
DEPTH = 1
DEC_BATCH = 8
DEC_SEQ = 8
PAST_LEN = 16384
PAGE_SIZE = 128

MIX_WIDTH = D_MODEL
CONV_WIDTH = MIX_WIDTH // 2
CONV_GROUPS = 8
CONV_K = 3
M_WIDTH = MIX_WIDTH - CONV_WIDTH
M_HEADS = 4
HEAD_DIM = M_WIDTH // M_HEADS
N_META = 16
CHUNK = 128
EPS = 1e-6
PROJ_SPLITS = [CONV_WIDTH, CONV_WIDTH, CONV_WIDTH, CONV_WIDTH,
               M_WIDTH, M_WIDTH, M_WIDTH, M_WIDTH, M_WIDTH,
               M_HEADS, M_HEADS]
PROJ_WIDTH = sum(PROJ_SPLITS)

kernel_name = 'hymba_conv_mlstm_decode_step'

def rmsnorm(x, g):
    xf = x.astype(jnp.float32)
    y = xf * lax.rsqrt(jnp.mean(xf * xf, axis=-1, keepdims=True) + EPS)
    return (y * g.astype(jnp.float32)).astype(x.dtype)

def short_conv(u, buf, w):
    T = u.shape[1]
    ucat = jnp.concatenate([buf.astype(u.dtype), u], axis=1)
    y = w[0] * ucat[:, 0:T]
    for j in range(1, CONV_K):
        y = y + w[j] * ucat[:, j:j + T]
    return y, ucat[:, -(CONV_K - 1):]

def mlstm_chunk(q, k, v, ig, lf, c_prev, n_prev, m_prev):
    L = q.shape[2]
    b = jnp.cumsum(lf, axis=-1)
    causal = jnp.tril(jnp.ones((L, L), dtype=bool))
    log_d = jnp.where(causal, b[..., :, None] - b[..., None, :] + ig[..., None, :], -jnp.inf)
    m_inter = b + m_prev[..., None]
    m_t = jnp.maximum(m_inter, jnp.max(log_d, axis=-1))
    d = jnp.exp(log_d - m_t[..., None])
    inter = jnp.exp(m_inter - m_t)
    s = jnp.einsum('bhjd,bhsd->bhjs', q, k) * d
    num = jnp.einsum('bhjs,bhsv->bhjv', s, v) + inter[..., None] * jnp.einsum('bhjd,bhdv->bhjv', q, c_prev)
    den = jnp.sum(s, axis=-1) + inter * jnp.einsum('bhjd,bhd->bhj', q, n_prev)
    h = num / jnp.maximum(jnp.abs(den), jnp.exp(-m_t))[..., None]
    m_new = m_t[..., -1]
    w_last = jnp.exp(log_d[..., -1, :] - m_new[..., None])
    decay = inter[..., -1]
    c_new = decay[..., None, None] * c_prev + jnp.einsum('bhs,bhsd,bhsv->bhdv', w_last, k, v)
    n_new = decay[..., None] * n_prev + jnp.einsum('bhs,bhsd->bhd', w_last, k)
    return h, (c_new, n_new, m_new)

def mlstm_seq(q, k, v, ig, lf, state):
    B, H, T, D = q.shape
    nf = T // CHUNK
    hs = []
    if nf > 0:
        def to_chunks(a):
            a = a[:, :, :nf * CHUNK]
            a = a.reshape(a.shape[:2] + (nf, CHUNK) + a.shape[3:])
            return jnp.moveaxis(a, 2, 0)

        def body(carry, xs):
            qc, kc, vc, ic, fc = xs
            h, new = mlstm_chunk(qc, kc, vc, ic, fc, *carry)
            return new, h

        state, hc = lax.scan(body, state, tuple(to_chunks(a) for a in (q, k, v, ig, lf)))
        hs.append(jnp.moveaxis(hc, 0, 2).reshape(B, H, nf * CHUNK, D))
    if T % CHUNK:
        s0 = nf * CHUNK
        h, state = mlstm_chunk(q[:, :, s0:], k[:, :, s0:], v[:, :, s0:], ig[:, :, s0:], lf[:, :, s0:], *state)
        hs.append(h)
    h = hs[0] if len(hs) == 1 else jnp.concatenate(hs, axis=2)
    return h, state

def mixer_layer(x, conv_buf, c0, n0, m0, lead, norm_gain, w_in, conv_w, b_igate, b_fgate, mh_norm_gain, w_out):
    B, T, _ = x.shape
    xn = rmsnorm(x, norm_gain)
    proj = jnp.einsum('btd,dp->btp', xn, w_in)
    gb, gc, hc, zc, q, k, v, o, zm, ig, fg = jnp.split(proj, np.cumsum(PROJ_SPLITS)[:-1].tolist(), axis=-1)
    yc, conv_new = short_conv(gc * hc, conv_buf, conv_w)
    y_conv = gb * yc * jax.nn.silu(zc)
    def heads(a):
        return a.astype(jnp.float32).reshape(B, T, M_HEADS, HEAD_DIM).transpose(0, 2, 1, 3)
    qh, kh, vh = heads(q), heads(k) * (HEAD_DIM ** -0.5), heads(v)
    igh = (ig + b_igate).astype(jnp.float32).transpose(0, 2, 1)
    lfh = jax.nn.log_sigmoid((fg + b_fgate).astype(jnp.float32)).transpose(0, 2, 1)
    state = (c0.astype(jnp.float32), n0.astype(jnp.float32), m0.astype(jnp.float32))
    if lead > 0:
        h_lead, state = mlstm_chunk(qh[:, :, :lead], kh[:, :, :lead], vh[:, :, :lead],
                                    igh[:, :, :lead], lfh[:, :, :lead], *state)
        h_rest, state = mlstm_seq(qh[:, :, lead:], kh[:, :, lead:], vh[:, :, lead:],
                                  igh[:, :, lead:], lfh[:, :, lead:], state)
        h = jnp.concatenate([h_lead, h_rest], axis=2)
    else:
        h, state = mlstm_seq(qh, kh, vh, igh, lfh, state)
    h = h * lax.rsqrt(jnp.mean(h * h, axis=-1, keepdims=True) + EPS)
    h = h.transpose(0, 2, 1, 3).reshape(B, T, M_WIDTH) * mh_norm_gain.astype(jnp.float32)
    y_m = (h.astype(x.dtype) * jax.nn.sigmoid(o)) * jax.nn.silu(zm)
    out = jnp.einsum('btw,wd->btd', jnp.concatenate([y_conv, y_m], axis=-1), w_out)
    c_new, n_new, m_new = state
    return x + out, (conv_new, c_new.astype(x.dtype), n_new.astype(x.dtype), m_new.astype(x.dtype))

def setup_inputs(seed: int = 0) -> dict:
    key = jax.random.key(seed)
    ks = jax.random.split(key, 16)
    f32 = jnp.float32
    return {
        'x_prompt': jax.random.normal(ks[0], (BATCH, SEQ, D_MODEL), f32),
        'x_sample': jax.random.normal(ks[1], (DEC_BATCH, DEC_SEQ, D_MODEL), f32),
        'state_conv': jax.random.normal(ks[2], (DEC_BATCH, CONV_K - 1, CONV_WIDTH), f32),
        'state_mlstm_c': 0.5 * jax.random.normal(ks[3], (DEC_BATCH, M_HEADS, HEAD_DIM, HEAD_DIM), f32),
        'state_mlstm_n': 0.5 * jax.random.normal(ks[4], (DEC_BATCH, M_HEADS, HEAD_DIM), f32),
        'state_mlstm_m': jax.random.normal(ks[5], (DEC_BATCH, M_HEADS), f32),
        'meta_tokens': jax.random.normal(ks[6], (N_META, D_MODEL), f32),
        'norm_gain': 1.0 + 0.05 * jax.random.normal(ks[7], (D_MODEL,), f32),
        'w_in': jax.random.normal(ks[8], (D_MODEL, PROJ_WIDTH), f32) * D_MODEL ** -0.5,
        'conv_w': jax.random.normal(ks[9], (CONV_K, CONV_WIDTH), f32) * CONV_K ** -0.5,
        'b_igate': 0.1 * jax.random.normal(ks[10], (M_HEADS,), f32),
        'b_fgate': jnp.linspace(3.0, 6.0, M_HEADS, dtype=f32) + 0.1 * jax.random.normal(ks[11], (M_HEADS,), f32),
        'mh_norm_gain': 1.0 + 0.05 * jax.random.normal(ks[12], (M_WIDTH,), f32),
        'w_out': jax.random.normal(ks[13], (MIX_WIDTH, D_MODEL), f32) * MIX_WIDTH ** -0.5,
        'final_norm_gain': 1.0 + 0.05 * jax.random.normal(ks[14], (D_MODEL,), f32),
    }

def reference(x_prompt, x_sample, state_conv, state_mlstm_c, state_mlstm_n, state_mlstm_m,
              meta_tokens, norm_gain, w_in, conv_w, b_igate, b_fgate, mh_norm_gain, w_out, final_norm_gain):
    weights = (norm_gain, w_in, conv_w, b_igate, b_fgate, mh_norm_gain, w_out)
    Bp = x_prompt.shape[0]
    meta = jnp.broadcast_to(meta_tokens.astype(x_prompt.dtype)[None], (Bp, N_META, D_MODEL))
    xp = jnp.concatenate([meta, x_prompt], axis=1)
    conv0 = jnp.zeros((Bp, CONV_K - 1, CONV_WIDTH), x_prompt.dtype)
    c0 = jnp.zeros((Bp, M_HEADS, HEAD_DIM, HEAD_DIM), jnp.float32)
    n0 = jnp.zeros((Bp, M_HEADS, HEAD_DIM), jnp.float32)
    m0 = jnp.zeros((Bp, M_HEADS), jnp.float32)
    xs = x_sample
    cs, ns, ms, bs = state_mlstm_c, state_mlstm_n, state_mlstm_m, state_conv
    for _ in range(DEPTH):
        xp, (conv0, c0, n0, m0) = mixer_layer(xp, conv0, c0, n0, m0, N_META, *weights)
        xs, (bs, cs, ns, ms) = mixer_layer(xs, bs, cs, ns, ms, 0, *weights)
    y_prompt = rmsnorm(xp[:, N_META:], final_norm_gain)
    y_sample = rmsnorm(xs, final_norm_gain)
    return (y_prompt, y_sample, conv0, c0, n0, m0, bs, cs, ns, ms)


_drawn_inputs = setup_inputs


def setup_inputs(seed=0):
    import zlib

    import numpy as np

    out = dict(_drawn_inputs(seed))
    spreads = {}
    factors = {'meta_tokens': 2.695, 'mh_norm_gain': 5.424}
    for name, (base, spread) in spreads.items():
        noise = np.random.default_rng([zlib.crc32(name.encode()), seed]).standard_normal(out[name].shape)
        drawn = base * np.exp(spread * noise) if base else spread * noise
        out[name] = __import__('jax').numpy.asarray(drawn.astype(out[name].dtype))
    for name, factor in factors.items():
        out[name] = (out[name] * factor).astype(out[name].dtype)
    return out
```

```python
import concourse.bass as bass
from concourse import mybir
from contextlib import ExitStack

F32 = mybir.dt.float32
F16 = mybir.dt.float16
BF16 = mybir.dt.bfloat16
ALU = mybir.AluOpType
ACT = mybir.ActivationFunctionType

P = 128
D = 1024
KT = D // P
SEQ = 2048
META = 16
DB, DS = 8, 8
MIX = META + DB * DS
H = 4
CW = 512
NB, CH = 4, 4
BT = CH * P
NTOK = MIX + SEQ
EPS = 1e-6
NEG = -1.0e30
WS = 64.0
SK = float(P) ** -0.5
K, V, Q, GC, HC, GB, ZC, O, ZM = range(9)
NT = 9
TILE_COL = {GB: 0, GC: CW, HC: 2 * CW, ZC: 3 * CW, Q: 4 * CW, K: 5 * CW, V: 6 * CW, O: 7 * CW, ZM: 8 * CW}
IG_COL, FG_COL = 9 * CW, 9 * CW + H
GR = 32 + H
DV1 = P + 1
STAGES = 3
XBUF = 3
SEGS = [(0, META)] + [(META + DS * i, DS) for i in range(DB)]
SAMPLE_ROUNDS = [(0, 3), (3, 6), (6, 8)]

T0_PRO = 2 + 2 * CH
T1_PRO = 4
X_HALF = {HC: (1,), GB: (3,), ZC: (5, 6)}
X_END = {GC: (0,), HC: (2,), GB: (4,), ZC: (7,)}
DVE_TURN = 63
ACT_TURN = 13


def t0_uses(b, first):
    names = []
    for t in range(NT):
        names += [("mix", t)] if b == 0 else []
        names += {V: [] if first and b == 0 else ["hT"], Q: ["kT"], GC: ["vT"]}.get(t, [])
        names += [("x", r) for r in X_HALF.get(t, ()) + X_END.get(t, ())] if first else []
    return names


def t1_uses(b, first):
    names = []
    for t in range(NT):
        names += ["gates"] if first and t == O else []
        names += {Q: ["args"], GC: ["kv"], HC: ["score"], GB: ["num"], O: ["hT"]}.get(t, []) if b == 0 else []
        names += [("state", t - V)] if b == 1 and t in (V, Q, GC) else []
        names += ["cols"] if first and t == ZM else []
    return names


def ordinal(uses, before, g, b, name, first):
    turn = sum(len(uses(x, False)) for x in range(NB))
    start = before + sum(len(uses(x, True)) for x in range(NB - 1))
    if first:
        return before + sum(len(uses(x, True)) for x in range(b)) + uses(b, True).index(name)
    if b == NB - 1:
        return g * turn + (start + uses(b, False).index(name))
    inside = len(uses(NB - 1, False)) + sum(len(uses(x, False)) for x in range(b))
    return (g - 1) * turn + (start + inside + uses(b, False).index(name))


def t0(g, b, name, first):
    return ordinal(t0_uses, T0_PRO, g, b, name, first)


def t1(g, b, name, first):
    return ordinal(t1_uses, T1_PRO, g, b, name, first)


def tok0(b):
    return MIX + BT * b


def nth(g, b):
    return g * NB + b


class Order:

    def __init__(self, eng, sem, per_turn):
        self.eng, self.sem, self.per_turn, self.n, self.base, self.last = eng, sem, per_turn, 0, 0, None

    def did(self, instruction):
        instruction.then_inc(self.sem, 1)
        self.n += 1
        self.last = (self.sem, self.base + self.n)

    def mark(self, instruction, sem, value):
        self.last = (sem, value)

    def settle(self):
        if self.last:
            self.eng.wait_ge(*self.last)

    def after(self, op):
        def run(*operands, **named):
            self.settle()
            return op(*operands, **named)
        return run

    def enter(self, g):
        self.settle()
        self.start, self.base, self.last = self.n, (g - 1) * self.per_turn, None

    def leave(self, turns):
        assert self.n - self.start == self.per_turn, (self.sem, self.n - self.start, self.per_turn)
        self.base, self.last = (turns - 1) * self.per_turn, None


def build(nc, x_prompt, x_sample, state_conv, state_c, state_n, state_m, meta, norm_gain, w_in, conv_w,
          b_igate, b_fgate, mh_gain, w_out, final_gain, y_prompt, y_sample, conv_p, c_p, n_p, m_p,
          conv_s, c_s, n_s, m_s, y_mid):
    ctx = ExitStack()
    with ctx:
        ctx.enter_context(nc.allow_non_contiguous_dma(reason="small parameters and states"))

        def sb(name, shape, dt=F32):
            return ctx.enter_context(nc.sbuf_tensor(name, shape, dt))

        def sem(name):
            return ctx.enter_context(nc.semaphore(name))

        xTh, xTl = sb("xTh", [P, KT, NTOK], F16), sb("xTl", [P, KT, NTOK], F16)
        Wh, Wl = sb("Wh", [P, NT, KT, P], F16), sb("Wl", [P, NT, KT, P], F16)
        Wgh, Wgl = sb("Wgh", [P, KT, GR], F16), sb("Wgl", [P, KT, GR], F16)
        rows = sb("rows", [P, NTOK])
        cols = sb("cols", [P, 1 + NB * CH, 3, H])
        decs = sb("decs", [P, DB, H])
        Woh, Wol = xTh[:, :, 0:D], xTl[:, :, 0:D]
        ybuf = [x[:, :, D + META:D + META + BT].rearrange("p k (s t) -> p k s t", s=2) for x in (xTh, xTl)]
        wst = [sb(f"wst{i}", [P, KT, P]) for i in range(STAGES)]
        result = [w[:, :, :].rearrange("p k c -> p (k c)") for w in wst[0:2]]
        wgst = sb("wgst", [P, KT, 2 * H])
        xs = [sb(f"xs{i}", [P, D]) for i in range(XBUF)]
        junk = sb("junk", [P, D], F16)
        xtmp = [sb(f"xtmp{i}", [P, BT]) for i in range(2)]
        fgain = sb("fgain", [P, D])
        ident, ones = sb("ident", [P, P]), sb("ones", [P, P])
        identb, maskb = sb("identb", [P, P], BF16), sb("maskb", [P, P], BF16)
        mixmask = sb("mixmask", [MIX, MIX], BF16)
        segind = sb("segind", [MIX, DB])
        selh, seln = sb("selh", [P, H]), sb("seln", [P, H])
        gain, cwt, mhg = sb("gain", [P, KT]), sb("cwt", [P, H, 3]), sb("mhg", [P, H])
        biasg, halves = sb("biasg", [GR, 1]), sb("halves", [P, CH])
        gwork = sb("gwork", [64 + GR, BT])
        grow, trr = gwork[0:GR, :], gwork[64:64 + GR, :]
        gt, lf = fgain[0:H, 0:BT], fgain[0:H, BT:2 * BT]
        mst = sb("mst", [H, NB * CH + 2])
        sm0, smn = sb("sm0", [H, DB]), sb("smn", [H, DB])
        rl, drl = sb("rl", [H, DB]), sb("drl", [H, DB * H])
        rb, rbm = sb("rb", [68, BT]), sb("rbm", [68, MIX])
        kf, vf, qf = sb("kf", [P, BT]), sb("vf", [P, BT]), sb("qf", [P, BT])
        v1 = sb("v1", [P, CH, DV1])
        dp = sb("dp", [P, BT])
        eh = sb("eh", [P, BT])
        kw = sb("kw", [P, BT])
        u, gcs, yc, zs = sb("u", [P, BT + 2]), sb("gcs", [P, BT]), sb("yc", [P, BT]), sb("zs", [P, BT])
        tz, to, G = sb("tz", [P, BT]), sb("to", [P, BT]), sb("G", [P, BT])
        bcum, mrow = G[0:H, :], zs[0:H, :]
        sel, cn = sb("sel", [P, CH, 3]), sb("cn", [P, DV1])
        den, rec, hss, hms, hrs, hf = (sb(n, [P, CH]) for n in ("den", "rec", "hss", "hms", "hrs", "hf"))
        yst = sb("yst", [P, 2, 2, BT], F16)
        kfm, vfm, qfm, gcm, ycm, zsm, tzm, tom, Gm, ehm, ymm = (
            sb(n, [P, MIX]) for n in ("kfm", "vfm", "qfm", "gcm", "ycm", "zsm", "tzm", "tom", "Gm", "ehm", "ymm"))
        um = sb("um", [P, META + 2 + DB * (DS + 2)])
        dpm, kwm, hnm = sb("dpm", [MIX, MIX]), sb("kwm", [MIX, P]), sb("hnm", [MIX, P])
        v1m, v1x = sb("v1m", [MIX, DV1]), sb("v1x", [MIX, DB, DV1])
        qm = sb("qm", [P, DB * (MIX + DS)])
        cs = sb("cs", [P, DB, DV1])
        selm, dselm = sb("selm", [MIX, 2]), sb("dselm", [P, DB])
        hm = sb("hm", [MIX, 6])
        ystm = sb("ystm", [P, 2, 2, MIX], F16)
        nst, npo = sb("nst", [P, DB, H]), sb("npo", [P, H])
        cst, cpo = sb("cst", [P, H, DB * 2]), sb("cpo", [P, H, 2])
        ssx, msx, rsx = sb("ssx", [P, 17]), sb("msx", [P, 17]), sb("rsx", [P, 17])

        bank = [ctx.enter_context(nc.psum_tensor(f"bank{i}", [P, BT], F32)) for i in range(8)]
        PB, T0, T1, A, S, N = bank[0:2], bank[2], bank[3], bank[4], bank[5], bank[6:8]
        OUT = [bank[0:2], bank[4:6]]

        par_in, par2_in, gate_in, fg_in, cs_in = (sem(n) for n in ("par_in", "par2_in", "gate_in", "fg_in", "cs_in"))
        x_in = [sem(f"x_in{i}") for i in range(XBUF)]
        w_in_s = [sem(f"w_in{i}") for i in range(STAGES)]
        const, const2, bias_clear = sem("const"), sem("const2"), sem("bias_clear")
        w_high, w_low, g_high, g_low = sem("w_high"), sem("w_low"), sem("g_high"), sem("g_low")
        x_sq, x_ms, x_rs, x_scaled = sem("x_sq"), sem("x_ms"), sem("x_rs"), sem("x_scaled")
        x_high, x_low = sem("x_high"), sem("x_low")
        tile_done, p_free = sem("tile_done"), [sem("p0_free"), sem("p1_free")]
        t0_full, t0_free, t1_full, t1_free = sem("t0_full"), sem("t0_free"), sem("t1_full"), sem("t1_free")
        a_full, a_free, s_full, s_free = sem("a_full"), sem("a_free"), sem("s_full"), sem("s_free")
        e_full, e_ready, n_full, n_free = sem("e_full"), sem("e_ready"), sem("n_full"), sem("n_free")
        gate_rows, g_abs, g_exp, g_ln, rows_ready, cols_ready = (
            sem(n) for n in ("gate_rows", "g_abs", "g_exp", "g_ln", "rows_ready", "cols_ready"))
        rb_ready, q_scaled, gc_used = sem("rb_ready"), sem("q_scaled"), sem("gc_used")
        tanh_zc, tanh_zm, g_done = sem("tanh_zc"), sem("tanh_zm"), sem("g_done")
        rec_ready, h_sq, h_ms, h_rs = sem("rec_ready"), sem("h_sq"), sem("h_ms"), sem("h_rs")
        yc_ready, yc_high, yc_low, ym_high, ym_low = (
            sem(n) for n in ("yc_ready", "yc_high", "yc_low", "ym_high", "ym_low"))
        y_out_c, y_out_m = sem("y_out_c"), sem("y_out_m")
        mx_exp, mx_q, mx_tanh_zc, mx_tanh_zm, mx_gc_used, mx_g = (
            sem(n) for n in ("mx_exp", "mx_q", "mx_tanh_zc", "mx_tanh_zm", "mx_gc_used", "mx_g"))
        mx_rec, mx_sq, mx_ms, mx_rs, mx_yc, mx_yc_high, mx_yc_low, mx_ym_high, mx_ym_low = (
            sem(n) for n in ("mx_rec", "mx_sq", "mx_ms", "mx_rs", "mx_yc", "mx_yc_high", "mx_yc_low",
                             "mx_ym_high", "mx_ym_low"))
        mx_out_c, mx_out_m, mx_v, mx_v_wide, mx_n, mx_states, cs_out = (
            sem(n) for n in ("mx_out_c", "mx_out_m", "mx_v", "mx_v_wide", "mx_n", "mx_states", "cs_out"))
        cn_meta, cn_out, dve_step, act_step, pool_step, out_sem = (
            sem(n) for n in ("cn_meta", "cn_out", "dve_step", "act_step", "pool_step", "out_sem"))
        wo_high, wo_low, finals = sem("wo_high"), sem("wo_low"), sem("finals")
        y_in, r_in, b_store = ([sem(f"{n}{i}") for i in range(2)] for n in ("y_in", "r_in", "b_store"))
        b_full, b_free, b_sum, b_sq, b_ms, b_rs, b_out = (
            sem(n) for n in ("b_full", "b_free", "b_sum", "b_sq", "b_ms", "b_rs", "b_out"))
        CONSTS, CONSTS2 = 1, 1

        useg = um[:, META + 2:].rearrange("p (b t) -> p b t", t=DS + 2)
        qdiag = qm[:, :].rearrange("p (b t) -> p b t", t=MIX + DS)[:, :, META:META + DS]

        def samples(ap):
            return ap[:, META:MIX].rearrange("p (b t) -> p b t", t=DS)

        def wide(ap, n):
            return ap.unsqueeze(2).broadcast_to([ap.shape[0], ap.shape[1], n])

        def evacuations(g, b, t):
            j = NT * b + t
            return j % 2, g * (NT * NB // 2) + j // 2

        def chunks(ap):
            return ap.rearrange("p (c t) -> p c t", c=CH)

        def load_w(queue, g, t):
            src = w_in[:, bass.ds(g * P + TILE_COL[t], P)].rearrange("(k p) c -> p k c", p=P)
            queue.dma_start(wst[t % STAGES][:, :, :], src).then_inc(w_in_s[t % STAGES], 16)

        def load_states(queue, g):
            src = state_c[:, bass.ds(g, 1), :, :].rearrange("b h d v -> d (b h) v")
            queue.dma_start(cs[:, :, 0:P], src).then_inc(cs_in, 16)

        block = ctx.enter_context(nc.Block())

        @block.sync
        def _(sp):
            def load_x(unit):
                s = unit % XBUF
                if unit >= XBUF:
                    sp.wait_ge(t0_full, t0_after_x(unit - XBUF))
                if unit == 0:
                    sp.dma_start(xs[0][0:META, :], meta).then_inc(x_in[0], 16)
                    sp.dma_start(xs[0][META:MIX, :], x_sample.rearrange("b t d -> (b t) d")).then_inc(x_in[0], 16)
                else:
                    r = (unit - 1) * P
                    sp.dma_start(xs[s][:, :], x_prompt[0, r:r + P, :]).then_inc(x_in[s], 16)

            def t0_after_x(unit):
                if unit <= CH:
                    return 2 * unit + 2
                b, c = divmod(unit - 1 - CH, CH)
                return t0(0, b, ("x", 2 * c + 1), True) + 1

            load_x(0)
            sp.dma_start(gain[:, :], norm_gain.rearrange("(k p) -> p k", p=P)).then_inc(par_in, 16)
            sp.wait_ge(bias_clear, 1)
            sp.dma_start(biasg[0:H, :], b_fgate.rearrange("(h o) -> h o", o=1)).then_inc(par_in, 16)
            sp.dma_start(biasg[32:GR, :], b_igate.rearrange("(h o) -> h o", o=1)).then_inc(par_in, 16)
            sp.dma_start(sm0[:, :], state_m.rearrange("b h -> h b")).then_inc(par_in, 16)
            sp.dma_start(mhg[:, :], mh_gain.rearrange("(h p) -> p h", p=P)).then_inc(par_in, 16)
            sp.dma_start(wgst[:, :, :], w_in[:, IG_COL:IG_COL + 2 * H].rearrange("(k p) c -> p k c", p=P)).then_inc(gate_in, 16)
            load_x(1)
            load_x(2)
            load_w(sp, 0, 0)
            load_w(sp, 0, 1)
            load_w(sp, 0, 2)
            load_x(3)
            load_x(4)
            for j in range(3):
                sp.dma_start(cwt[:, :, j], conv_w[j, :].rearrange("(h p) -> p h", p=P)).then_inc(par2_in, 16)
            sp.dma_start(nst[:, :, :].rearrange("p b h -> p (b h)"), state_n.rearrange("b h p -> p (b h)")).then_inc(par2_in, 16)
            for h in range(H):
                sp.dma_start(cst[:, h, :], state_conv[:, :, h * P:(h + 1) * P].rearrange("b j p -> p (b j)")).then_inc(par2_in, 16)
            load_states(sp, 0)
            for t in range(STAGES, NT):
                if t >= 2 * STAGES - 1:
                    load_x(1 + CH + t - (2 * STAGES - 1))
                sp.wait_ge(w_low, t - STAGES + 1)
                load_w(sp, 0, t)
            for unit in range(1 + 2 * CH, 1 + CH * NB):
                load_x(unit)
            for t in range(KT):
                if t < STAGES:
                    sp.wait_ge(w_low, NT * H - STAGES + t + 1)
                else:
                    sp.wait_ge(wo_low, t - STAGES + 1)
                sp.dma_start(wst[t % STAGES][:, :, :],
                             w_out[:, t * P:(t + 1) * P].rearrange("(k p) c -> p k c", p=P)).then_inc(w_in_s[t % STAGES], 16)

            def load_y(slot, tok, n):
                for k in range(KT):
                    sp.dma_start(ybuf[slot][:, k, :, 0:n], y_mid[k, :, :, bass.ds(tok, n)]).then_inc(y_in[slot], 16)

            sp.dma_start(fgain[:, :], final_gain.rearrange("(o d) -> o d", o=1).broadcast_to([P, D])).then_inc(fg_in, 16)
            sp.wait_ge(mx_out_c, 16 * H)
            sp.wait_ge(mx_out_m, 16 * H)
            sp.wait_ge(tile_done, NT * (NB * H - 1) + 1)
            load_y(0, META, DB * DS)
            sp.wait_ge(x_scaled, 17)
            sp.dma_start(xs[0][0:DB * DS, :], x_sample.rearrange("b t d -> (b t) d")).then_inc(r_in[0], 16)
            for j in range(NB):
                sp.wait_ge(y_out_c, (j + (NB * (H - 1) + 1)) * 16)
                sp.wait_ge(y_out_m, (j + (NB * (H - 1) + 1)) * 16)
                for c in range(CH):
                    if c % 2 == 0:
                        slot = 1 - c // 2
                        sp.wait_ge(b_full, j * (2 * CH) + (0 if slot else 2))
                        load_y(slot, j * BT + (MIX + c * P), 2 * P)
                    i = (1 + c) % 2
                    sp.wait_ge(b_out, j * CH + c)
                    sp.dma_start(xs[i][:, :], x_prompt[0, bass.ds(j * BT + c * P, P), :]).then_inc(r_in[i], 16)

        @block.gpsimd
        def _(pool):
            made = [0]

            def step(ins):
                ins.then_inc(pool_step, 1)
                made[0] += 1
                pool.wait_ge(pool_step, made[0])

            pool.memset(biasg[:, :], 0.0).then_inc(bias_clear, 1)
            pool.wait_ge(bias_clear, 1)
            step(pool.memset(ident[:, :], 0.0))
            step(pool.affine_select(out=ident[:, :], in_=ident[:, :], compare_op=ALU.not_equal, fill=1.0, base=0,
                                    pattern=[[-1, P]], channel_multiplier=1))
            step(pool.memset(halves[:, :], -0.5))
            step(pool.memset(ones[:, :], 1.0))
            step(pool.memset(Wgh[:, :, :], 0.0))
            step(pool.memset(Wgl[:, :, :], 0.0))
            step(pool.memset(trr, 0.0))
            step(pool.memset(mst[:, :], 0.0))
            step(pool.memset(rows[0:32, :], 0.0))
            step(pool.memset(rows[32:GR, :], 1.0))
            pool.memset(rb[:, :], 0.0).then_inc(const, 1)
            pool.wait_ge(const, 1)
            step(pool.memset(qm[:, :], 0.0))
            step(pool.memset(maskb[:, :], 0.0))
            step(pool.affine_select(out=maskb[:, :], in_=maskb[:, :], compare_op=ALU.is_ge, fill=NEG, base=0,
                                    pattern=[[1, P]], channel_multiplier=-1))
            step(pool.tensor_copy(mixmask[:, :], maskb[0:MIX, 0:MIX]))
            for at, n in SEGS[1:]:
                step(pool.affine_select(out=mixmask[:, at:at + n], in_=mixmask[:, at:at + n], compare_op=ALU.is_ge,
                                        fill=NEG, base=-at, pattern=[[0, n]], channel_multiplier=1))
            step(pool.memset(segind[:, :], 1.0))
            step(pool.affine_select(out=segind[:, :], in_=segind[:, :], compare_op=ALU.is_ge, fill=0.0, base=-META,
                                    pattern=[[-DS, DB]], channel_multiplier=1))
            step(pool.affine_select(out=segind[:, :], in_=segind[:, :], compare_op=ALU.is_ge, fill=0.0, base=META + DS - 1,
                                    pattern=[[DS, DB]], channel_multiplier=-1))
            step(pool.memset(v1[:, :, P:DV1], 1.0))
            step(pool.memset(um[:, 0:2], 0.0))
            step(pool.memset(v1m[:, P:DV1], 1.0))
            pool.memset(rbm[:, :], 0.0).then_inc(const2, 1)
            pool.wait_ge(const2, 1)

            def x_power(unit):
                pool.wait_ge(x_ms, unit + 1)
                n = MIX if unit == 0 else P
                pool.tensor_tensor(rsx[0:n, unit:unit + 1], msx[0:n, unit:unit + 1], halves[0:n, 0:1], ALU.pow).then_inc(x_rs, 1)

            def store_y(g, b, part):
                done, out = ((yc_low, y_out_c), (ym_low, y_out_m))[part]
                pool.wait_ge(done, nth(g, b) + 1)
                dst = y_mid[bass.ds(g + H * part, 1), :, :, tok0(b):tok0(b) + BT].rearrange("k p s t -> p (k s) t")
                pool.dma_start(dst, yst[:, part, :, :]).then_inc(out, 16)

            def store_mixed(g, part):
                done, out = ((mx_yc_low, mx_out_c), (mx_ym_low, mx_out_m))[part]
                pool.wait_ge(done, g + 1)
                dst = y_mid[bass.ds(g + H * part, 1), :, :, 0:MIX].rearrange("k p s t -> p (k s) t")
                pool.dma_start(dst, ystm[:, part, :, :]).then_inc(out, 16)

            def pool_block(g, b, first):
                if not (first and b == 0):
                    store_y(g if b else g - 1, b - 1 if b else NB - 1, 1)
                if first:
                    for c in range(CH - 1):
                        x_power(1 + CH * (b + 1) + c)
                if b == 0:
                    pool.wait_ge(mx_ms, g + 1)
                    pool.tensor_tensor(hm[:, 4:5], hm[:, 3:4], halves[0:MIX, 0:1], ALU.pow).then_inc(mx_rs, 1)
                if first:
                    x_power(1 + CH * (b + 1) + CH - 1)
                if b == 0:
                    store_mixed(g, 0)
                if b == 1:
                    pool.wait_ge(mx_states, g + 1)
                    dst = c_s[:, bass.ds(g, 1), :, :].rearrange("b h d v -> d (b h) v")
                    pool.dma_start(dst, cs[:, :, 0:P]).then_inc(cs_out, 16)
                store_y(g, b, 0)
                pool.wait_ge(h_ms, nth(g, b) + 1)
                pool.tensor_tensor(hrs[:, :], hms[:, :], halves[:, :], ALU.pow).then_inc(h_rs, 1)
                if b == 0:
                    store_mixed(g, 1)
                if b == NB - 1:
                    pool.wait_ge(s_free, nth(g, b) * 3 + 3)
                    pool.dma_start(c_p[0, bass.ds(g, 1), :, :].rearrange("h d v -> d (h v)"), cn[:, 0:P]).then_inc(cn_out, 16)

            for unit in range(1 + CH):
                x_power(unit)
            for b in range(NB - 1):
                pool_block(0, b, True)
            with pool.Fori(1, H) as g:
                pool_block(g - 1, NB - 1, False)
                for b in range(NB - 1):
                    pool_block(g, b, False)
            pool_block(H - 1, NB - 1, False)
            store_y(H - 1, NB - 1, 1)

            def b_tile(tile, n, c, dst):
                pool.wait_ge(b_ms, tile + 1)
                pool.tensor_tensor(rsx[0:n, c:c + 1], msx[0:n, c:c + 1], halves[0:n, 0:1], ALU.pow).then_inc(b_rs, 1)
                pool.wait_ge(b_out, tile + 1)
                pool.dma_start(dst, result[c % 2][0:n, :]).then_inc(b_store[c % 2], 16)

            pool.wait_ge(finals, 1)
            pool.dma_start(n_s.rearrange("b h p -> p (b h)"), nst[:, :, :].rearrange("p b h -> p (b h)")).then_inc(out_sem, 16)
            pool.dma_start(n_p[0].rearrange("h p -> p h"), npo[:, :]).then_inc(out_sem, 16)
            pool.dma_start(m_p.rearrange("o h -> h o"), mst[:, NB * CH + 1:NB * CH + 2]).then_inc(out_sem, 16)
            pool.dma_start(m_s.rearrange("b h -> h b"), smn[:, :]).then_inc(out_sem, 16)
            for h in range(H):
                pool.dma_start(conv_s[:, :, h * P:(h + 1) * P].rearrange("b j p -> p (b j)"), cst[:, h, :]).then_inc(out_sem, 16)
                pool.dma_start(conv_p[0, :, h * P:(h + 1) * P].rearrange("j p -> p j"), cpo[:, h, :]).then_inc(out_sem, 16)
            b_tile(0, DB * DS, 0, y_sample.rearrange("b t d -> (b t) d"))
            with pool.Fori(0, NB) as j:
                for c in range(CH):
                    b_tile(j * CH + (1 + c), P, 1 + c, y_prompt[0, bass.ds(j * BT + c * P, P), :])
            pool.wait_ge(b_store[0], 16 * 9)
            pool.wait_ge(b_store[1], 16 * 8)
            pool.wait_ge(out_sem, 16 * 12)
            pool.wait_ge(cs_out, 16 * H)
            pool.wait_ge(cn_out, 16 * H)

        @block.tensor
        def _(pe):
            mm = nc.tensor.matmul

            def split_product(out, wh, wl, k0, k1, tok, n):
                for k in range(k0, k1):
                    xh, xl = xTh[:, k, tok:tok + n], xTl[:, k, tok:tok + n]
                    mm(out, wh[:, k, :], xh, start=(k == 0), stop=False)
                    mm(out, wh[:, k, :], xl, start=False, stop=False)
                    last = mm(out, wl[:, k, :], xh, start=False, stop=(k == KT - 1))
                return last

            def use_t0(count):
                pe.wait_ge(t0_free, count)

            def use_t1(count):
                pe.wait_ge(t1_free, count)

            def x_round(unit, r, count):
                n = MIX if unit == 0 else P
                pe.wait_ge(x_scaled, unit + 1)
                use_t0(count)
                for k in range(4):
                    last = nc.tensor.transpose(T0[:, k * n:k * n + n], xs[unit % XBUF][0:n, (4 * r + k) * P:(4 * r + k + 1) * P],
                                               ident[0:n, 0:n])
                last.then_inc(t0_full, 1)

            def gates(rounds, tok, n, count):
                pe.wait_ge(x_low, rounds)
                use_t1(count)
                split_product(T1[0:GR, 0:n], Wgh, Wgl, 0, KT, tok, n).then_inc(t1_full, 1)

            def columns(units, n, segs, count):
                pe.wait_ge(rows_ready, units)
                use_t1(count)
                for c in range(1 if n == MIX else CH):
                    nc.tensor.transpose(T1[0:min(n, P), c * 64:c * 64 + GR], trr[:, c * P:c * P + min(n, P)], ident[64:64 + GR, 64:64 + GR])
                mm(T1[:, 256:256 + segs * H], ones[0:H, :], drl[:, 0:segs * H], start=True, stop=True).then_inc(t1_full, 1)

            def transposed(src, count):
                use_t0(count)
                for c in range(CH):
                    last = nc.tensor.transpose(T0[:, c * P:(c + 1) * P], src[:, c * P:(c + 1) * P], ident[:, :])
                last.then_inc(t0_full, 1)

            def chunk(g, b, c, first):
                n = nth(g, b)
                out = N[c // 2][:, (c % 2) * DV1:(c % 2 + 1) * DV1]
                if c == 0:
                    pe.wait_ge(s_free, n * 3 + 1)
                    pe.wait_ge(q_scaled, n + 1)
                    pe.wait_ge(t0_free, t0(g, b, "vT", first) + 1)
                    if b == 0:
                        pe.wait_ge(cn_meta, g + 1)
                    else:
                        pe.wait_ge(s_free, n * 3)
                else:
                    pe.wait_ge(a_free if c % 2 else s_free, n * 3 + 2 + (c - 1) // 2)
                mm(out, dp[:, c * P:(c + 1) * P], v1[:, c, :], start=True, stop=False)
                last = mm(out, eh[:, c * P:(c + 1) * P], cn[:, :], start=False, stop=True)
                if c == CH - 1:
                    last.then_inc(n_full, 1)
                kv, full, free = ((S, s_full, s_free), (A, a_full, a_free))[1 - c % 2]
                pe.wait_ge(free, n * 3 + 1 + c // 2)
                mm(kv[:, 0:DV1], kw[:, c * P:(c + 1) * P], v1[:, c, :], start=True, stop=True).then_inc(full, 1)

            def at_half(g, b, t, first):
                n = nth(g, b)
                if t == V and not (first and b == 0):
                    pe.wait_ge(n_free, n)
                    transposed(eh, t0(g, b, "hT", first))
                if t == Q:
                    bank_, left = evacuations(g, b, K)
                    pe.wait_ge(p_free[bank_], left + 1)
                    transposed(kf, t0(g, b, "kT", first))
                if t == GC:
                    bank_, left = evacuations(g, b, V)
                    pe.wait_ge(p_free[bank_], left + 1)
                    transposed(vf, t0(g, b, "vT", first))
                if t == ZC:
                    chunk(g, b, 0, first)
                if t == O:
                    chunk(g, b, 2, first)
                if first:
                    for r in X_HALF.get(t, ()):
                        x_round(1 + CH * (b + 1) + r // 2, r % 2, t0(g, b, ("x", r), first))
                    if t == O:
                        gates(2 + 2 * CH * (b + 2), tok0(b + 1), BT, t1(g, b, "gates", first))

            def at_end(g, b, t, first):
                n = nth(g, b)
                if t == Q:
                    pe.wait_ge(rb_ready, n + 1)
                    pe.wait_ge(a_free, n * 3)
                    for c in range(CH):
                        o = A[:, c * P:(c + 1) * P]
                        mm(o, rows[0:GR, tok0(b) + c * P:tok0(b) + (c + 1) * P], rb[0:GR, c * P:(c + 1) * P], start=True, stop=False)
                        last = mm(o, identb[:, :], maskb[:, :], start=False, stop=True)
                    last.then_inc(a_full, 1)
                    pe.wait_ge(n_free, n)
                    mm(N[0][:, :], ones[64:64 + H, :], rb[64:64 + H, :], start=True, stop=True).then_inc(e_full, 1)
                if t == GC:
                    bank_, left = evacuations(g, b, Q)
                    pe.wait_ge(p_free[bank_], left + 1)
                    pe.wait_ge(s_free, n * 3)
                    for c in range(CH):
                        cc = slice(c * P, (c + 1) * P)
                        last = mm(S[:, cc], kf[:, cc], qf[:, cc], start=True, stop=True)
                    last.then_inc(s_full, 1)
                if t == ZC:
                    chunk(g, b, 1, first)
                if t == O:
                    chunk(g, b, 3, first)
                if first:
                    for r in X_END.get(t, ()):
                        x_round(1 + CH * (b + 1) + r // 2, r % 2, t0(g, b, ("x", r), first))
                if b == 0:
                    mixed_end(g, b, t, first)
                if b == 1 and t in (V, Q, GC):
                    i0, i1 = SAMPLE_ROUNDS[t - V]
                    pe.wait_ge(mx_v_wide, g + 1)
                    use_t1(t1(g, b, ("state", t - V), first))
                    mm(T1[:, 0:(i1 - i0) * DV1], kwm[:, :], v1x[:, i0:i1, :].rearrange("p b v -> p (b v)"),
                       start=True, stop=True).then_inc(t1_full, 1)
                if first and t == ZM:
                    columns(b + 3, BT, CH, t1(g, b, "cols", first))

            def mixed_end(g, b, t, first):
                if t == Q:
                    use_t1(t1(g, b, "args", first))
                    mm(T1[0:MIX, 0:MIX], rows[0:GR, 0:MIX], rbm[0:GR, :], start=True, stop=False)
                    mm(T1[0:MIX, 0:MIX], identb[0:MIX, 0:MIX], mixmask[:, :], start=False, stop=True)
                    mm(T1[:, P:P + MIX], ones[64:64 + H, :], rbm[64:64 + H, :], start=True, stop=True).then_inc(t1_full, 1)
                if t == GC:
                    pe.wait_ge(t0_free, t0(g, b, ("mix", V), first) + 1)
                    use_t1(t1(g, b, "kv", first))
                    nc.tensor.transpose(T1[0:MIX, 0:P], kfm[:, :], ident[:, :])
                    nc.tensor.transpose(T1[0:MIX, P:2 * P], vfm[:, :], ident[:, :]).then_inc(t1_full, 1)
                if t == HC:
                    pe.wait_ge(t0_free, t0(g, b, ("mix", Q), first) + 1)
                    use_t1(t1(g, b, "score", first))
                    mm(T1[0:MIX, 0:MIX], kfm[:, :], qfm[:, :], start=True, stop=True).then_inc(t1_full, 1)
                if t == GB:
                    use_t1(t1(g, b, "num", first))
                    pe.wait_ge(mx_q, g + 1)
                    pe.wait_ge(cs_in, (g + 1) * 16)
                    pe.wait_ge(mx_n, g + 1)
                    o = T1[0:MIX, 0:DV1]
                    mm(o, dpm[:, :], v1m[:, :], start=True, stop=False)
                    for i in range(DB):
                        mm(o, qm[:, i * MIX:(i + 1) * MIX], cs[:, i, :], start=False, stop=(i == DB - 1))
                    mm(T1[:, 2 * P:2 * P + DV1], kwm[0:META, :], v1m[0:META, :], start=True, stop=True).then_inc(t1_full, 1)
                if t == O:
                    use_t1(t1(g, b, "hT", first))
                    nc.tensor.transpose(T1[:, 0:MIX], hnm[:, :], ident[0:MIX, 0:MIX]).then_inc(t1_full, 1)

            def pe_block(g, b, first):
                for t in range(NT):
                    if b == 0:
                        pe.wait_ge(w_low, g * NT + (t + 1))
                    if b == 0:
                        use_t0(t0(g, b, ("mix", t), first))
                        split_product(T0[:, 0:MIX], Wh[:, t, :, :], Wl[:, t, :, :], 0, KT, 0, MIX).then_inc(t0_full, 1)
                    bank_, left = evacuations(g, b, t)
                    pe.wait_ge(p_free[bank_], left)
                    out = PB[bank_][:, :]
                    split_product(out, Wh[:, t, :, :], Wl[:, t, :, :], 0, KT // 2, tok0(b), BT)
                    at_half(g, b, t, first)
                    split_product(out, Wh[:, t, :, :], Wl[:, t, :, :], KT // 2, KT, tok0(b), BT).then_inc(tile_done, 1)
                    at_end(g, b, t, first)

            pe.wait_ge(const, CONSTS)
            for r in range(2):
                x_round(0, r, r)
            for c in range(CH):
                x_round(1 + c, 0, 2 * c + 2)
                x_round(1 + c, 1, 2 * c + 3)
                if c == 0:
                    pe.wait_ge(g_low, 1)
                    gates(2, 0, MIX, 0)
            columns(1, MIX, DB, 1)
            gates(2 + 2 * CH, MIX, BT, 2)
            columns(2, BT, CH, 3)
            pe.wait_ge(const2, CONSTS2)
            for b in range(NB - 1):
                pe_block(0, b, True)
            with pe.Fori(1, H) as g:
                pe_block(g - 1, NB - 1, False)
                for b in range(NB - 1):
                    pe_block(g, b, False)
            pe_block(H - 1, NB - 1, False)
            pe.wait_ge(n_free, NB * H)
            transposed(eh, t0(H, 0, "hT", False) - t0_uses(0, False).index("hT"))

            def b_tile(tile, n, slot, i, at):
                for h in range(2):
                    if not isinstance(tile, int):
                        pe.wait_ge(b_free, tile * 2 + (h - 2))
                    o = OUT[i][h][0:n, :]
                    for k in range(KT):
                        yh, yl = ybuf[slot][:, k, 0, at:at + n], ybuf[slot][:, k, 1, at:at + n]
                        wh, wl = Woh[:, k, h * BT:(h + 1) * BT], Wol[:, k, h * BT:(h + 1) * BT]
                        mm(o, yh, wh, start=(k == 0), stop=False)
                        mm(o, yh, wl, start=False, stop=False)
                        last = mm(o, yl, wh, start=False, stop=(k == KT - 1))
                    last.then_inc(b_full, 1)

            pe.wait_ge(wo_low, KT)
            pe.wait_ge(y_in[0], 16 * KT)
            pe.wait_ge(p_free[0], H * NT * NB // 2)
            pe.wait_ge(p_free[1], H * NT * NB // 2)
            pe.wait_ge(a_free, 3 * NB * H)
            pe.wait_ge(s_free, 3 * NB * H)
            b_tile(0, DB * DS, 0, 0, 0)
            with pe.Fori(0, NB) as j:
                for c in range(CH):
                    if c == 0:
                        pe.wait_ge(y_in[1], (j + 1) * 16 * KT)
                    if c == 2:
                        pe.wait_ge(y_in[0], (j + 2) * 16 * KT)
                    b_tile(j * CH + (1 + c), P, 1 - c // 2, (1 + c) % 2, (c % 2) * P)

        @block.scalar
        def _(act):
            order = Order(act, act_step, ACT_TURN)
            did, mark, fn = order.did, order.mark, order.after(nc.scalar.activation)

            def x_square(unit):
                n, s = (MIX if unit == 0 else P), unit % XBUF
                loads = unit // XBUF + (2 if s == 0 else 1)
                act.wait_ge(x_in[s], 16 * loads)
                mark(fn(junk[0:n, :], xs[s][0:n, :], ACT.Square, accum_out=ssx[0:n, unit:unit + 1]).then_inc(x_sq, 1), x_sq, unit + 1)

            def x_high_part(unit, r, count):
                n, tok = (MIX, 0) if unit == 0 else (P, MIX + (unit - 1) * P)
                i = 2 * unit + r
                act.wait_ge(t0_free, count + 1)
                mark(fn(xTh[:, 4 * r:4 * r + 4, tok:tok + n], xtmp[i % 2][:, 0:4 * n].rearrange("p (k t) -> p k t", k=4),
                   ACT.Copy).then_inc(x_high, 1), x_high, i + 1)

            def gate_part(unit, n, count):
                act.wait_ge(t1_full, count + 1)
                if unit:
                    act.wait_ge(rows_ready, unit)
                mark(fn(grow[:, 0:n], T1[0:GR, 0:n], ACT.Identity, bias=biasg[:, :], scale=1.0 / WS).then_inc(t1_free, 1), t1_free, count + 1)
                act.wait_ge(g_abs, unit + 1)
                mark(fn(gt[:, 0:n], gt[:, 0:n], ACT.Exp).then_inc(g_exp, 1), g_exp, unit + 1)
                mark(fn(gt[:, 0:n], gt[:, 0:n], ACT.Ln, bias=1.0).then_inc(g_ln, 1), g_ln, unit + 1)

            def columns_part(first_chunk, chunks_, n, count):
                act.wait_ge(t1_full, count + 1)
                src = T1[0:n, 0:64 * chunks_].rearrange("p (c k r) -> p c k r", k=2, r=32)[:, :, :, 0:H]
                for kind in range(2):
                    did(fn(cols[0:n, first_chunk:first_chunk + chunks_, kind, :], src[:, :, kind, :], ACT.Exp))
                if first_chunk == 0:
                    out = decs[:, :, :]
                else:
                    out = cols[:, first_chunk:first_chunk + chunks_, 2, :]
                k = DB if first_chunk == 0 else CH
                mark(fn(out, T1[:, 256:256 + k * H].rearrange("p (c h) -> p c h", h=H), ACT.Exp).then_inc(t1_free, 1), t1_free, count + 1)

            def split_w(g, t):
                act.wait_ge(w_in_s[t % STAGES], g * (16 * NT // STAGES) + 16 * (t // STAGES + 1))
                mark(fn(Wh[:, t, :, :], wst[t % STAGES][:, :, :], ACT.Copy, scale=WS).then_inc(w_high, 1), w_high, g * NT + (t + 1))

            def copy(out, src, scale):
                return fn(out, src, ACT.Copy, scale=scale)

            def mixed_start(g, b, t, first):
                count = t0(g, b, ("mix", t), first)
                src = T0[:, 0:MIX]
                if t in (HC, GB):
                    return
                act.wait_ge(t0_full, count + 1)
                if t == K:
                    mark(copy(kfm[:, :], src, SK / WS).then_inc(t0_free, 1), t0_free, count + 1)
                if t == V:
                    mark(copy(vfm[:, :], src, 1 / WS).then_inc(t0_free, 1), t0_free, count + 1)
                if t == Q:
                    act.wait_ge(mx_q, g)
                    mark(copy(qfm[:, :], src, 1 / WS).then_inc(t0_free, 1), t0_free, count + 1)
                if t == GC:
                    act.wait_ge(mx_gc_used, g)
                    mark(copy(gcm[:, :], src, 1 / WS).then_inc(t0_free, 1), t0_free, count + 1)
                if t == ZC:
                    act.wait_ge(mx_g, g)
                    mark(fn(tzm[:, :], src, ACT.Tanh, scale=0.5 / WS).then_inc(mx_tanh_zc, 1), mx_tanh_zc, g + 1)
                if t == O:
                    mark(fn(tom[:, :], src, ACT.Tanh, scale=0.5 / WS).then_inc(t0_free, 1), t0_free, count + 1)
                if t == ZM:
                    mark(fn(tzm[:, :], src, ACT.Tanh, scale=0.5 / WS).then_inc(mx_tanh_zm, 1), mx_tanh_zm, g + 1)

            def heads_high(g, b, count):
                n = nth(g, b)
                act.wait_ge(t0_free, count + 1)
                act.wait_ge(y_out_m, (n - 1) * 16)
                mark(fn(yst[:, 1, 0, :], dp[:, :], ACT.Copy).then_inc(ym_high, 1), ym_high, n)

            def at_half(g, b, t, first):
                if t == V and not (first and b == 0):
                    heads_high(g, b, t0(g, b, "hT", first))
                if t == GC:
                    act.wait_ge(t0_full, t0(g, b, "vT", first) + 1)
                    mark(fn(v1[:, :, 0:P], chunks(T0[:, :]), ACT.Copy).then_inc(t0_free, 1), t0_free, t0(g, b, "vT", first) + 1)
                if first:
                    for r in X_HALF.get(t, ()):
                        x_high_part(1 + CH * (b + 1) + r // 2, r % 2, t0(g, b, ("x", r), first))
                    if t == O:
                        gate_part(b + 2, BT, t1(g, b, "gates", first))

            def evacuate(g, b, t):
                n = nth(g, b)
                i, left = evacuations(g, b, t)
                src, free = PB[i][:, :], p_free[i]
                if t in (HC, GB):
                    return
                act.wait_ge(tile_done, n * NT + (t + 1))
                if t == K:
                    mark(copy(kf[:, :], src, SK / WS).then_inc(free, 1), free, left + 1)
                if t == V:
                    mark(copy(vf[:, :], src, 1 / WS).then_inc(free, 1), free, left + 1)
                if t == Q:
                    act.wait_ge(q_scaled, n)
                    mark(copy(qf[:, :], src, 1 / WS).then_inc(free, 1), free, left + 1)
                if t == GC:
                    act.wait_ge(gc_used, n)
                    mark(copy(gcs[:, :], src, 1 / WS).then_inc(free, 1), free, left + 1)
                if t == ZC:
                    act.wait_ge(g_done, n)
                    mark(fn(tz[:, :], src, ACT.Tanh, scale=0.5 / WS).then_inc(tanh_zc, 1), tanh_zc, n + 1)
                if t == O:
                    mark(fn(to[:, :], src, ACT.Tanh, scale=0.5 / WS).then_inc(free, 1), free, left + 1)
                if t == ZM:
                    act.wait_ge(yc_ready, n + 1)
                    mark(fn(tz[:, :], src, ACT.Tanh, scale=0.5 / WS).then_inc(tanh_zm, 1), tanh_zm, n + 1)

            def at_end(g, b, t, first):
                n = nth(g, b)
                if t == Q:
                    act.wait_ge(a_full, n * 3 + 1)
                    act.wait_ge(ym_low, n)
                    mark(fn(dp[:, :], A[:, :], ACT.Exp).then_inc(a_free, 1), a_free, n * 3 + 1)
                    act.wait_ge(e_full, n + 1)
                    mark(fn(eh[:, :], N[0][:, :], ACT.Exp).then_inc(e_ready, 1), e_ready, n + 1)
                    if b == 0:
                        act.wait_ge(t1_full, t1(g, b, "args", first) + 1)
                        did(fn(dpm[:, :], T1[0:MIX, 0:MIX], ACT.Exp))
                        mark(fn(ehm[:, :], T1[:, P:P + MIX], ACT.Exp).then_inc(t1_free, 1), t1_free, t1(g, b, "args", first) + 1)
                if t == GB and b == 0:
                    act.wait_ge(mx_rec, g + 1)
                    mark(fn(junk[0:MIX, 0:P], T1[0:MIX, 0:P], ACT.Square, scale=hm[:, 1:2], accum_out=hm[:, 2:3]).then_inc(mx_sq, 1), mx_sq, g + 1)
                if t == ZC:
                    act.wait_ge(yc_ready, n + 1)
                    act.wait_ge(y_out_c, n * 16)
                    mark(fn(yst[:, 0, 0, :], yc[:, :], ACT.Copy).then_inc(yc_high, 1), yc_high, n + 1)
                    if b == 0:
                        act.wait_ge(mx_yc, g + 1)
                        act.wait_ge(mx_out_c, g * 16)
                        mark(fn(ystm[:, 0, 0, :], ycm[:, :], ACT.Copy).then_inc(mx_yc_high, 1), mx_yc_high, g + 1)
                if t == O:
                    act.wait_ge(rec_ready, n + 1)
                    for c in range(CH):
                        last = fn(junk[:, 0:P], N[c // 2][:, (c % 2) * DV1:(c % 2) * DV1 + P], ACT.Square,
                                  scale=rec[:, c:c + 1], accum_out=hss[:, c:c + 1])
                        if c < CH - 1:
                            did(last)
                    mark(last.then_inc(h_sq, 1), h_sq, n + 1)
                if t == ZM and b == 0:
                    act.wait_ge(t1_free, t1(g, b, "hT", first) + 1)
                    act.wait_ge(mx_out_m, g * 16)
                    mark(fn(ystm[:, 1, 0, :], ymm[:, :], ACT.Copy).then_inc(mx_ym_high, 1), mx_ym_high, g + 1)
                if first:
                    if t in (Q, GC, HC, GB):
                        x_square(1 + CH * (b + 1) + (Q, GC, HC, GB).index(t))
                    for r in X_END.get(t, ()):
                        x_high_part(1 + CH * (b + 1) + r // 2, r % 2, t0(g, b, ("x", r), first))
                    if t == ZM:
                        columns_part(1 + CH * (b + 1), CH, P, t1(g, b, "cols", first))
                    if b == 0 and t < NT - STAGES:
                        split_w(0, t + STAGES)

            def act_block(g, b, first, following):
                if following == "weights":
                    act.wait_ge(w_low, (g + 1) * NT - 1)
                    load_w(act, g + 1, 0)
                    load_w(act, g + 1, 1)
                    act.wait_ge(cs_out, (g + 1) * 16)
                    load_states(act, g + 1)
                for t in range(NT):
                    if b == 0:
                        mixed_start(g, b, t, first)
                    at_half(g, b, t, first)
                    evacuate(g, b, t)
                    at_end(g, b, t, first)
                    if following == "weights":
                        act.wait_ge(tile_done, nth(g, b) * NT + (t + 1))
                        split_w(g + 1, t)
                        if t < NT - 2:
                            act.wait_ge(w_low, (g + 1) * NT + t)
                            load_w(act, g + 1, t + 2)
                    if following == "output weights" and t < KT:
                        act.wait_ge(w_in_s[t % STAGES], 16 * (NT * H // STAGES + t // STAGES + 1))
                        mark(fn(Woh[:, :, t * P:(t + 1) * P], wst[t % STAGES][:, :, :], ACT.Copy, scale=WS).then_inc(wo_high, 1), wo_high, t + 1)

            act.wait_ge(par_in, 16 * 5)
            act.wait_ge(const, CONSTS)
            x_square(0)
            act.wait_ge(gate_in, 16)
            did(fn(Wgh[:, :, 0:H], wgst[:, :, H:2 * H], ACT.Copy, scale=WS))
            mark(fn(Wgh[:, :, 32:GR], wgst[:, :, 0:H], ACT.Copy, scale=WS).then_inc(g_high, 1), g_high, 1)
            for r in range(2):
                x_high_part(0, r, r)
            for c in range(CH):
                x_square(1 + c)
                if c == 1:
                    gate_part(0, MIX, 0)
                if c < STAGES:
                    split_w(0, c)
                for r in range(2):
                    x_high_part(1 + c, r, 2 + 2 * c + r)
            columns_part(0, 1, MIX, 1)
            gate_part(1, BT, 2)
            columns_part(1, CH, P, 3)
            for b in range(NB - 1):
                act_block(0, b, True, None)
            with act.Fori(1, H) as g:
                order.enter(g)
                act_block(g - 1, NB - 1, False, "weights")
                for b in range(NB - 1):
                    act_block(g, b, False, None)
            order.leave(H - 1)
            act_block(H - 1, NB - 1, False, "output weights")
            heads_high(H, 0, t0(H, 0, "hT", False) - t0_uses(0, False).index("hT"))

            def b_tile(tile, n, i, c):
                act.wait_ge(b_free, tile * 2 + 2)
                mark(fn(junk[0:n, :], xs[i][0:n, :], ACT.Square, accum_out=ssx[0:n, c:c + 1]).then_inc(b_sq, 1), b_sq, tile + 1)

            b_tile(0, DB * DS, 0, 0)
            with act.Fori(0, NB) as j:
                for c in range(CH):
                    b_tile(j * CH + (1 + c), P, (1 + c) % 2, 1 + c)

        @block.vector
        def _(dve):
            order = Order(dve, dve_step, DVE_TURN)
            did, mark = order.did, order.mark
            tt, ts, stt, scan, copy, reciprocal, memset = (order.after(op) for op in (
                nc.vector.tensor_tensor, nc.vector.tensor_scalar, nc.vector.scalar_tensor_tensor,
                nc.vector.tensor_tensor_scan, nc.vector.tensor_copy, nc.vector.reciprocal, nc.vector.memset))

            def pick(out, src):
                return ts(out, src, 1.0, None, ALU.mult)

            def x_prepare(unit):
                n, s = (MIX if unit == 0 else P), unit % XBUF
                dve.wait_ge(x_sq, unit + 1)
                mark(ts(msx[0:n, unit:unit + 1], ssx[0:n, unit:unit + 1], 1.0 / D, EPS, ALU.mult, ALU.add).then_inc(x_ms, 1), x_ms, unit + 1)
                dve.wait_ge(x_rs, unit + 1)
                mark(ts(xs[s][0:n, :], xs[s][0:n, :], rsx[0:n, unit:unit + 1], None, ALU.mult).then_inc(x_scaled, 1), x_scaled, unit + 1)

            def x_low_part(i):
                unit, r = divmod(i, 2)
                n, tok = (MIX, 0) if unit == 0 else (P, MIX + (unit - 1) * P)
                dve.wait_ge(x_high, i + 1)
                mark(tt(xTl[:, 4 * r:4 * r + 4, tok:tok + n], xtmp[i % 2][:, 0:4 * n].rearrange("p (k t) -> p k t", k=4),
                   xTh[:, 4 * r:4 * r + 4, tok:tok + n], ALU.subtract).then_inc(x_low, 1), x_low, i + 1)

            def x_gain(unit, r, count0):
                n, i = (MIX if unit == 0 else P), 2 * unit + r
                dve.wait_ge(t0_full, count0 + 1)
                mark(tt(xtmp[i % 2][:, 0:4 * n].rearrange("p (k t) -> p k t", k=4), T0[:, 0:4 * n].rearrange("p (k t) -> p k t", k=4),
                   wide(gain[:, 4 * r:4 * r + 4], n), ALU.mult).then_inc(t0_free, 1), t0_free, count0 + 1)

            def gate_part(unit, tok, n, segs):
                dve.wait_ge(t1_free, GATE_COUNTS[unit] + 1)
                f, t = grow[0:H, 0:n], gt[:, 0:n]
                mark(stt(t, f, -1.0, f, ALU.mult, ALU.min).then_inc(g_abs, 1), g_abs, unit + 1)
                dve.wait_ge(g_ln, unit + 1)
                did(stt(lf[:, 0:n], f, 0.0, t, ALU.min, ALU.subtract))
                did(copy(t, grow[32:GR, 0:n]))
                for at, length, _ in segs:
                    sl = slice(at, at + length)
                    did(scan(bcum[:, sl], ones[0:H, 0:length], lf[:, sl], 0.0, ALU.mult, ALU.add))
                a = rows[0:H, tok:tok + n]
                did(tt(a, t, bcum[:, 0:n], ALU.subtract))
                for at, length, (before, after) in segs:
                    sl = slice(at, at + length)
                    end = at + length - 1
                    did(scan(mrow[:, sl], a[:, sl], a[:, sl], before, ALU.max, ALU.max))
                    if after is not None:
                        did(tt(after, bcum[:, end:end + 1], mrow[:, end:end + 1], ALU.add))
                if unit:
                    dve.wait_ge(t1_free, COLS_COUNTS[unit - 1] + 1)
                for at, length, (before, _) in segs:
                    sl = slice(at, at + length)
                    did(ts(rows[96:96 + H, tok + at:tok + at + length], mrow[:, sl], before, -1.0, ALU.subtract, ALU.mult))
                    did(ts(trr[32:GR, sl], a[:, sl], mrow[:, at + length - 1:at + length], None, ALU.subtract))
                did(copy(rows[64:64 + H, tok:tok + n], mrow[:, 0:n]))
                did(stt(trr[0:H, 0:n], bcum[:, 0:n], -1.0, mrow[:, 0:n], ALU.mult, ALU.subtract))
                if unit == 0:
                    did(tt(rl[:, :], sm0[:, :], samples(mrow)[:, :, DS - 1], ALU.subtract))
                    did(tt(smn[:, :], samples(bcum)[:, :, DS - 1], samples(mrow)[:, :, DS - 1], ALU.add))
                    k = DB
                else:
                    c0 = 1 + CH * (unit - 1)
                    did(tt(rl[:, 0:CH], mst[:, c0:c0 + CH], chunks(mrow[:, 0:n])[:, :, P - 1], ALU.subtract))
                    k = CH
                mark(tt(drl[:, 0:k * H].rearrange("p (c h) -> p c h", h=H), wide(rl[:, 0:k], H),
                   selh[0:H, :].unsqueeze(1).broadcast_to([H, k, H]), ALU.mult).then_inc(rows_ready, 1), rows_ready, unit + 1)

            def block_segs(b):
                c0 = 1 + CH * b
                return [(P * c, P, (mst[:, c0 + c:c0 + c + 1], mst[:, c0 + c + 1:c0 + c + 2])) for c in range(CH)]

            def split_w(g, t):
                dve.wait_ge(w_high, g * NT + (t + 1))
                mark(stt(Wl[:, t, :, :], wst[t % STAGES][:, :, :], WS, Wh[:, t, :, :], ALU.mult, ALU.subtract).then_inc(w_low, 1), w_low, g * NT + (t + 1))

            def conv(out, w, g, tap):
                did(ts(out, tap(0), cwt[:, bass.ds(g, 1), 0], None, ALU.mult))
                for j in (1, 2):
                    did(stt(out, tap(j), cwt[:, bass.ds(g, 1), j], out, ALU.mult, ALU.add))

            def mixed_start(g, b, t, first):
                at = t0(g, b, ("mix", t), first)
                src = T0[:, 0:MIX]
                if t == K:
                    tt_ = pick(cs[:, :, P], nst[:, :, bass.ds(g, 1)].rearrange("p b o -> p (b o)"))
                    mark(tt_.then_inc(mx_n, 1), mx_n, g + 1)
                if t == HC:
                    dve.wait_ge(t0_full, at + 1)
                    dve.wait_ge(t0_free, t0(g, b, ("mix", GC), first) + 1)
                    states = cst[:, bass.ds(g, 1), :].rearrange("p o (b j) -> p (o b) j", j=2)
                    did(pick(useg[:, :, 0:2], states))
                    did(stt(um[:, 2:2 + META], src[:, 0:META], 1 / WS, gcm[:, 0:META], ALU.mult, ALU.mult))
                    mark(stt(useg[:, :, 2:], samples(src), 1 / WS, samples(gcm), ALU.mult, ALU.mult).then_inc(t0_free, 1), t0_free, at + 1)
                    dve.wait_ge(t0_free, at + 1)
                    mark(pick(states, useg[:, :, DS:DS + 2]).then_inc(mx_gc_used, 1), mx_gc_used, g + 1)
                    conv(ycm[:, 0:META], None, g, lambda j: um[:, j:j + META])
                    conv(samples(ycm), None, g, lambda j: useg[:, :, j:j + DS])
                    did(copy(u[:, 0:2], um[:, META:META + 2]))
                if t == GB:
                    dve.wait_ge(t0_full, at + 1)
                    mark(stt(ycm[:, :], src, 1 / WS, ycm[:, :], ALU.mult, ALU.mult).then_inc(t0_free, 1), t0_free, at + 1)
                if t == ZC:
                    dve.wait_ge(mx_tanh_zc, g + 1)
                    mark(stt(zsm[:, :], tzm[:, :], 1.0, src, ALU.add, ALU.mult).then_inc(t0_free, 1), t0_free, at + 1)
                    dve.wait_ge(t0_free, at + 1)
                    mark(stt(ycm[:, :], ycm[:, :], 0.5 / WS, zsm[:, :], ALU.mult, ALU.mult).then_inc(mx_yc, 1), mx_yc, g + 1)
                if t == ZM:
                    dve.wait_ge(t0_free, t0(g, b, ("mix", O), first) + 1)
                    did(ts(tom[:, :], tom[:, :], 1.0, mhg[:, bass.ds(g, 1)], ALU.add, ALU.mult))
                    dve.wait_ge(mx_tanh_zm, g + 1)
                    mark(stt(zsm[:, :], tzm[:, :], 1.0, src, ALU.add, ALU.mult).then_inc(t0_free, 1), t0_free, at + 1)
                    dve.wait_ge(t0_free, at + 1)
                    mark(stt(Gm[:, :], tom[:, :], 0.25 / WS, zsm[:, :], ALU.mult, ALU.mult).then_inc(mx_g, 1), mx_g, g + 1)
                    dve.wait_ge(mx_g, g + 1)
                    dve.wait_ge(t1_full, t1(g, b, "hT", first) + 1)
                    mark(tt(ymm[:, :], T1[:, 0:MIX], Gm[:, :], ALU.mult).then_inc(t1_free, 1), t1_free, t1(g, b, "hT", first) + 1)

            def heads_out(g, b, at):
                n = nth(g, b)
                dve.wait_ge(t0_full, at + 1)
                dve.wait_ge(g_done, n)
                mark(tt(dp[:, :], T0[:, :], G[:, :], ALU.mult).then_inc(t0_free, 1), t0_free, at + 1)
                dve.wait_ge(ym_high, n)
                mark(tt(yst[:, 1, 1, :], dp[:, :], yst[:, 1, 0, :], ALU.subtract).then_inc(ym_low, 1), ym_low, n)

            def update(g, b, c):
                n = nth(g, b)
                kv, full, free = ((A, a_full, a_free), (S, s_full, s_free))[c % 2]
                dve.wait_ge(full, n * 3 + (2 + c // 2))
                mark(stt(cn[:, :], cn[:, :], sel[:, c, 2:3], kv[:, 0:DV1], ALU.mult, ALU.add).then_inc(free, 1), free, n * 3 + (2 + c // 2))

            def at_half(g, b, t, first):
                n = nth(g, b)
                if t == V and not (first and b == 0):
                    heads_out(g, b, t0(g, b, "hT", first))
                if t == Q:
                    dve.wait_ge(t0_full, t0(g, b, "kT", first) + 1)
                    mark(tt(chunks(kw[:, :]), chunks(T0[:, :]), wide(sel[:, :, 1], P), ALU.mult).then_inc(t0_free, 1), t0_free, t0(g, b, "kT", first) + 1)
                if t == ZC:
                    if b == 0:
                        dve.wait_ge(cn_meta, g + 1)
                    else:
                        dve.wait_ge(s_free, n * 3)
                    update(g, b, 0)
                if t == O:
                    dve.wait_ge(s_free, n * 3 + 2)
                    update(g, b, 2)
                if first:
                    for r in X_HALF.get(t, ()):
                        x_gain(1 + CH * (b + 1) + r // 2, r % 2, t0(g, b, ("x", r), first))
                        x_low_part(2 * (1 + CH * (b + 1)) + r)
                    if t == O:
                        gate_part(b + 2, tok0(b + 1), BT, block_segs(b + 1))

            def evacuate(g, b, t):
                n = nth(g, b)
                i, left = evacuations(g, b, t)
                src, free = PB[i][:, :], p_free[i]
                if t == HC:
                    if b:
                        did(copy(u[:, 0:2], u[:, BT:BT + 2]))
                    dve.wait_ge(tile_done, n * NT + (t + 1))
                    j, before = evacuations(g, b, GC)
                    dve.wait_ge(p_free[j], before + 1)
                    mark(stt(u[:, 2:], src, 1 / WS, gcs[:, :], ALU.mult, ALU.mult).then_inc(free, 1), free, left + 1)
                    dve.wait_ge(free, left + 1)
                    mark(ts(yc[:, :], u[:, 0:BT], cwt[:, bass.ds(g, 1), 0], None, ALU.mult).then_inc(gc_used, 1), gc_used, n + 1)
                    dve.wait_ge(gc_used, n + 1)
                    did(stt(yc[:, :], u[:, 1:1 + BT], cwt[:, bass.ds(g, 1), 1], yc[:, :], ALU.mult, ALU.add))
                    did(stt(yc[:, :], u[:, 2:2 + BT], cwt[:, bass.ds(g, 1), 2], yc[:, :], ALU.mult, ALU.add))
                    if b == NB - 1:
                        did(pick(cpo[:, bass.ds(g, 1), :].rearrange("p o j -> p (o j)"), u[:, BT:BT + 2]))
                if t == GB:
                    dve.wait_ge(tile_done, n * NT + (t + 1))
                    mark(stt(yc[:, :], src, 1 / WS, yc[:, :], ALU.mult, ALU.mult).then_inc(free, 1), free, left + 1)
                if t == ZC:
                    j, before = evacuations(g, b, GB)
                    dve.wait_ge(p_free[j], before + 1)
                    dve.wait_ge(tanh_zc, n + 1)
                    mark(stt(zs[:, :], tz[:, :], 1.0, src, ALU.add, ALU.mult).then_inc(free, 1), free, left + 1)
                    dve.wait_ge(free, left + 1)
                    mark(stt(yc[:, :], yc[:, :], 0.5 / WS, zs[:, :], ALU.mult, ALU.mult).then_inc(yc_ready, 1), yc_ready, n + 1)
                if t == ZM:
                    j, before = evacuations(g, b, O)
                    dve.wait_ge(p_free[j], before + 1)
                    did(ts(to[:, :], to[:, :], 1.0, mhg[:, bass.ds(g, 1)], ALU.add, ALU.mult))
                    dve.wait_ge(tanh_zm, n + 1)
                    mark(stt(zs[:, :], tz[:, :], 1.0, src, ALU.add, ALU.mult).then_inc(free, 1), free, left + 1)
                    dve.wait_ge(free, left + 1)
                    mark(stt(G[:, :], to[:, :], 0.25 / WS, zs[:, :], ALU.mult, ALU.mult).then_inc(g_done, 1), g_done, n + 1)

            def select(g, b, first):
                n = nth(g, b)
                if first or b == NB - 1:
                    dve.wait_ge(t1_free, COLS_COUNTS[b + 1] + 1)
                dve.wait_ge(tile_done, n * NT + 1)
                dve.wait_ge(rows_ready, b + 2)
                did(pick(sel[:, :, :], cols[:, 1 + CH * b:1 + CH * (b + 1), :, bass.ds(g, 1)]
                                          .rearrange("p c k o -> p c (k o)")))
                if b == 0:
                    did(pick(selm[:, :], cols[0:MIX, 0, 0:2, bass.ds(g, 1)].rearrange("p k o -> p (k o)")))
                    did(pick(dselm[:, :], decs[:, :, bass.ds(g, 1)].rearrange("p k o -> p (k o)")))
                    right_factors(g, rbm, 0, MIX)
                mark(right_factors(g, rb, tok0(b), BT).then_inc(rb_ready, 1), rb_ready, n + 1)

            def right_factors(g, out, tok, n):
                one = bass.ds(g, 1)
                k = -(-n // P)
                ts(out[0:H, :].rearrange("p (c t) -> p c t", c=k), ones[0:H, 0:n // k].unsqueeze(1).broadcast_to([H, k, n // k]),
                   selh[0:H, one], None, ALU.mult)
                ts(out[32:GR, :], rows[64:64 + H, tok:tok + n], seln[64:64 + H, one], None, ALU.mult)
                return ts(out[64:64 + H, :], rows[96:96 + H, tok:tok + n], selh[96:96 + H, one], None, ALU.mult)

            def at_end(g, b, t, first):
                n = nth(g, b)
                if t == K:
                    select(g, b, first)
                if t == Q:
                    dve.wait_ge(e_ready, n + 1)
                    mark(tt(eh[:, :], eh[:, :], qf[:, :], ALU.mult).then_inc(q_scaled, 1), q_scaled, n + 1)
                if t == GC:
                    dve.wait_ge(s_full, n * 3 + 1)
                    dve.wait_ge(a_free, n * 3 + 1)
                    mark(tt(dp[:, :], dp[:, :], S[:, :], ALU.mult).then_inc(s_free, 1), s_free, n * 3 + 1)
                if t == ZC:
                    dve.wait_ge(a_free, n * 3 + 2)
                    update(g, b, 1)
                    dve.wait_ge(yc_high, n + 1)
                    mark(tt(yst[:, 0, 1, :], yc[:, :], yst[:, 0, 0, :], ALU.subtract).then_inc(yc_low, 1), yc_low, n + 1)
                if t == O:
                    dve.wait_ge(a_free, n * 3 + 3)
                    update(g, b, 3)
                    if b == NB - 1:
                        dve.wait_ge(s_free, n * 3 + 3)
                        did(pick(npo[:, bass.ds(g, 1)], cn[:, P:DV1]))
                    dve.wait_ge(n_full, n + 1)
                    for i in range(2):
                        nv = N[i][:, 0:2 * DV1].rearrange("p (c v) -> p c v", c=2)
                        did(copy(den[:, 2 * i:2 * i + 2], nv[:, :, P]))
                    did(stt(den[:, :], den[:, :], -1.0, den[:, :], ALU.mult, ALU.max))
                    did(tt(den[:, :], den[:, :], sel[:, :, 0], ALU.max))
                    mark(reciprocal(rec[:, :], den[:, :]).then_inc(rec_ready, 1), rec_ready, n + 1)
                    dve.wait_ge(h_sq, n + 1)
                    mark(ts(hms[:, :], hss[:, :], 1.0 / P, EPS, ALU.mult, ALU.add).then_inc(h_ms, 1), h_ms, n + 1)
                    dve.wait_ge(h_rs, n + 1)
                    did(tt(hf[:, :], rec[:, :], hrs[:, :], ALU.mult))
                    for i in range(2):
                        nv = N[i][:, 0:2 * DV1].rearrange("p (c v) -> p c v", c=2)[:, :, 0:P]
                        last = tt(eh[:, 2 * P * i:2 * P * (i + 1)].rearrange("p (c v) -> p c v", c=2), nv,
                                  wide(hf[:, 2 * i:2 * i + 2], P), ALU.mult)
                    mark(last.then_inc(n_free, 1), n_free, n + 1)
                if b == 0:
                    mixed_end(g, b, t, first)
                if b == 1 and t in (V, Q, GC):
                    i0, i1 = SAMPLE_ROUNDS[t - V]
                    at = t1(g, b, ("state", t - V), first)
                    dve.wait_ge(t1_full, at + 1)
                    for i in range(i0, i1):
                        ins = stt(cs[:, i, :], cs[:, i, :], dselm[:, i:i + 1], T1[:, (i - i0) * DV1:(i - i0 + 1) * DV1], ALU.mult, ALU.add)
                        if i == i1 - 1:
                            mark(ins.then_inc(t1_free, 1), t1_free, at + 1)
                        else:
                            did(ins)
                    if t == GC:
                        dve.wait_ge(t1_free, at + 1)
                        mark(pick(nst[:, :, bass.ds(g, 1)].rearrange("p b o -> p (b o)"), cs[:, :, P]).then_inc(mx_states, 1), mx_states, g + 1)
                if first:
                    if t in (Q, GC, HC, GB):
                        x_prepare(1 + CH * (b + 1) + (Q, GC, HC, GB).index(t))
                    for r in X_END.get(t, ()):
                        x_gain(1 + CH * (b + 1) + r // 2, r % 2, t0(g, b, ("x", r), first))
                        x_low_part(2 * (1 + CH * (b + 1)) + r)
                    if b == 0 and t < NT - STAGES:
                        split_w(0, t + STAGES)

            def mixed_end(g, b, t, first):
                if t == Q:
                    dve.wait_ge(t1_free, t1(g, b, "args", first) + 1)
                    mark(tt(qdiag, samples(ehm), samples(qfm), ALU.mult).then_inc(mx_q, 1), mx_q, g + 1)
                if t == GC:
                    at = t1(g, b, "kv", first)
                    dve.wait_ge(t1_full, at + 1)
                    did(ts(kwm[:, :], T1[0:MIX, 0:P], selm[:, 1:2], None, ALU.mult))
                    mark(copy(v1m[:, 0:P], T1[0:MIX, P:2 * P]).then_inc(t1_free, 1), t1_free, at + 1)
                    dve.wait_ge(t1_free, at + 1)
                    mark(tt(v1x[:, :, :], v1m[:, :].unsqueeze(1).broadcast_to([MIX, DB, DV1]), wide(segind[:, :], DV1), ALU.mult)\
                        .then_inc(mx_v_wide, 1), mx_v_wide, g + 1)
                if t == HC:
                    at = t1(g, b, "score", first)
                    dve.wait_ge(t1_full, at + 1)
                    mark(tt(dpm[:, :], dpm[:, :], T1[0:MIX, 0:MIX], ALU.mult).then_inc(t1_free, 1), t1_free, at + 1)
                if t == GB:
                    at = t1(g, b, "num", first)
                    dve.wait_ge(t1_full, at + 1)
                    dve.wait_ge(cn_out, g * 16)
                    mark(copy(cn[:, :], T1[:, 2 * P:2 * P + DV1]).then_inc(cn_meta, 1), cn_meta, g + 1)
                    did(copy(hm[:, 0:1], T1[0:MIX, P:DV1]))
                    did(stt(hm[:, 0:1], hm[:, 0:1], -1.0, hm[:, 0:1], ALU.mult, ALU.max))
                    did(tt(hm[:, 0:1], hm[:, 0:1], selm[:, 0:1], ALU.max))
                    mark(reciprocal(hm[:, 1:2], hm[:, 0:1]).then_inc(mx_rec, 1), mx_rec, g + 1)
                    dve.wait_ge(mx_sq, g + 1)
                    mark(ts(hm[:, 3:4], hm[:, 2:3], 1.0 / P, EPS, ALU.mult, ALU.add).then_inc(mx_ms, 1), mx_ms, g + 1)
                    dve.wait_ge(mx_rs, g + 1)
                    did(tt(hm[:, 5:6], hm[:, 1:2], hm[:, 4:5], ALU.mult))
                    mark(ts(hnm[:, :], T1[0:MIX, 0:P], hm[:, 5:6], None, ALU.mult).then_inc(t1_free, 1), t1_free, at + 1)
                if t == ZC:
                    dve.wait_ge(mx_yc_high, g + 1)
                    mark(tt(ystm[:, 0, 1, :], ycm[:, :], ystm[:, 0, 0, :], ALU.subtract).then_inc(mx_yc_low, 1), mx_yc_low, g + 1)
                if t == ZM:
                    dve.wait_ge(mx_ym_high, g + 1)
                    mark(tt(ystm[:, 1, 1, :], ymm[:, :], ystm[:, 1, 0, :], ALU.subtract).then_inc(mx_ym_low, 1), mx_ym_low, g + 1)

            def dve_block(g, b, first, following):
                for t in range(NT):
                    if b == 0:
                        mixed_start(g, b, t, first)
                    at_half(g, b, t, first)
                    evacuate(g, b, t)
                    at_end(g, b, t, first)
                    if following == "weights":
                        split_w(g + 1, t)
                    if following == "output weights" and t < KT:
                        dve.wait_ge(wo_high, t + 1)
                        mark(stt(Wol[:, :, t * P:(t + 1) * P], wst[t % STAGES][:, :, :], WS, Woh[:, :, t * P:(t + 1) * P],
                            ALU.mult, ALU.subtract).then_inc(wo_low, 1), wo_low, t + 1)

            GATE_COUNTS = [0, 2] + [t1(0, b, "gates", True) for b in range(NB - 1)]
            COLS_COUNTS = [1, 3] + [t1(0, b, "cols", True) for b in range(NB - 1)]

            dve.wait_ge(const, CONSTS)
            did(memset(selh[:, :], 0.0))
            did(copy(identb[:, :], ident[:, :]))
            for q in range(4):
                did(copy(selh[32 * q:32 * q + H, :], ident[32 * q:32 * q + H, 32 * q:32 * q + H]))
            did(ts(seln[:, :], selh[:, :], -1.0, None, ALU.mult))
            dve.wait_ge(par_in, 16 * 5)
            x_prepare(0)
            dve.wait_ge(g_high, 1)
            did(stt(Wgl[:, :, 0:H], wgst[:, :, H:2 * H], WS, Wgh[:, :, 0:H], ALU.mult, ALU.subtract))
            mark(stt(Wgl[:, :, 32:GR], wgst[:, :, 0:H], WS, Wgh[:, :, 32:GR], ALU.mult, ALU.subtract).then_inc(g_low, 1), g_low, 1)
            for r in range(2):
                x_gain(0, r, r)
                x_low_part(r)
            for c in range(CH):
                x_prepare(1 + c)
                if c == 1:
                    gate_part(0, 0, MIX, [(0, META, (mst[:, 0:1], mst[:, 1:2]))] +
                              [(at, n, (sm0[:, i:i + 1], None)) for i, (at, n) in enumerate(SEGS[1:])])
                if c < STAGES:
                    split_w(0, c)
                for r in range(2):
                    x_gain(1 + c, r, 2 + 2 * c + r)
                    x_low_part(2 * (1 + c) + r)
            gate_part(1, MIX, BT, block_segs(0))
            dve.wait_ge(par2_in, 16 * 8)
            dve.wait_ge(const2, CONSTS2)
            for b in range(NB - 1):
                dve_block(0, b, True, None)
            with dve.Fori(1, H) as g:
                order.enter(g)
                dve_block(g - 1, NB - 1, False, "weights")
                for b in range(NB - 1):
                    dve_block(g, b, False, None)
            order.leave(H - 1)
            dve_block(H - 1, NB - 1, False, "output weights")
            heads_out(H, 0, t0(H, 0, "hT", False) - t0_uses(0, False).index("hT"))
            mark(memset(den[:, 0:1], 0.0).then_inc(finals, 1), finals, 1)

            def b_tile(tile, n, i, c, half_count):
                dve.wait_ge(r_in[i], half_count * 16 + 16)
                for h in range(2):
                    dve.wait_ge(b_full, tile * 2 + (h + 1))
                    z = xs[i][0:n, h * BT:(h + 1) * BT]
                    mark(stt(z, OUT[i][h][0:n, :], 1 / WS, z, ALU.mult, ALU.add).then_inc(b_free, 1), b_free, tile * 2 + (h + 1))
                dve.wait_ge(b_sq, tile + 1)
                mark(ts(msx[0:n, c:c + 1], ssx[0:n, c:c + 1], 1.0 / D, EPS, ALU.mult, ALU.add).then_inc(b_ms, 1), b_ms, tile + 1)
                dve.wait_ge(b_rs, tile + 1)
                dve.wait_ge(b_store[i], half_count * 16)
                mark(stt(result[i][0:n, :], xs[i][0:n, :], rsx[0:n, c:c + 1], fgain[0:n, :], ALU.mult, ALU.mult).then_inc(b_out, 1), b_out, tile + 1)

            dve.wait_ge(fg_in, 16)
            b_tile(0, DB * DS, 0, 0, 0)
            with dve.Fori(0, NB) as j:
                for c in range(CH):
                    b_tile(j * CH + (1 + c), P, (1 + c) % 2, 1 + c, j * 2 + (1 + c) // 2)


_INS = ['x_prompt', 'x_sample', 'state_conv', 'state_mlstm_c', 'state_mlstm_n', 'state_mlstm_m', 'meta_tokens',
        'norm_gain', 'w_in', 'conv_w', 'b_igate', 'b_fgate', 'mh_norm_gain', 'w_out', 'final_norm_gain']
_OUTS = [(1, SEQ, D), (DB, DS, D), (1, 2, CW), (1, H, P, P), (1, H, P), (1, H),
         (DB, 2, CW), (DB, H, P, P), (DB, H, P), (DB, H)]


def kernel(**inputs):
    import numpy as _np
    import concourse.bacc as _bacc
    from concourse import mybir as _mybir
    from concourse.bass_utils import run_bass_kernel_spmd as _run

    nc = _bacc.Bacc("TRN2", target_bir_lowering=False, num_devices=1)
    arrays, args = {}, []
    for name in _INS:
        a = _np.ascontiguousarray(inputs[name])
        arrays[f"in_{name}"] = a
        args.append(nc.dram_tensor(f"in_{name}", a.shape, _mybir.dt.from_np(a.dtype), kind="ExternalInput").ap())
    for i, shape in enumerate(_OUTS):
        args.append(nc.dram_tensor(f"out_{i}", shape, _mybir.dt.float32, kind="ExternalOutput").ap())
    args.append(nc.dram_tensor("y_mid", (KT, P, 2, NTOK), _mybir.dt.float16, kind="Internal").ap())
    build(nc, *args)
    r = _run(nc, [arrays], core_ids=[0])
    return tuple(r.results[0][f"out_{i}"] for i in range(len(_OUTS)))
```

```python
import concourse.bass as bass
from concourse import mybir
from contextlib import ExitStack

F32 = mybir.dt.float32
F16 = mybir.dt.float16
BF16 = mybir.dt.bfloat16
ALU = mybir.AluOpType
ACT = mybir.ActivationFunctionType

P = 128
D = 1024
KT = D // P
SEQ = 2048
META = 16
DB, DS = 8, 8
MIX = META + DB * DS
H = 4
CW = 512
NB, CH = 4, 4
BT = CH * P
NTOK = MIX + SEQ
EPS = 1e-6
NEG = -1.0e30
WS = 64.0
SK = float(P) ** -0.5
K, V, Q, GC, HC, GB, ZC, O, ZM = range(9)
NT = 9
TILE_COL = {GB: 0, GC: CW, HC: 2 * CW, ZC: 3 * CW, Q: 4 * CW, K: 5 * CW, V: 6 * CW, O: 7 * CW, ZM: 8 * CW}
IG_COL, FG_COL = 9 * CW, 9 * CW + H
GR = 32 + H
DV1 = P + 1
STAGES = 3
XBUF = 3
SEGS = [(0, META)] + [(META + DS * i, DS) for i in range(DB)]
SAMPLE_ROUNDS = [(0, 3), (3, 6), (6, 8)]

T0_PRO = 2 + 2 * CH
T1_PRO = 2
X_HALF = {HC: (3,), GB: (5,), ZC: (7,)}
X_END = {V: (0,), Q: (1,), GC: (2,), HC: (4,), GB: (6,)}
X_SQUARE = {K: 0, Q: 1, GC: 2, HC: 3}
DVE_TURN = 63
ACT_TURN = 13


def t0_uses(b, first):
    names = []
    for t in range(NT):
        names += [("mix", t)] if b == 0 else []
        names += {V: [] if first and b == 0 else ["hT"], Q: ["kT"], GC: ["vT"]}.get(t, [])
        names += [("x", r) for r in X_HALF.get(t, ()) + X_END.get(t, ())] if first else []
    return names


def t1_uses(b, first):
    names = []
    for t in range(NT):
        names += {K: ["mix cols"] if b == 0 else [], Q: ["cols"]}.get(t, []) if first else []
        names += {Q: ["args"], GC: ["kv"], HC: ["score"], GB: ["num"], O: ["hT"]}.get(t, []) if b == 0 else []
        names += [("state", t - V)] if b == 1 and t in (V, Q, GC) else []
        names += {ZC: ["gates"], ZM: ["next cols"] if b == NB - 2 else []}.get(t, []) if first else []
    return names


def ordinal(uses, before, g, b, name, first):
    turn = sum(len(uses(x, False)) for x in range(NB))
    start = before + sum(len(uses(x, True)) for x in range(NB - 1))
    if first:
        return before + sum(len(uses(x, True)) for x in range(b)) + uses(b, True).index(name)
    if b == NB - 1:
        return g * turn + (start + uses(b, False).index(name))
    inside = len(uses(NB - 1, False)) + sum(len(uses(x, False)) for x in range(b))
    return (g - 1) * turn + (start + inside + uses(b, False).index(name))


def t0(g, b, name, first):
    return ordinal(t0_uses, T0_PRO, g, b, name, first)


def t1(g, b, name, first):
    return ordinal(t1_uses, T1_PRO, g, b, name, first)


def tok0(b):
    return MIX + BT * b


def nth(g, b):
    return g * NB + b


class Order:

    def __init__(self, eng, sem, per_turn):
        self.eng, self.sem, self.per_turn, self.n, self.base, self.last = eng, sem, per_turn, 0, 0, None

    def did(self, instruction):
        instruction.then_inc(self.sem, 1)
        self.n += 1
        self.last = (self.sem, self.base + self.n)

    def mark(self, instruction, sem, value):
        self.last = (sem, value)

    def settle(self):
        if self.last:
            self.eng.wait_ge(*self.last)

    def after(self, op):
        def run(*operands, **named):
            self.settle()
            return op(*operands, **named)
        return run

    def enter(self, g):
        self.settle()
        self.start, self.base, self.last = self.n, (g - 1) * self.per_turn, None

    def leave(self, turns):
        assert self.n - self.start == self.per_turn, (self.sem, self.n - self.start, self.per_turn)
        self.base, self.last = (turns - 1) * self.per_turn, None


def build(nc, x_prompt, x_sample, state_conv, state_c, state_n, state_m, meta, norm_gain, w_in, conv_w,
          b_igate, b_fgate, mh_gain, w_out, final_gain, y_prompt, y_sample, conv_p, c_p, n_p, m_p,
          conv_s, c_s, n_s, m_s, y_mid):
    ctx = ExitStack()
    with ctx:
        ctx.enter_context(nc.allow_non_contiguous_dma(reason="small parameters and states"))

        def sb(name, shape, dt=F32):
            return ctx.enter_context(nc.sbuf_tensor(name, shape, dt))

        def sem(name):
            return ctx.enter_context(nc.semaphore(name))

        xTh, xTl = sb("xTh", [P, KT, NTOK], F16), sb("xTl", [P, KT, NTOK], F16)
        Wh, Wl = sb("Wh", [P, NT, KT, P], F16), sb("Wl", [P, NT, KT, P], F16)
        Wgh, Wgl = sb("Wgh", [P, KT, GR], F16), sb("Wgl", [P, KT, GR], F16)
        rows = sb("rows", [P, NTOK])
        cols = sb("cols", [P, 1 + NB * CH, 3, H])
        decs = sb("decs", [P, DB, H])
        Woh, Wol = xTh[:, :, 0:D], xTl[:, :, 0:D]
        ybuf = [x[:, :, D + META:D + META + BT].rearrange("p k (s t) -> p k s t", s=2) for x in (xTh, xTl)]
        wst = [sb(f"wst{i}", [P, KT, P]) for i in range(STAGES)]
        result = [w[:, :, :].rearrange("p k c -> p (k c)") for w in wst[0:2]]
        wgst = sb("wgst", [P, KT, 2 * H])
        xs = [sb(f"xs{i}", [P, D]) for i in range(XBUF)]
        junk = sb("junk", [P, D], F16)
        xtmp = [sb(f"xtmp{i}", [P, BT]) for i in range(2)]
        fgain = sb("fgain", [P, D])
        ident, ones = sb("ident", [P, P]), sb("ones", [P, P])
        identb, maskb = sb("identb", [P, P], BF16), sb("maskb", [P, P], BF16)
        mixmask = sb("mixmask", [MIX, MIX], BF16)
        segind = sb("segind", [MIX, DB])
        selh, seln = sb("selh", [P, H]), sb("seln", [P, H])
        gain, cwt, mhg = sb("gain", [P, KT]), sb("cwt", [P, H, 3]), sb("mhg", [P, H])
        biasg, halves = sb("biasg", [GR, 1]), sb("halves", [P, CH])
        gwork = sb("gwork", [64 + GR, BT])
        grow, trr = gwork[0:GR, :], gwork[64:64 + GR, :]
        gt, lf = fgain[0:H, 0:BT], fgain[0:H, BT:2 * BT]
        mst = sb("mst", [H, NB * CH + 2])
        sm0, smn = sb("sm0", [H, DB]), sb("smn", [H, DB])
        restart, remix, forget = sb("restart", [H, BT]), sb("remix", [H, MIX]), sb("forget", [H, DB * DS])
        rl, drl = sb("rl", [H, DB]), sb("drl", [H, DB * H])
        rb, rbm = sb("rb", [68, BT]), sb("rbm", [68, MIX])
        kf, vf, qf = sb("kf", [P, BT]), sb("vf", [P, BT]), sb("qf", [P, BT])
        v1 = sb("v1", [P, CH, DV1])
        dp = sb("dp", [P, BT])
        eh = sb("eh", [P, BT])
        kw = sb("kw", [P, BT])
        u, gcs, yc, zs = sb("u", [P, BT + 2]), sb("gcs", [P, BT]), sb("yc", [P, BT]), sb("zs", [P, BT])
        tz, to, G = sb("tz", [P, BT]), sb("to", [P, BT]), sb("G", [P, BT])
        bcum, mrow = G[0:H, :], zs[0:H, :]
        sel, cn = sb("sel", [P, CH, 3]), sb("cn", [P, DV1])
        den, rec, hss, hms, hrs, hf = (sb(n, [P, CH]) for n in ("den", "rec", "hss", "hms", "hrs", "hf"))
        yst = sb("yst", [P, 2, 2, BT], F16)
        kfm, vfm, qfm, gcm, ycm, zsm, tzm, tom, Gm, ehm, ymm = (
            sb(n, [P, MIX]) for n in ("kfm", "vfm", "qfm", "gcm", "ycm", "zsm", "tzm", "tom", "Gm", "ehm", "ymm"))
        um = sb("um", [P, META + 2 + DB * (DS + 2)])
        dpm, kwm, hnm = sb("dpm", [MIX, MIX]), sb("kwm", [MIX, P]), sb("hnm", [MIX, P])
        v1m, v1x = sb("v1m", [MIX, DV1]), sb("v1x", [MIX, DB, DV1])
        qm = sb("qm", [P, DB * (MIX + DS)])
        cs = sb("cs", [P, DB, DV1])
        selm, dselm = sb("selm", [MIX, 2]), sb("dselm", [P, DB])
        hm = sb("hm", [MIX, 6])
        ystm = sb("ystm", [P, 2, 2, MIX], F16)
        nst, npo = sb("nst", [P, DB, H]), sb("npo", [P, H])
        cst, cpo = sb("cst", [P, H, DB * 2]), sb("cpo", [P, H, 2])
        ssx, msx, rsx = sb("ssx", [P, 17]), sb("msx", [P, 17]), sb("rsx", [P, 17])

        bank = [ctx.enter_context(nc.psum_tensor(f"bank{i}", [P, BT], F32)) for i in range(8)]
        PB, T0, T1, A, S, N = bank[0:2], bank[2], bank[3], bank[4], bank[5], bank[6:8]
        OUT = [bank[0:2], bank[4:6]]

        par_in, gain_in, par2_in, gate_in, fg_in, cs_in = (sem(n) for n in ("par_in", "gain_in", "par2_in", "gate_in", "fg_in", "cs_in"))
        x_in = [sem(f"x_in{i}") for i in range(XBUF)]
        w_in_s = [sem(f"w_in{i}") for i in range(STAGES)]
        const, rows_const, const2, bias_clear = (sem(n) for n in ("const", "rows_const", "const2", "bias_clear"))
        w_high, w_low, g_high, g_low = sem("w_high"), sem("w_low"), sem("g_high"), sem("g_low")
        x_sq, x_ms, x_rs, x_scaled = sem("x_sq"), sem("x_ms"), sem("x_rs"), sem("x_scaled")
        x_high, x_low = sem("x_high"), sem("x_low")
        tile_done, p_free = sem("tile_done"), [sem("p0_free"), sem("p1_free")]
        t0_full, t0_free, t1_full, t1_free = sem("t0_full"), sem("t0_free"), sem("t1_full"), sem("t1_free")
        a_full, a_free, s_full, s_free = sem("a_full"), sem("a_free"), sem("s_full"), sem("s_free")
        e_full, e_ready, n_full, n_free = sem("e_full"), sem("e_ready"), sem("n_full"), sem("n_free")
        gate_rows, g_abs, g_exp, g_ln, rows_ready, cols_ready = (
            sem(n) for n in ("gate_rows", "g_abs", "g_exp", "g_ln", "rows_ready", "cols_ready"))
        rb_ready, q_scaled, gc_used = sem("rb_ready"), sem("q_scaled"), sem("gc_used")
        tanh_zc, tanh_zm, g_done = sem("tanh_zc"), sem("tanh_zm"), sem("g_done")
        rec_ready, h_sq, h_ms, h_rs = sem("rec_ready"), sem("h_sq"), sem("h_ms"), sem("h_rs")
        yc_ready, yc_high, yc_low, ym_high, ym_low = (
            sem(n) for n in ("yc_ready", "yc_high", "yc_low", "ym_high", "ym_low"))
        y_out_c, y_out_m = sem("y_out_c"), sem("y_out_m")
        mx_exp, mx_q, mx_tanh_zc, mx_tanh_zm, mx_gc_used, mx_g = (
            sem(n) for n in ("mx_exp", "mx_q", "mx_tanh_zc", "mx_tanh_zm", "mx_gc_used", "mx_g"))
        mx_rec, mx_sq, mx_ms, mx_rs, mx_yc, mx_yc_high, mx_yc_low, mx_ym_high, mx_ym_low = (
            sem(n) for n in ("mx_rec", "mx_sq", "mx_ms", "mx_rs", "mx_yc", "mx_yc_high", "mx_yc_low",
                             "mx_ym_high", "mx_ym_low"))
        mx_out_c, mx_out_m, mx_v, mx_v_wide, mx_n, mx_states, cs_out = (
            sem(n) for n in ("mx_out_c", "mx_out_m", "mx_v", "mx_v_wide", "mx_n", "mx_states", "cs_out"))
        cn_meta, cn_out, dve_step, act_step, pool_step, out_sem = (
            sem(n) for n in ("cn_meta", "cn_out", "dve_step", "act_step", "pool_step", "out_sem"))
        wo_high, wo_low, finals = sem("wo_high"), sem("wo_low"), sem("finals")
        y_in, r_in, b_store = ([sem(f"{n}{i}") for i in range(2)] for n in ("y_in", "r_in", "b_store"))
        b_full, b_free, b_sum, b_sq, b_ms, b_rs, b_out = (
            sem(n) for n in ("b_full", "b_free", "b_sum", "b_sq", "b_ms", "b_rs", "b_out"))

        useg = um[:, META + 2:].rearrange("p (b t) -> p b t", t=DS + 2)
        qdiag = qm[:, :].rearrange("p (b t) -> p b t", t=MIX + DS)[:, :, META:META + DS]

        def samples(ap):
            return ap[:, META:MIX].rearrange("p (b t) -> p b t", t=DS)

        def wide(ap, n):
            return ap.unsqueeze(2).broadcast_to([ap.shape[0], ap.shape[1], n])

        def evacuations(g, b, t):
            j = NT * b + t
            return j % 2, g * (NT * NB // 2) + j // 2

        def chunks(ap):
            return ap.rearrange("p (c t) -> p c t", c=CH)

        def load_w(queue, g, t):
            src = w_in[:, bass.ds(g * P + TILE_COL[t], P)].rearrange("(k p) c -> p k c", p=P)
            queue.dma_start(wst[t % STAGES][:, :, :], src).then_inc(w_in_s[t % STAGES], 16)

        def load_states(queue, g):
            src = state_c[:, bass.ds(g, 1), :, :].rearrange("b h d v -> d (b h) v")
            queue.dma_start(cs[:, :, 0:P], src).then_inc(cs_in, 16)

        block = ctx.enter_context(nc.Block())

        @block.sync
        def _(sp):
            def load_x(unit):
                s = unit % XBUF
                if unit >= XBUF:
                    sp.wait_ge(t0_full, t0_after_x(unit - XBUF))
                if unit == 0:
                    sp.dma_start(xs[0][0:META, :], meta).then_inc(x_in[0], 16)
                    sp.dma_start(xs[0][META:MIX, :], x_sample.rearrange("b t d -> (b t) d")).then_inc(x_in[0], 16)
                else:
                    r = (unit - 1) * P
                    sp.dma_start(xs[s][:, :], x_prompt[0, r:r + P, :]).then_inc(x_in[s], 16)

            def t0_after_x(unit):
                if unit <= CH:
                    return 2 * unit + 2
                b, c = divmod(unit - 1 - CH, CH)
                return t0(0, b, ("x", 2 * c + 1), True) + 1

            load_x(0)
            load_x(1)
            load_x(2)
            load_w(sp, 0, 0)
            load_w(sp, 0, 1)
            load_w(sp, 0, 2)
            load_x(3)
            load_x(4)
            load_states(sp, 0)
            for j in range(3):
                sp.dma_start(cwt[:, :, j], conv_w[j, :].rearrange("(h p) -> p h", p=P)).then_inc(par2_in, 16)
            sp.dma_start(nst[:, :, :].rearrange("p b h -> p (b h)"), state_n.rearrange("b h p -> p (b h)")).then_inc(par2_in, 16)
            for h in range(H):
                sp.dma_start(cst[:, h, :], state_conv[:, :, h * P:(h + 1) * P].rearrange("b j p -> p (b j)")).then_inc(par2_in, 16)
            load_x(5)
            for t in range(STAGES, NT):
                sp.wait_ge(w_low, t - STAGES + 1)
                load_w(sp, 0, t)
                if t - STAGES in (1, 3):
                    load_x(6 + (t - STAGES) // 2)
            for unit in range(2 * CH, 1 + CH * NB):
                load_x(unit)
            for t in range(KT):
                if t < STAGES:
                    sp.wait_ge(w_low, NT * H - STAGES + t + 1)
                else:
                    sp.wait_ge(wo_low, t - STAGES + 1)
                sp.dma_start(wst[t % STAGES][:, :, :],
                             w_out[:, t * P:(t + 1) * P].rearrange("(k p) c -> p k c", p=P)).then_inc(w_in_s[t % STAGES], 16)

            def load_y(slot, tok, n):
                for k in range(KT):
                    sp.dma_start(ybuf[slot][:, k, :, 0:n], y_mid[k, :, :, bass.ds(tok, n)]).then_inc(y_in[slot], 16)

            sp.dma_start(fgain[:, :], final_gain.rearrange("(o d) -> o d", o=1).broadcast_to([P, D])).then_inc(fg_in, 16)
            sp.wait_ge(mx_out_c, 16 * H)
            sp.wait_ge(mx_out_m, 16 * H)
            sp.wait_ge(tile_done, NT * (NB * H - 1) + 1)
            load_y(0, META, DB * DS)
            sp.wait_ge(x_scaled, 17)
            sp.dma_start(xs[0][0:DB * DS, :], x_sample.rearrange("b t d -> (b t) d")).then_inc(r_in[0], 16)
            for j in range(NB):
                sp.wait_ge(y_out_c, (j + (NB * (H - 1) + 1)) * 16)
                sp.wait_ge(y_out_m, (j + (NB * (H - 1) + 1)) * 16)
                for c in range(CH):
                    if c % 2 == 0:
                        slot = 1 - c // 2
                        sp.wait_ge(b_full, j * (2 * CH) + (0 if slot else 2))
                        load_y(slot, j * BT + (MIX + c * P), 2 * P)
                    i = (1 + c) % 2
                    sp.wait_ge(b_out, j * CH + c)
                    sp.dma_start(xs[i][:, :], x_prompt[0, bass.ds(j * BT + c * P, P), :]).then_inc(r_in[i], 16)

        @block.gpsimd
        def _(pool):
            made = [0]

            def step(ins):
                ins.then_inc(pool_step, 1)
                made[0] += 1
                pool.wait_ge(pool_step, made[0])

            pool.memset(biasg[:, :], 0.0).then_inc(bias_clear, 1)
            pool.wait_ge(bias_clear, 1)
            step(pool.memset(ident[:, :], 0.0))
            step(pool.affine_select(out=ident[:, :], in_=ident[:, :], compare_op=ALU.not_equal, fill=1.0, base=0,
                                    pattern=[[-1, P]], channel_multiplier=1))
            step(pool.memset(halves[:, :], -0.5))
            step(pool.memset(Wgh[:, :, :], 0.0))
            pool.memset(Wgl[:, :, :], 0.0).then_inc(const, 1)
            pool.wait_ge(const, 1)

            def x_power(unit):
                n = MIX if unit == 0 else P
                pool.wait_ge(x_sq, unit + 1)
                pool.tensor_scalar(msx[0:n, unit:unit + 1], ssx[0:n, unit:unit + 1], 1.0 / D, EPS, ALU.mult, ALU.add).then_inc(x_ms, 1)
                pool.wait_ge(x_ms, unit + 1)
                pool.tensor_tensor(rsx[0:n, unit:unit + 1], msx[0:n, unit:unit + 1], halves[0:n, 0:1], ALU.pow).then_inc(x_rs, 1)

            x_power(0)
            x_power(1)
            step(pool.memset(ones[:, :], 1.0))
            step(pool.memset(trr, 0.0))
            step(pool.memset(mst[:, :], 0.0))
            for tile, first_of, rest, start in ((restart, chunks(restart[:, :]), 1.0, 0.0), (remix, samples(remix), 1.0, 0.0),
                                               (forget, forget[:, :].rearrange("p (b t) -> p b t", t=DS), 0.0, NEG)):
                step(pool.memset(tile[:, :], rest))
                step(pool.memset(first_of[:, :, 0], start))
            step(pool.memset(rows[0:32, :], 0.0))
            step(pool.memset(rows[32:GR, :], 1.0))
            pool.memset(rb[:, :], 0.0).then_inc(rows_const, 1)
            pool.wait_ge(rows_const, 1)
            x_power(2)
            step(pool.memset(maskb[:, :], 0.0))
            step(pool.affine_select(out=maskb[:, :], in_=maskb[:, :], compare_op=ALU.is_ge, fill=NEG, base=0,
                                    pattern=[[1, P]], channel_multiplier=-1))
            step(pool.tensor_copy(mixmask[:, :], maskb[0:MIX, 0:MIX]))
            x_power(3)
            step(pool.memset(v1[:, :, P:DV1], 1.0))
            step(pool.memset(um[:, 0:2], 0.0))
            step(pool.memset(v1m[:, P:DV1], 1.0))
            step(pool.memset(rbm[:, :], 0.0))
            x_power(4)
            step(pool.memset(qm[:, :], 0.0))
            for at, n in SEGS[1:]:
                step(pool.affine_select(out=mixmask[:, at:at + n], in_=mixmask[:, at:at + n], compare_op=ALU.is_ge,
                                        fill=NEG, base=-at, pattern=[[0, n]], channel_multiplier=1))
            step(pool.memset(segind[:, :], 1.0))
            step(pool.affine_select(out=segind[:, :], in_=segind[:, :], compare_op=ALU.is_ge, fill=0.0, base=-META,
                                    pattern=[[-DS, DB]], channel_multiplier=1))
            pool.affine_select(out=segind[:, :], in_=segind[:, :], compare_op=ALU.is_ge, fill=0.0, base=META + DS - 1,
                               pattern=[[DS, DB]], channel_multiplier=-1).then_inc(const2, 1)
            pool.wait_ge(const2, 1)

            def store_y(g, b, part):
                done, out = ((yc_low, y_out_c), (ym_low, y_out_m))[part]
                pool.wait_ge(done, nth(g, b) + 1)
                dst = y_mid[bass.ds(g + H * part, 1), :, :, tok0(b):tok0(b) + BT].rearrange("k p s t -> p (k s) t")
                pool.dma_start(dst, yst[:, part, :, :]).then_inc(out, 16)

            def store_mixed(g, part):
                done, out = ((mx_yc_low, mx_out_c), (mx_ym_low, mx_out_m))[part]
                pool.wait_ge(done, g + 1)
                dst = y_mid[bass.ds(g + H * part, 1), :, :, 0:MIX].rearrange("k p s t -> p (k s) t")
                pool.dma_start(dst, ystm[:, part, :, :]).then_inc(out, 16)

            def pool_block(g, b, first):
                if first:
                    x_power(1 + CH * (b + 1))
                if not (first and b == 0):
                    store_y(g if b else g - 1, b - 1 if b else NB - 1, 1)
                if first:
                    for c in range(1, CH):
                        x_power(1 + CH * (b + 1) + c)
                if b == 0:
                    pool.wait_ge(mx_ms, g + 1)
                    pool.tensor_tensor(hm[:, 4:5], hm[:, 3:4], halves[0:MIX, 0:1], ALU.pow).then_inc(mx_rs, 1)
                    store_mixed(g, 0)
                if b == 1:
                    pool.wait_ge(mx_states, g + 1)
                    dst = c_s[:, bass.ds(g, 1), :, :].rearrange("b h d v -> d (b h) v")
                    pool.dma_start(dst, cs[:, :, 0:P]).then_inc(cs_out, 16)
                store_y(g, b, 0)
                pool.wait_ge(h_ms, nth(g, b) + 1)
                pool.tensor_tensor(hrs[:, :], hms[:, :], halves[:, :], ALU.pow).then_inc(h_rs, 1)
                if b == 0:
                    store_mixed(g, 1)
                if b == NB - 1:
                    pool.wait_ge(s_free, nth(g, b) * 3 + 3)
                    pool.dma_start(c_p[0, bass.ds(g, 1), :, :].rearrange("h d v -> d (h v)"), cn[:, 0:P]).then_inc(cn_out, 16)

            for b in range(NB - 1):
                pool_block(0, b, True)
            with pool.Fori(1, H) as g:
                pool_block(g - 1, NB - 1, False)
                for b in range(NB - 1):
                    pool_block(g, b, False)
            pool_block(H - 1, NB - 1, False)
            store_y(H - 1, NB - 1, 1)

            def b_tile(tile, n, c, dst):
                pool.wait_ge(b_ms, tile + 1)
                pool.tensor_tensor(rsx[0:n, c:c + 1], msx[0:n, c:c + 1], halves[0:n, 0:1], ALU.pow).then_inc(b_rs, 1)
                pool.wait_ge(b_out, tile + 1)
                pool.dma_start(dst, result[c % 2][0:n, :]).then_inc(b_store[c % 2], 16)

            pool.wait_ge(finals, 1)
            pool.dma_start(n_s.rearrange("b h p -> p (b h)"), nst[:, :, :].rearrange("p b h -> p (b h)")).then_inc(out_sem, 16)
            pool.dma_start(n_p[0].rearrange("h p -> p h"), npo[:, :]).then_inc(out_sem, 16)
            pool.dma_start(m_p.rearrange("o h -> h o"), mst[:, NB * CH + 1:NB * CH + 2]).then_inc(out_sem, 16)
            pool.dma_start(m_s.rearrange("b h -> h b"), smn[:, :]).then_inc(out_sem, 16)
            for h in range(H):
                pool.dma_start(conv_s[:, :, h * P:(h + 1) * P].rearrange("b j p -> p (b j)"), cst[:, h, :]).then_inc(out_sem, 16)
                pool.dma_start(conv_p[0, :, h * P:(h + 1) * P].rearrange("j p -> p j"), cpo[:, h, :]).then_inc(out_sem, 16)
            b_tile(0, DB * DS, 0, y_sample.rearrange("b t d -> (b t) d"))
            with pool.Fori(0, NB) as j:
                for c in range(CH):
                    b_tile(j * CH + (1 + c), P, 1 + c, y_prompt[0, bass.ds(j * BT + c * P, P), :])
            pool.wait_ge(b_store[0], 16 * 9)
            pool.wait_ge(b_store[1], 16 * 8)
            pool.wait_ge(out_sem, 16 * 12)
            pool.wait_ge(cs_out, 16 * H)
            pool.wait_ge(cn_out, 16 * H)

        @block.tensor
        def _(pe):
            mm = nc.tensor.matmul

            def split_product(out, wh, wl, k0, k1, tok, n):
                for k in range(k0, k1):
                    xh, xl = xTh[:, k, tok:tok + n], xTl[:, k, tok:tok + n]
                    mm(out, wh[:, k, :], xh, start=(k == 0), stop=False)
                    mm(out, wh[:, k, :], xl, start=False, stop=False)
                    last = mm(out, wl[:, k, :], xh, start=False, stop=(k == KT - 1))
                return last

            def use_t0(count):
                pe.wait_ge(t0_free, count)

            def use_t1(count):
                pe.wait_ge(t1_free, count)

            def x_round(unit, r, count):
                n = MIX if unit == 0 else P
                pe.wait_ge(x_scaled, unit + 1)
                use_t0(count)
                for k in range(4):
                    last = nc.tensor.transpose(T0[:, k * n:k * n + n], xs[unit % XBUF][0:n, (4 * r + k) * P:(4 * r + k + 1) * P],
                                               ident[0:n, 0:n])
                last.then_inc(t0_full, 1)

            def gates(rounds, tok, n, count):
                pe.wait_ge(x_low, rounds)
                use_t1(count)
                split_product(T1[0:GR, 0:n], Wgh, Wgl, 0, KT, tok, n).then_inc(t1_full, 1)

            def columns(units, n, segs, count):
                pe.wait_ge(rows_const, 1)
                pe.wait_ge(rows_ready, units)
                use_t1(count)
                for c in range(1 if n == MIX else CH):
                    nc.tensor.transpose(T1[0:min(n, P), c * 64:c * 64 + GR], trr[:, c * P:c * P + min(n, P)], ident[64:64 + GR, 64:64 + GR])
                mm(T1[:, 256:256 + segs * H], ones[0:H, :], drl[:, 0:segs * H], start=True, stop=True).then_inc(t1_full, 1)

            def transposed(src, count):
                use_t0(count)
                for c in range(CH):
                    last = nc.tensor.transpose(T0[:, c * P:(c + 1) * P], src[:, c * P:(c + 1) * P], ident[:, :])
                last.then_inc(t0_full, 1)

            def chunk(g, b, c, first):
                n = nth(g, b)
                out = N[c // 2][:, (c % 2) * DV1:(c % 2 + 1) * DV1]
                if c == 0:
                    pe.wait_ge(s_free, n * 3 + 1)
                    pe.wait_ge(q_scaled, n + 1)
                    pe.wait_ge(t0_free, t0(g, b, "vT", first) + 1)
                    if b == 0:
                        pe.wait_ge(cn_meta, g + 1)
                    else:
                        pe.wait_ge(s_free, n * 3)
                else:
                    pe.wait_ge(a_free if c % 2 else s_free, n * 3 + 2 + (c - 1) // 2)
                mm(out, dp[:, c * P:(c + 1) * P], v1[:, c, :], start=True, stop=False)
                last = mm(out, eh[:, c * P:(c + 1) * P], cn[:, :], start=False, stop=True)
                if c == CH - 1:
                    last.then_inc(n_full, 1)
                kv, full, free = ((S, s_full, s_free), (A, a_full, a_free))[1 - c % 2]
                pe.wait_ge(free, n * 3 + 1 + c // 2)
                mm(kv[:, 0:DV1], kw[:, c * P:(c + 1) * P], v1[:, c, :], start=True, stop=True).then_inc(full, 1)

            def at_half(g, b, t, first):
                n = nth(g, b)
                if t == V and not (first and b == 0):
                    pe.wait_ge(n_free, n)
                    transposed(eh, t0(g, b, "hT", first))
                if t == K and first and b == 0:
                    columns(1, MIX, DB, t1(g, b, "mix cols", first))
                if t == Q:
                    if first:
                        pe.wait_ge(const2, 1)
                        columns(b + 2, BT, CH, t1(g, b, "cols", first))
                    bank_, left = evacuations(g, b, K)
                    pe.wait_ge(p_free[bank_], left + 1)
                    transposed(kf, t0(g, b, "kT", first))
                if t == GC:
                    bank_, left = evacuations(g, b, V)
                    pe.wait_ge(p_free[bank_], left + 1)
                    transposed(vf, t0(g, b, "vT", first))
                if t == ZC:
                    chunk(g, b, 0, first)
                if t == O:
                    chunk(g, b, 2, first)
                if first:
                    for r in X_HALF.get(t, ()):
                        x_round(1 + CH * (b + 1) + r // 2, r % 2, t0(g, b, ("x", r), first))

            def at_end(g, b, t, first):
                n = nth(g, b)
                if first:
                    for r in X_END.get(t, ()):
                        x_round(1 + CH * (b + 1) + r // 2, r % 2, t0(g, b, ("x", r), first))
                if t == Q:
                    pe.wait_ge(rb_ready, n + 1)
                    pe.wait_ge(a_free, n * 3)
                    for c in range(CH):
                        o = A[:, c * P:(c + 1) * P]
                        mm(o, rows[0:GR, tok0(b) + c * P:tok0(b) + (c + 1) * P], rb[0:GR, c * P:(c + 1) * P], start=True, stop=False)
                        last = mm(o, identb[:, :], maskb[:, :], start=False, stop=True)
                    last.then_inc(a_full, 1)
                    pe.wait_ge(n_free, n)
                    mm(N[0][:, :], ones[64:64 + H, :], rb[64:64 + H, :], start=True, stop=True).then_inc(e_full, 1)
                if t == GC:
                    bank_, left = evacuations(g, b, Q)
                    pe.wait_ge(p_free[bank_], left + 1)
                    pe.wait_ge(s_free, n * 3)
                    for c in range(CH):
                        cc = slice(c * P, (c + 1) * P)
                        last = mm(S[:, cc], kf[:, cc], qf[:, cc], start=True, stop=True)
                    last.then_inc(s_full, 1)
                if t == ZC:
                    chunk(g, b, 1, first)
                if t == O:
                    chunk(g, b, 3, first)
                if b == 0:
                    mixed_end(g, b, t, first)
                if b == 1 and t in (V, Q, GC):
                    i0, i1 = SAMPLE_ROUNDS[t - V]
                    pe.wait_ge(mx_v_wide, g + 1)
                    use_t1(t1(g, b, ("state", t - V), first))
                    mm(T1[:, 0:(i1 - i0) * DV1], kwm[:, :], v1x[:, i0:i1, :].rearrange("p b v -> p (b v)"),
                       start=True, stop=True).then_inc(t1_full, 1)
                if first and t == ZC:
                    gates(2 + 2 * CH * (b + 2), tok0(b + 1), BT, t1(g, b, "gates", first))
                if first and b == NB - 2 and t == ZM:
                    columns(b + 3, BT, CH, t1(g, b, "next cols", first))

            def mixed_end(g, b, t, first):
                if t == Q:
                    use_t1(t1(g, b, "args", first))
                    mm(T1[0:MIX, 0:MIX], rows[0:GR, 0:MIX], rbm[0:GR, :], start=True, stop=False)
                    mm(T1[0:MIX, 0:MIX], identb[0:MIX, 0:MIX], mixmask[:, :], start=False, stop=True)
                    mm(T1[:, P:P + MIX], ones[64:64 + H, :], rbm[64:64 + H, :], start=True, stop=True).then_inc(t1_full, 1)
                if t == GC:
                    pe.wait_ge(t0_free, t0(g, b, ("mix", V), first) + 1)
                    use_t1(t1(g, b, "kv", first))
                    nc.tensor.transpose(T1[0:MIX, 0:P], kfm[:, :], ident[:, :])
                    nc.tensor.transpose(T1[0:MIX, P:2 * P], vfm[:, :], ident[:, :]).then_inc(t1_full, 1)
                if t == HC:
                    pe.wait_ge(t0_free, t0(g, b, ("mix", Q), first) + 1)
                    use_t1(t1(g, b, "score", first))
                    mm(T1[0:MIX, 0:MIX], kfm[:, :], qfm[:, :], start=True, stop=True).then_inc(t1_full, 1)
                if t == GB:
                    use_t1(t1(g, b, "num", first))
                    pe.wait_ge(mx_q, g + 1)
                    pe.wait_ge(cs_in, (g + 1) * 16)
                    pe.wait_ge(mx_n, g + 1)
                    o = T1[0:MIX, 0:DV1]
                    mm(o, dpm[:, :], v1m[:, :], start=True, stop=False)
                    for i in range(DB):
                        mm(o, qm[:, i * MIX:(i + 1) * MIX], cs[:, i, :], start=False, stop=(i == DB - 1))
                    mm(T1[:, 2 * P:2 * P + DV1], kwm[0:META, :], v1m[0:META, :], start=True, stop=True).then_inc(t1_full, 1)
                if t == O:
                    use_t1(t1(g, b, "hT", first))
                    nc.tensor.transpose(T1[:, 0:MIX], hnm[:, :], ident[0:MIX, 0:MIX]).then_inc(t1_full, 1)

            def pe_block(g, b, first):
                for t in range(NT):
                    if b == 0:
                        pe.wait_ge(w_low, g * NT + (t + 1))
                    if b == 0:
                        use_t0(t0(g, b, ("mix", t), first))
                        split_product(T0[:, 0:MIX], Wh[:, t, :, :], Wl[:, t, :, :], 0, KT, 0, MIX).then_inc(t0_full, 1)
                    bank_, left = evacuations(g, b, t)
                    pe.wait_ge(p_free[bank_], left)
                    out = PB[bank_][:, :]
                    split_product(out, Wh[:, t, :, :], Wl[:, t, :, :], 0, KT // 2, tok0(b), BT)
                    at_half(g, b, t, first)
                    split_product(out, Wh[:, t, :, :], Wl[:, t, :, :], KT // 2, KT, tok0(b), BT).then_inc(tile_done, 1)
                    at_end(g, b, t, first)

            pe.wait_ge(const, 1)
            for unit in range(1 + CH):
                x_round(unit, 0, 2 * unit)
                x_round(unit, 1, 2 * unit + 1)
                if unit == 1:
                    pe.wait_ge(g_low, 1)
                    gates(2, 0, MIX, 0)
            gates(2 + 2 * CH, MIX, BT, 1)
            for b in range(NB - 1):
                pe_block(0, b, True)
            with pe.Fori(1, H) as g:
                pe_block(g - 1, NB - 1, False)
                for b in range(NB - 1):
                    pe_block(g, b, False)
            pe_block(H - 1, NB - 1, False)
            pe.wait_ge(n_free, NB * H)
            transposed(eh, t0(H, 0, "hT", False) - t0_uses(0, False).index("hT"))

            def b_tile(tile, n, slot, i, at):
                for h in range(2):
                    if not isinstance(tile, int):
                        pe.wait_ge(b_free, tile * 2 + (h - 2))
                    o = OUT[i][h][0:n, :]
                    for k in range(KT):
                        yh, yl = ybuf[slot][:, k, 0, at:at + n], ybuf[slot][:, k, 1, at:at + n]
                        wh, wl = Woh[:, k, h * BT:(h + 1) * BT], Wol[:, k, h * BT:(h + 1) * BT]
                        mm(o, yh, wh, start=(k == 0), stop=False)
                        mm(o, yh, wl, start=False, stop=False)
                        last = mm(o, yl, wh, start=False, stop=(k == KT - 1))
                    last.then_inc(b_full, 1)

            pe.wait_ge(wo_low, KT)
            pe.wait_ge(y_in[0], 16 * KT)
            pe.wait_ge(p_free[0], H * NT * NB // 2)
            pe.wait_ge(p_free[1], H * NT * NB // 2)
            pe.wait_ge(a_free, 3 * NB * H)
            pe.wait_ge(s_free, 3 * NB * H)
            b_tile(0, DB * DS, 0, 0, 0)
            with pe.Fori(0, NB) as j:
                for c in range(CH):
                    if c == 0:
                        pe.wait_ge(y_in[1], (j + 1) * 16 * KT)
                    if c == 2:
                        pe.wait_ge(y_in[0], (j + 2) * 16 * KT)
                    b_tile(j * CH + (1 + c), P, 1 - c // 2, (1 + c) % 2, (c % 2) * P)

        @block.scalar
        def _(act):
            order = Order(act, act_step, ACT_TURN)
            did, mark, fn = order.did, order.mark, order.after(nc.scalar.activation)

            def x_square(unit):
                n, s = (MIX if unit == 0 else P), unit % XBUF
                loads = unit // XBUF + (2 if s == 0 else 1)
                act.wait_ge(x_in[s], 16 * loads)
                mark(fn(junk[0:n, :], xs[s][0:n, :], ACT.Square, accum_out=ssx[0:n, unit:unit + 1]).then_inc(x_sq, 1), x_sq, unit + 1)

            def x_high_part(unit, r, count):
                n, tok = (MIX, 0) if unit == 0 else (P, MIX + (unit - 1) * P)
                i = 2 * unit + r
                act.wait_ge(t0_free, count + 1)
                mark(fn(xTh[:, 4 * r:4 * r + 4, tok:tok + n], xtmp[i % 2][:, 0:4 * n].rearrange("p (k t) -> p k t", k=4),
                   ACT.Copy).then_inc(x_high, 1), x_high, i + 1)

            def gate_logits(unit, n, count):
                act.wait_ge(t1_full, count + 1)
                if unit:
                    act.wait_ge(rows_ready, unit)
                mark(fn(grow[:, 0:n], T1[0:GR, 0:n], ACT.Identity, bias=biasg[:, :], scale=1.0 / WS).then_inc(t1_free, 1), t1_free, count + 1)

            def gate_logs(unit, n):
                act.wait_ge(g_abs, unit + 1)
                mark(fn(gt[:, 0:n], gt[:, 0:n], ACT.Exp).then_inc(g_exp, 1), g_exp, unit + 1)
                mark(fn(gt[:, 0:n], gt[:, 0:n], ACT.Ln, bias=1.0).then_inc(g_ln, 1), g_ln, unit + 1)

            def columns_part(first_chunk, chunks_, n, count):
                act.wait_ge(t1_full, count + 1)
                src = T1[0:n, 0:64 * chunks_].rearrange("p (c k r) -> p c k r", k=2, r=32)[:, :, :, 0:H]
                for kind in range(2):
                    did(fn(cols[0:n, first_chunk:first_chunk + chunks_, kind, :], src[:, :, kind, :], ACT.Exp))
                if first_chunk == 0:
                    out = decs[:, :, :]
                else:
                    out = cols[:, first_chunk:first_chunk + chunks_, 2, :]
                k = DB if first_chunk == 0 else CH
                mark(fn(out, T1[:, 256:256 + k * H].rearrange("p (c h) -> p c h", h=H), ACT.Exp).then_inc(t1_free, 1), t1_free, count + 1)

            def split_w(g, t):
                act.wait_ge(w_in_s[t % STAGES], g * (16 * NT // STAGES) + 16 * (t // STAGES + 1))
                mark(fn(Wh[:, t, :, :], wst[t % STAGES][:, :, :], ACT.Copy, scale=WS).then_inc(w_high, 1), w_high, g * NT + (t + 1))

            def copy(out, src, scale):
                return fn(out, src, ACT.Copy, scale=scale)

            def mixed_start(g, b, t, first):
                count = t0(g, b, ("mix", t), first)
                src = T0[:, 0:MIX]
                if t in (HC, GB):
                    return
                act.wait_ge(t0_full, count + 1)
                if t == K:
                    mark(copy(kfm[:, :], src, SK / WS).then_inc(t0_free, 1), t0_free, count + 1)
                if t == V:
                    mark(copy(vfm[:, :], src, 1 / WS).then_inc(t0_free, 1), t0_free, count + 1)
                if t == Q:
                    act.wait_ge(mx_q, g)
                    mark(copy(qfm[:, :], src, 1 / WS).then_inc(t0_free, 1), t0_free, count + 1)
                if t == GC:
                    act.wait_ge(mx_gc_used, g)
                    mark(copy(gcm[:, :], src, 1 / WS).then_inc(t0_free, 1), t0_free, count + 1)
                if t == ZC:
                    act.wait_ge(mx_g, g)
                    mark(fn(tzm[:, :], src, ACT.Tanh, scale=0.5 / WS).then_inc(mx_tanh_zc, 1), mx_tanh_zc, g + 1)
                if t == O:
                    mark(fn(tom[:, :], src, ACT.Tanh, scale=0.5 / WS).then_inc(t0_free, 1), t0_free, count + 1)
                if t == ZM:
                    mark(fn(tzm[:, :], src, ACT.Tanh, scale=0.5 / WS).then_inc(mx_tanh_zm, 1), mx_tanh_zm, g + 1)

            def heads_high(g, b, count):
                n = nth(g, b)
                act.wait_ge(t0_free, count + 1)
                act.wait_ge(y_out_m, (n - 1) * 16)
                mark(fn(yst[:, 1, 0, :], dp[:, :], ACT.Copy).then_inc(ym_high, 1), ym_high, n)

            def at_half(g, b, t, first):
                if first and b == 0 and t < NT - STAGES:
                    split_w(0, t + STAGES)
                if t == V and not (first and b == 0):
                    heads_high(g, b, t0(g, b, "hT", first))
                if t == GC:
                    act.wait_ge(t0_full, t0(g, b, "vT", first) + 1)
                    mark(fn(v1[:, :, 0:P], chunks(T0[:, :]), ACT.Copy).then_inc(t0_free, 1), t0_free, t0(g, b, "vT", first) + 1)
                if first:
                    for r in X_HALF.get(t, ()):
                        x_high_part(1 + CH * (b + 1) + r // 2, r % 2, t0(g, b, ("x", r), first))
                    if b == 0 and t == K:
                        columns_part(0, 1, MIX, t1(g, b, "mix cols", first))
                    if t == Q:
                        columns_part(1 + CH * b, CH, P, t1(g, b, "cols", first))
                    if t in X_SQUARE:
                        x_square(1 + CH * (b + 1) + X_SQUARE[t])

            def evacuate(g, b, t):
                n = nth(g, b)
                i, left = evacuations(g, b, t)
                src, free = PB[i][:, :], p_free[i]
                if t in (HC, GB):
                    return
                act.wait_ge(tile_done, n * NT + (t + 1))
                if t == K:
                    mark(copy(kf[:, :], src, SK / WS).then_inc(free, 1), free, left + 1)
                if t == V:
                    mark(copy(vf[:, :], src, 1 / WS).then_inc(free, 1), free, left + 1)
                if t == Q:
                    act.wait_ge(q_scaled, n)
                    mark(copy(qf[:, :], src, 1 / WS).then_inc(free, 1), free, left + 1)
                if t == GC:
                    act.wait_ge(gc_used, n)
                    mark(copy(gcs[:, :], src, 1 / WS).then_inc(free, 1), free, left + 1)
                if t == ZC:
                    act.wait_ge(g_done, n)
                    mark(fn(tz[:, :], src, ACT.Tanh, scale=0.5 / WS).then_inc(tanh_zc, 1), tanh_zc, n + 1)
                if t == O:
                    mark(fn(to[:, :], src, ACT.Tanh, scale=0.5 / WS).then_inc(free, 1), free, left + 1)
                if t == ZM:
                    act.wait_ge(yc_ready, n + 1)
                    mark(fn(tz[:, :], src, ACT.Tanh, scale=0.5 / WS).then_inc(tanh_zm, 1), tanh_zm, n + 1)

            def at_end(g, b, t, first):
                n = nth(g, b)
                if t == Q:
                    act.wait_ge(a_full, n * 3 + 1)
                    act.wait_ge(ym_low, n)
                    mark(fn(dp[:, :], A[:, :], ACT.Exp).then_inc(a_free, 1), a_free, n * 3 + 1)
                    act.wait_ge(e_full, n + 1)
                    mark(fn(eh[:, :], N[0][:, :], ACT.Exp).then_inc(e_ready, 1), e_ready, n + 1)
                    if b == 0:
                        act.wait_ge(t1_full, t1(g, b, "args", first) + 1)
                        did(fn(dpm[:, :], T1[0:MIX, 0:MIX], ACT.Exp))
                        mark(fn(ehm[:, :], T1[:, P:P + MIX], ACT.Exp).then_inc(t1_free, 1), t1_free, t1(g, b, "args", first) + 1)
                if t == GB and b == 0:
                    act.wait_ge(mx_rec, g + 1)
                    mark(fn(junk[0:MIX, 0:P], T1[0:MIX, 0:P], ACT.Square, scale=hm[:, 1:2], accum_out=hm[:, 2:3]).then_inc(mx_sq, 1), mx_sq, g + 1)
                if t == ZC:
                    act.wait_ge(yc_ready, n + 1)
                    act.wait_ge(y_out_c, n * 16)
                    mark(fn(yst[:, 0, 0, :], yc[:, :], ACT.Copy).then_inc(yc_high, 1), yc_high, n + 1)
                    if b == 0:
                        act.wait_ge(mx_yc, g + 1)
                        act.wait_ge(mx_out_c, g * 16)
                        mark(fn(ystm[:, 0, 0, :], ycm[:, :], ACT.Copy).then_inc(mx_yc_high, 1), mx_yc_high, g + 1)
                if t == O:
                    act.wait_ge(rec_ready, n + 1)
                    for c in range(CH):
                        last = fn(junk[:, 0:P], N[c // 2][:, (c % 2) * DV1:(c % 2) * DV1 + P], ACT.Square,
                                  scale=rec[:, c:c + 1], accum_out=hss[:, c:c + 1])
                        if c < CH - 1:
                            did(last)
                    mark(last.then_inc(h_sq, 1), h_sq, n + 1)
                if t == ZM and b == 0:
                    act.wait_ge(t1_free, t1(g, b, "hT", first) + 1)
                    act.wait_ge(mx_out_m, g * 16)
                    mark(fn(ystm[:, 1, 0, :], ymm[:, :], ACT.Copy).then_inc(mx_ym_high, 1), mx_ym_high, g + 1)
                if first:
                    if t == ZC:
                        gate_logits(b + 2, BT, t1(g, b, "gates", first))
                        gate_logs(b + 2, BT)
                    if t == ZM and b == NB - 2:
                        columns_part(1 + CH * (b + 1), CH, P, t1(g, b, "next cols", first))

            def x_end(b, t, first):
                for r in X_END.get(t, ()) if first else ():
                    x_high_part(1 + CH * (b + 1) + r // 2, r % 2, t0(0, b, ("x", r), first))

            def act_block(g, b, first, following):
                if following == "weights":
                    act.wait_ge(w_low, (g + 1) * NT - 1)
                    load_w(act, g + 1, 0)
                    load_w(act, g + 1, 1)
                    act.wait_ge(cs_out, (g + 1) * 16)
                    load_states(act, g + 1)
                for t in range(NT):
                    if b == 0:
                        mixed_start(g, b, t, first)
                    at_half(g, b, t, first)
                    if t in (HC, GB):
                        x_end(b, t, first)
                    evacuate(g, b, t)
                    if t not in (HC, GB):
                        x_end(b, t, first)
                    at_end(g, b, t, first)
                    if following == "weights":
                        act.wait_ge(tile_done, nth(g, b) * NT + (t + 1))
                        split_w(g + 1, t)
                        if t < NT - 2:
                            act.wait_ge(w_low, (g + 1) * NT + t)
                            load_w(act, g + 1, t + 2)
                    if following == "output weights" and t < KT:
                        act.wait_ge(w_in_s[t % STAGES], 16 * (NT * H // STAGES + t // STAGES + 1))
                        mark(fn(Woh[:, :, t * P:(t + 1) * P], wst[t % STAGES][:, :, :], ACT.Copy, scale=WS).then_inc(wo_high, 1), wo_high, t + 1)

            act.dma_start(gain[:, :], norm_gain.rearrange("(k p) -> p k", p=P)).then_inc(gain_in, 16)
            act.dma_start(wgst[:, :, :], w_in[:, IG_COL:IG_COL + 2 * H].rearrange("(k p) c -> p k c", p=P)).then_inc(gate_in, 16)
            x_square(0)
            x_square(1)
            act.wait_ge(bias_clear, 1)
            act.dma_start(biasg[0:H, :], b_fgate.rearrange("(h o) -> h o", o=1)).then_inc(par_in, 16)
            act.dma_start(biasg[32:GR, :], b_igate.rearrange("(h o) -> h o", o=1)).then_inc(par_in, 16)
            act.dma_start(sm0[:, :], state_m.rearrange("b h -> h b")).then_inc(par_in, 16)
            act.dma_start(mhg[:, :], mh_gain.rearrange("(h p) -> p h", p=P)).then_inc(par_in, 16)
            act.wait_ge(const, 1)
            act.wait_ge(gate_in, 16)
            did(fn(Wgh[:, :, 0:H], wgst[:, :, H:2 * H], ACT.Copy, scale=WS))
            mark(fn(Wgh[:, :, 32:GR], wgst[:, :, 0:H], ACT.Copy, scale=WS).then_inc(g_high, 1), g_high, 1)
            x_high_part(0, 0, 0)
            x_high_part(0, 1, 1)
            x_square(2)
            x_high_part(1, 0, 2)
            x_high_part(1, 1, 3)
            act.wait_ge(par_in, 16 * 4)
            gate_logits(0, MIX, 0)
            x_square(3)
            x_high_part(2, 0, 4)
            x_high_part(2, 1, 5)
            gate_logs(0, MIX)
            x_square(4)
            split_w(0, 0)
            x_high_part(3, 0, 6)
            x_high_part(3, 1, 7)
            x_high_part(4, 0, 8)
            x_high_part(4, 1, 9)
            split_w(0, 1)
            split_w(0, 2)
            gate_logits(1, BT, 1)
            gate_logs(1, BT)
            for b in range(NB - 1):
                act_block(0, b, True, None)
            with act.Fori(1, H) as g:
                order.enter(g)
                act_block(g - 1, NB - 1, False, "weights")
                for b in range(NB - 1):
                    act_block(g, b, False, None)
            order.leave(H - 1)
            act_block(H - 1, NB - 1, False, "output weights")
            heads_high(H, 0, t0(H, 0, "hT", False) - t0_uses(0, False).index("hT"))

            def b_tile(tile, n, i, c):
                act.wait_ge(b_free, tile * 2 + 2)
                mark(fn(junk[0:n, :], xs[i][0:n, :], ACT.Square, accum_out=ssx[0:n, c:c + 1]).then_inc(b_sq, 1), b_sq, tile + 1)

            b_tile(0, DB * DS, 0, 0)
            with act.Fori(0, NB) as j:
                for c in range(CH):
                    b_tile(j * CH + (1 + c), P, (1 + c) % 2, 1 + c)

        @block.vector
        def _(dve):
            order = Order(dve, dve_step, DVE_TURN)
            did, mark = order.did, order.mark
            tt, ts, stt, scan, copy, reciprocal, memset = (order.after(op) for op in (
                nc.vector.tensor_tensor, nc.vector.tensor_scalar, nc.vector.scalar_tensor_tensor,
                nc.vector.tensor_tensor_scan, nc.vector.tensor_copy, nc.vector.reciprocal, nc.vector.memset))

            def pick(out, src):
                return ts(out, src, 1.0, None, ALU.mult)

            def x_prepare(unit):
                n, s = (MIX if unit == 0 else P), unit % XBUF
                dve.wait_ge(x_rs, unit + 1)
                mark(ts(xs[s][0:n, :], xs[s][0:n, :], rsx[0:n, unit:unit + 1], None, ALU.mult).then_inc(x_scaled, 1), x_scaled, unit + 1)

            def x_low_part(i):
                unit, r = divmod(i, 2)
                n, tok = (MIX, 0) if unit == 0 else (P, MIX + (unit - 1) * P)
                dve.wait_ge(x_high, i + 1)
                mark(tt(xTl[:, 4 * r:4 * r + 4, tok:tok + n], xtmp[i % 2][:, 0:4 * n].rearrange("p (k t) -> p k t", k=4),
                   xTh[:, 4 * r:4 * r + 4, tok:tok + n], ALU.subtract).then_inc(x_low, 1), x_low, i + 1)

            def x_gain(unit, r, count0):
                n, i = (MIX if unit == 0 else P), 2 * unit + r
                dve.wait_ge(t0_full, count0 + 1)
                mark(tt(xtmp[i % 2][:, 0:4 * n].rearrange("p (k t) -> p k t", k=4), T0[:, 0:4 * n].rearrange("p (k t) -> p k t", k=4),
                   wide(gain[:, 4 * r:4 * r + 4], n), ALU.mult).then_inc(t0_free, 1), t0_free, count0 + 1)

            def gate_abs(unit, n):
                dve.wait_ge(t1_free, GATE_COUNTS[unit] + 1)
                f, t = grow[0:H, 0:n], gt[:, 0:n]
                mark(stt(t, f, -1.0, f, ALU.mult, ALU.min).then_inc(g_abs, 1), g_abs, unit + 1)

            def gate_rows(unit, tok, n):
                f, t = grow[0:H, 0:n], gt[:, 0:n]
                a = rows[0:H, tok:tok + n]
                ends = (chunks(mrow[:, :])[:, :, P - 1], samples(mrow)[:, :, DS - 1])[unit == 0]
                dve.wait_ge(g_ln, unit + 1)
                did(stt(lf[:, 0:n], f, 0.0, t, ALU.min, ALU.subtract))
                if unit:
                    did(scan(bcum[:, :], restart[:, :], lf[:, :], 0.0, ALU.mult, ALU.add))
                else:
                    did(scan(bcum[:, 0:MIX], remix[:, :], lf[:, 0:MIX], 0.0, ALU.mult, ALU.add))
                did(copy(t, grow[32:GR, 0:n]))
                did(tt(a, t, bcum[:, 0:n], ALU.subtract))
                for c in range(CH if unit else 1):
                    before, length = CH * (unit - 1) + c + 1 if unit else 0, P if unit else META
                    sl = slice(c * P, c * P + length)
                    did(scan(mrow[:, sl], a[:, sl], a[:, sl], mst[:, before:before + 1], ALU.max, ALU.max))
                    end = c * P + length - 1
                    did(tt(mst[:, before + 1:before + 2], bcum[:, end:end + 1], mrow[:, end:end + 1], ALU.add))
                if unit == 0:
                    did(copy(t, a))
                    did(tt(samples(t)[:, :, 0], samples(t)[:, :, 0], sm0[:, :], ALU.max))
                    did(scan(mrow[:, META:MIX], forget[:, :], t[:, META:MIX], 0.0, ALU.add, ALU.max))
                else:
                    dve.wait_ge(t1_free, COLS_COUNTS[unit - 1] + 1)
                if unit:
                    k, length, cut = CH, P, chunks
                    before = mst[:, 1 + CH * (unit - 1):1 + CH * unit]
                else:
                    k, length, cut, before = DB, DS, samples, sm0[:, :]
                    did(ts(rows[96:96 + H, 0:META], mrow[:, 0:META], -1.0, None, ALU.mult))
                    did(ts(trr[32:GR, 0:META], a[:, 0:META], mrow[:, META - 1:META], None, ALU.subtract))
                did(tt(cut(rows[96:96 + H, tok:tok + n]), wide(before, length), cut(mrow[:, 0:n]), ALU.subtract))
                did(tt(cut(trr[32:GR, 0:n]), cut(a), wide(ends, length), ALU.subtract))
                did(copy(rows[64:64 + H, tok:tok + n], mrow[:, 0:n]))
                did(stt(trr[0:H, 0:n], bcum[:, 0:n], -1.0, mrow[:, 0:n], ALU.mult, ALU.subtract))
                did(tt(rl[:, 0:k], before, ends, ALU.subtract))
                if unit == 0:
                    did(tt(smn[:, :], samples(bcum)[:, :, DS - 1], ends, ALU.add))
                mark(tt(drl[:, 0:k * H].rearrange("p (c h) -> p c h", h=H), wide(rl[:, 0:k], H),
                   selh[0:H, :].unsqueeze(1).broadcast_to([H, k, H]), ALU.mult).then_inc(rows_ready, 1), rows_ready, unit + 1)

            def split_w(g, t):
                dve.wait_ge(w_high, g * NT + (t + 1))
                mark(stt(Wl[:, t, :, :], wst[t % STAGES][:, :, :], WS, Wh[:, t, :, :], ALU.mult, ALU.subtract).then_inc(w_low, 1), w_low, g * NT + (t + 1))

            def conv(out, w, g, tap):
                did(ts(out, tap(0), cwt[:, bass.ds(g, 1), 0], None, ALU.mult))
                for j in (1, 2):
                    did(stt(out, tap(j), cwt[:, bass.ds(g, 1), j], out, ALU.mult, ALU.add))

            def mixed_start(g, b, t, first):
                at = t0(g, b, ("mix", t), first)
                src = T0[:, 0:MIX]
                if t == GC:
                    if first:
                        dve.wait_ge(par2_in, 16 * 8)
                    tt_ = pick(cs[:, :, P], nst[:, :, bass.ds(g, 1)].rearrange("p b o -> p (b o)"))
                    mark(tt_.then_inc(mx_n, 1), mx_n, g + 1)
                if t == HC:
                    dve.wait_ge(t0_full, at + 1)
                    dve.wait_ge(t0_free, t0(g, b, ("mix", GC), first) + 1)
                    states = cst[:, bass.ds(g, 1), :].rearrange("p o (b j) -> p (o b) j", j=2)
                    did(pick(useg[:, :, 0:2], states))
                    did(stt(um[:, 2:2 + META], src[:, 0:META], 1 / WS, gcm[:, 0:META], ALU.mult, ALU.mult))
                    mark(stt(useg[:, :, 2:], samples(src), 1 / WS, samples(gcm), ALU.mult, ALU.mult).then_inc(t0_free, 1), t0_free, at + 1)
                    dve.wait_ge(t0_free, at + 1)
                    mark(pick(states, useg[:, :, DS:DS + 2]).then_inc(mx_gc_used, 1), mx_gc_used, g + 1)
                    conv(ycm[:, 0:META], None, g, lambda j: um[:, j:j + META])
                    conv(samples(ycm), None, g, lambda j: useg[:, :, j:j + DS])
                    did(copy(u[:, 0:2], um[:, META:META + 2]))
                if t == GB:
                    dve.wait_ge(t0_full, at + 1)
                    mark(stt(ycm[:, :], src, 1 / WS, ycm[:, :], ALU.mult, ALU.mult).then_inc(t0_free, 1), t0_free, at + 1)
                if t == ZC:
                    dve.wait_ge(mx_tanh_zc, g + 1)
                    mark(stt(zsm[:, :], tzm[:, :], 1.0, src, ALU.add, ALU.mult).then_inc(t0_free, 1), t0_free, at + 1)
                    dve.wait_ge(t0_free, at + 1)
                    mark(stt(ycm[:, :], ycm[:, :], 0.5 / WS, zsm[:, :], ALU.mult, ALU.mult).then_inc(mx_yc, 1), mx_yc, g + 1)
                if t == ZM:
                    dve.wait_ge(t0_free, t0(g, b, ("mix", O), first) + 1)
                    did(ts(tom[:, :], tom[:, :], 1.0, mhg[:, bass.ds(g, 1)], ALU.add, ALU.mult))
                    dve.wait_ge(mx_tanh_zm, g + 1)
                    mark(stt(zsm[:, :], tzm[:, :], 1.0, src, ALU.add, ALU.mult).then_inc(t0_free, 1), t0_free, at + 1)
                    dve.wait_ge(t0_free, at + 1)
                    mark(stt(Gm[:, :], tom[:, :], 0.25 / WS, zsm[:, :], ALU.mult, ALU.mult).then_inc(mx_g, 1), mx_g, g + 1)
                    dve.wait_ge(mx_g, g + 1)
                    dve.wait_ge(t1_full, t1(g, b, "hT", first) + 1)
                    mark(tt(ymm[:, :], T1[:, 0:MIX], Gm[:, :], ALU.mult).then_inc(t1_free, 1), t1_free, t1(g, b, "hT", first) + 1)

            def heads_out(g, b, at):
                n = nth(g, b)
                dve.wait_ge(t0_full, at + 1)
                dve.wait_ge(g_done, n)
                mark(tt(dp[:, :], T0[:, :], G[:, :], ALU.mult).then_inc(t0_free, 1), t0_free, at + 1)
                dve.wait_ge(ym_high, n)
                mark(tt(yst[:, 1, 1, :], dp[:, :], yst[:, 1, 0, :], ALU.subtract).then_inc(ym_low, 1), ym_low, n)

            def update(g, b, c):
                n = nth(g, b)
                kv, full, free = ((A, a_full, a_free), (S, s_full, s_free))[c % 2]
                dve.wait_ge(full, n * 3 + (2 + c // 2))
                mark(stt(cn[:, :], cn[:, :], sel[:, c, 2:3], kv[:, 0:DV1], ALU.mult, ALU.add).then_inc(free, 1), free, n * 3 + (2 + c // 2))

            def at_half(g, b, t, first):
                n = nth(g, b)
                if first and b == 0 and t < NT - STAGES:
                    split_w(0, t + STAGES)
                if t == V and not (first and b == 0):
                    heads_out(g, b, t0(g, b, "hT", first))
                if t == Q:
                    if first:
                        select(g, b, first)
                    dve.wait_ge(t0_full, t0(g, b, "kT", first) + 1)
                    mark(tt(chunks(kw[:, :]), chunks(T0[:, :]), wide(sel[:, :, 1], P), ALU.mult).then_inc(t0_free, 1), t0_free, t0(g, b, "kT", first) + 1)
                if t == ZC:
                    if b == 0:
                        dve.wait_ge(cn_meta, g + 1)
                    else:
                        dve.wait_ge(s_free, n * 3)
                    update(g, b, 0)
                if t == O:
                    dve.wait_ge(s_free, n * 3 + 2)
                    update(g, b, 2)
                    if first:
                        gate_rows(b + 2, tok0(b + 1), BT)
                if first:
                    for r in X_HALF.get(t, ()):
                        x_gain(1 + CH * (b + 1) + r // 2, r % 2, t0(g, b, ("x", r), first))
                        x_low_part(2 * (1 + CH * (b + 1)) + r)

            def evacuate(g, b, t):
                n = nth(g, b)
                i, left = evacuations(g, b, t)
                src, free = PB[i][:, :], p_free[i]
                if t == HC:
                    if b:
                        did(copy(u[:, 0:2], u[:, BT:BT + 2]))
                    dve.wait_ge(tile_done, n * NT + (t + 1))
                    j, before = evacuations(g, b, GC)
                    dve.wait_ge(p_free[j], before + 1)
                    mark(stt(u[:, 2:], src, 1 / WS, gcs[:, :], ALU.mult, ALU.mult).then_inc(free, 1), free, left + 1)
                    dve.wait_ge(free, left + 1)
                    mark(ts(yc[:, :], u[:, 0:BT], cwt[:, bass.ds(g, 1), 0], None, ALU.mult).then_inc(gc_used, 1), gc_used, n + 1)
                    dve.wait_ge(gc_used, n + 1)
                    did(stt(yc[:, :], u[:, 1:1 + BT], cwt[:, bass.ds(g, 1), 1], yc[:, :], ALU.mult, ALU.add))
                    did(stt(yc[:, :], u[:, 2:2 + BT], cwt[:, bass.ds(g, 1), 2], yc[:, :], ALU.mult, ALU.add))
                    if b == NB - 1:
                        did(pick(cpo[:, bass.ds(g, 1), :].rearrange("p o j -> p (o j)"), u[:, BT:BT + 2]))
                if t == GB:
                    dve.wait_ge(tile_done, n * NT + (t + 1))
                    mark(stt(yc[:, :], src, 1 / WS, yc[:, :], ALU.mult, ALU.mult).then_inc(free, 1), free, left + 1)
                if t == ZC:
                    j, before = evacuations(g, b, GB)
                    dve.wait_ge(p_free[j], before + 1)
                    dve.wait_ge(tanh_zc, n + 1)
                    mark(stt(zs[:, :], tz[:, :], 1.0, src, ALU.add, ALU.mult).then_inc(free, 1), free, left + 1)
                    dve.wait_ge(free, left + 1)
                    mark(stt(yc[:, :], yc[:, :], 0.5 / WS, zs[:, :], ALU.mult, ALU.mult).then_inc(yc_ready, 1), yc_ready, n + 1)
                if t == ZM:
                    j, before = evacuations(g, b, O)
                    dve.wait_ge(p_free[j], before + 1)
                    did(ts(to[:, :], to[:, :], 1.0, mhg[:, bass.ds(g, 1)], ALU.add, ALU.mult))
                    dve.wait_ge(tanh_zm, n + 1)
                    mark(stt(zs[:, :], tz[:, :], 1.0, src, ALU.add, ALU.mult).then_inc(free, 1), free, left + 1)
                    dve.wait_ge(free, left + 1)
                    mark(stt(G[:, :], to[:, :], 0.25 / WS, zs[:, :], ALU.mult, ALU.mult).then_inc(g_done, 1), g_done, n + 1)

            def select(g, b, first):
                n = nth(g, b)
                if first and b == 0:
                    dve.wait_ge(const2, 1)
                if first or b == NB - 1:
                    dve.wait_ge(t1_free, COLS_COUNTS[b + 1] + 1)
                dve.wait_ge(tile_done, n * NT + 1)
                dve.wait_ge(rows_ready, b + 2)
                did(pick(sel[:, :, :], cols[:, 1 + CH * b:1 + CH * (b + 1), :, bass.ds(g, 1)]
                                          .rearrange("p c k o -> p c (k o)")))
                if b == 0:
                    did(pick(selm[:, :], cols[0:MIX, 0, 0:2, bass.ds(g, 1)].rearrange("p k o -> p (k o)")))
                    did(pick(dselm[:, :], decs[:, :, bass.ds(g, 1)].rearrange("p k o -> p (k o)")))
                    right_factors(g, rbm, 0, MIX)
                mark(right_factors(g, rb, tok0(b), BT).then_inc(rb_ready, 1), rb_ready, n + 1)

            def right_factors(g, out, tok, n):
                one = bass.ds(g, 1)
                k = -(-n // P)
                ts(out[0:H, :].rearrange("p (c t) -> p c t", c=k), ones[0:H, 0:n // k].unsqueeze(1).broadcast_to([H, k, n // k]),
                   selh[0:H, one], None, ALU.mult)
                ts(out[32:GR, :], rows[64:64 + H, tok:tok + n], seln[64:64 + H, one], None, ALU.mult)
                return ts(out[64:64 + H, :], rows[96:96 + H, tok:tok + n], selh[96:96 + H, one], None, ALU.mult)

            def at_end(g, b, t, first):
                n = nth(g, b)
                if t == K and not first:
                    select(g, b, first)
                if t == Q:
                    dve.wait_ge(e_ready, n + 1)
                    mark(tt(eh[:, :], eh[:, :], qf[:, :], ALU.mult).then_inc(q_scaled, 1), q_scaled, n + 1)
                if t == GC:
                    dve.wait_ge(s_full, n * 3 + 1)
                    dve.wait_ge(a_free, n * 3 + 1)
                    mark(tt(dp[:, :], dp[:, :], S[:, :], ALU.mult).then_inc(s_free, 1), s_free, n * 3 + 1)
                if t == ZC:
                    dve.wait_ge(a_free, n * 3 + 2)
                    update(g, b, 1)
                    dve.wait_ge(yc_high, n + 1)
                    mark(tt(yst[:, 0, 1, :], yc[:, :], yst[:, 0, 0, :], ALU.subtract).then_inc(yc_low, 1), yc_low, n + 1)
                if t == O:
                    dve.wait_ge(a_free, n * 3 + 3)
                    update(g, b, 3)
                    if b == NB - 1:
                        dve.wait_ge(s_free, n * 3 + 3)
                        did(pick(npo[:, bass.ds(g, 1)], cn[:, P:DV1]))
                    dve.wait_ge(n_full, n + 1)
                    for i in range(2):
                        nv = N[i][:, 0:2 * DV1].rearrange("p (c v) -> p c v", c=2)
                        did(copy(den[:, 2 * i:2 * i + 2], nv[:, :, P]))
                    did(stt(den[:, :], den[:, :], -1.0, den[:, :], ALU.mult, ALU.max))
                    did(tt(den[:, :], den[:, :], sel[:, :, 0], ALU.max))
                    mark(reciprocal(rec[:, :], den[:, :]).then_inc(rec_ready, 1), rec_ready, n + 1)
                    dve.wait_ge(h_sq, n + 1)
                    mark(ts(hms[:, :], hss[:, :], 1.0 / P, EPS, ALU.mult, ALU.add).then_inc(h_ms, 1), h_ms, n + 1)
                    dve.wait_ge(h_rs, n + 1)
                    did(tt(hf[:, :], rec[:, :], hrs[:, :], ALU.mult))
                    for i in range(2):
                        nv = N[i][:, 0:2 * DV1].rearrange("p (c v) -> p c v", c=2)[:, :, 0:P]
                        last = tt(eh[:, 2 * P * i:2 * P * (i + 1)].rearrange("p (c v) -> p c v", c=2), nv,
                                  wide(hf[:, 2 * i:2 * i + 2], P), ALU.mult)
                    mark(last.then_inc(n_free, 1), n_free, n + 1)
                if b == 0:
                    mixed_end(g, b, t, first)
                if b == 1 and t in (V, Q, GC):
                    i0, i1 = SAMPLE_ROUNDS[t - V]
                    at = t1(g, b, ("state", t - V), first)
                    dve.wait_ge(t1_full, at + 1)
                    for i in range(i0, i1):
                        ins = stt(cs[:, i, :], cs[:, i, :], dselm[:, i:i + 1], T1[:, (i - i0) * DV1:(i - i0 + 1) * DV1], ALU.mult, ALU.add)
                        if i == i1 - 1:
                            mark(ins.then_inc(t1_free, 1), t1_free, at + 1)
                        else:
                            did(ins)
                    if t == GC:
                        dve.wait_ge(t1_free, at + 1)
                        mark(pick(nst[:, :, bass.ds(g, 1)].rearrange("p b o -> p (b o)"), cs[:, :, P]).then_inc(mx_states, 1), mx_states, g + 1)
                if first:
                    if t in X_SQUARE:
                        x_prepare(1 + CH * (b + 1) + X_SQUARE[t])
                    if t == ZC:
                        gate_abs(b + 2, BT)

            def mixed_end(g, b, t, first):
                if t == Q:
                    dve.wait_ge(t1_free, t1(g, b, "args", first) + 1)
                    mark(tt(qdiag, samples(ehm), samples(qfm), ALU.mult).then_inc(mx_q, 1), mx_q, g + 1)
                if t == GC:
                    at = t1(g, b, "kv", first)
                    dve.wait_ge(t1_full, at + 1)
                    did(ts(kwm[:, :], T1[0:MIX, 0:P], selm[:, 1:2], None, ALU.mult))
                    mark(copy(v1m[:, 0:P], T1[0:MIX, P:2 * P]).then_inc(t1_free, 1), t1_free, at + 1)
                    dve.wait_ge(t1_free, at + 1)
                    mark(tt(v1x[:, :, :], v1m[:, :].unsqueeze(1).broadcast_to([MIX, DB, DV1]), wide(segind[:, :], DV1), ALU.mult)\
                        .then_inc(mx_v_wide, 1), mx_v_wide, g + 1)
                if t == HC:
                    at = t1(g, b, "score", first)
                    dve.wait_ge(t1_full, at + 1)
                    mark(tt(dpm[:, :], dpm[:, :], T1[0:MIX, 0:MIX], ALU.mult).then_inc(t1_free, 1), t1_free, at + 1)
                if t == GB:
                    at = t1(g, b, "num", first)
                    dve.wait_ge(t1_full, at + 1)
                    dve.wait_ge(cn_out, g * 16)
                    mark(copy(cn[:, :], T1[:, 2 * P:2 * P + DV1]).then_inc(cn_meta, 1), cn_meta, g + 1)
                    did(copy(hm[:, 0:1], T1[0:MIX, P:DV1]))
                    did(stt(hm[:, 0:1], hm[:, 0:1], -1.0, hm[:, 0:1], ALU.mult, ALU.max))
                    did(tt(hm[:, 0:1], hm[:, 0:1], selm[:, 0:1], ALU.max))
                    mark(reciprocal(hm[:, 1:2], hm[:, 0:1]).then_inc(mx_rec, 1), mx_rec, g + 1)
                    dve.wait_ge(mx_sq, g + 1)
                    mark(ts(hm[:, 3:4], hm[:, 2:3], 1.0 / P, EPS, ALU.mult, ALU.add).then_inc(mx_ms, 1), mx_ms, g + 1)
                    dve.wait_ge(mx_rs, g + 1)
                    did(tt(hm[:, 5:6], hm[:, 1:2], hm[:, 4:5], ALU.mult))
                    mark(ts(hnm[:, :], T1[0:MIX, 0:P], hm[:, 5:6], None, ALU.mult).then_inc(t1_free, 1), t1_free, at + 1)
                if t == ZC:
                    dve.wait_ge(mx_yc_high, g + 1)
                    mark(tt(ystm[:, 0, 1, :], ycm[:, :], ystm[:, 0, 0, :], ALU.subtract).then_inc(mx_yc_low, 1), mx_yc_low, g + 1)
                if t == ZM:
                    dve.wait_ge(mx_ym_high, g + 1)
                    mark(tt(ystm[:, 1, 1, :], ymm[:, :], ystm[:, 1, 0, :], ALU.subtract).then_inc(mx_ym_low, 1), mx_ym_low, g + 1)

            def dve_block(g, b, first, following):
                for t in range(NT):
                    if b == 0:
                        mixed_start(g, b, t, first)
                    at_half(g, b, t, first)
                    if first:
                        for r in X_END.get(t, ()):
                            x_gain(1 + CH * (b + 1) + r // 2, r % 2, t0(g, b, ("x", r), first))
                    evacuate(g, b, t)
                    if first:
                        for r in X_END.get(t, ()):
                            x_low_part(2 * (1 + CH * (b + 1)) + r)
                    at_end(g, b, t, first)
                    if following == "weights":
                        split_w(g + 1, t)
                    if following == "output weights" and t < KT:
                        dve.wait_ge(wo_high, t + 1)
                        mark(stt(Wol[:, :, t * P:(t + 1) * P], wst[t % STAGES][:, :, :], WS, Woh[:, :, t * P:(t + 1) * P],
                            ALU.mult, ALU.subtract).then_inc(wo_low, 1), wo_low, t + 1)

            GATE_COUNTS = [0, 1] + [t1(0, b, "gates", True) for b in range(NB - 1)]
            COLS_COUNTS = ([t1(0, 0, "mix cols", True)] + [t1(0, b, "cols", True) for b in range(NB - 1)] +
                           [t1(0, NB - 2, "next cols", True)])

            dve.wait_ge(const, 1)
            x_prepare(0)
            x_prepare(1)
            dve.wait_ge(gain_in, 16)
            x_gain(0, 0, 0)
            x_gain(0, 1, 1)
            x_low_part(0)
            x_low_part(1)
            dve.wait_ge(g_high, 1)
            did(stt(Wgl[:, :, 0:H], wgst[:, :, H:2 * H], WS, Wgh[:, :, 0:H], ALU.mult, ALU.subtract))
            mark(stt(Wgl[:, :, 32:GR], wgst[:, :, 0:H], WS, Wgh[:, :, 32:GR], ALU.mult, ALU.subtract).then_inc(g_low, 1), g_low, 1)
            x_gain(1, 0, 2)
            x_gain(1, 1, 3)
            x_prepare(2)
            x_low_part(2)
            x_low_part(3)
            x_gain(2, 0, 4)
            x_prepare(3)
            x_gain(2, 1, 5)
            x_low_part(4)
            x_low_part(5)
            dve.wait_ge(rows_const, 1)
            dve.wait_ge(par_in, 16 * 4)
            gate_abs(0, MIX)
            x_gain(3, 0, 6)
            x_prepare(4)
            x_gain(3, 1, 7)
            x_low_part(6)
            x_low_part(7)
            did(memset(selh[:, :], 0.0))
            for q in range(4):
                did(copy(selh[32 * q:32 * q + H, :], ident[32 * q:32 * q + H, 32 * q:32 * q + H]))
            x_gain(4, 0, 8)
            x_gain(4, 1, 9)
            x_low_part(8)
            x_low_part(9)
            split_w(0, 0)
            gate_rows(0, 0, MIX)
            split_w(0, 1)
            split_w(0, 2)
            did(copy(identb[:, :], ident[:, :]))
            did(ts(seln[:, :], selh[:, :], -1.0, None, ALU.mult))
            gate_abs(1, BT)
            gate_rows(1, MIX, BT)
            for b in range(NB - 1):
                dve_block(0, b, True, None)
            with dve.Fori(1, H) as g:
                order.enter(g)
                dve_block(g - 1, NB - 1, False, "weights")
                for b in range(NB - 1):
                    dve_block(g, b, False, None)
            order.leave(H - 1)
            dve_block(H - 1, NB - 1, False, "output weights")
            heads_out(H, 0, t0(H, 0, "hT", False) - t0_uses(0, False).index("hT"))
            mark(memset(den[:, 0:1], 0.0).then_inc(finals, 1), finals, 1)

            def b_tile(tile, n, i, c, half_count):
                dve.wait_ge(r_in[i], half_count * 16 + 16)
                for h in range(2):
                    dve.wait_ge(b_full, tile * 2 + (h + 1))
                    z = xs[i][0:n, h * BT:(h + 1) * BT]
                    mark(stt(z, OUT[i][h][0:n, :], 1 / WS, z, ALU.mult, ALU.add).then_inc(b_free, 1), b_free, tile * 2 + (h + 1))
                dve.wait_ge(b_sq, tile + 1)
                mark(ts(msx[0:n, c:c + 1], ssx[0:n, c:c + 1], 1.0 / D, EPS, ALU.mult, ALU.add).then_inc(b_ms, 1), b_ms, tile + 1)
                dve.wait_ge(b_rs, tile + 1)
                dve.wait_ge(b_store[i], half_count * 16)
                mark(stt(result[i][0:n, :], xs[i][0:n, :], rsx[0:n, c:c + 1], fgain[0:n, :], ALU.mult, ALU.mult).then_inc(b_out, 1), b_out, tile + 1)

            dve.wait_ge(fg_in, 16)
            b_tile(0, DB * DS, 0, 0, 0)
            with dve.Fori(0, NB) as j:
                for c in range(CH):
                    b_tile(j * CH + (1 + c), P, (1 + c) % 2, 1 + c, j * 2 + (1 + c) // 2)


_INS = ['x_prompt', 'x_sample', 'state_conv', 'state_mlstm_c', 'state_mlstm_n', 'state_mlstm_m', 'meta_tokens',
        'norm_gain', 'w_in', 'conv_w', 'b_igate', 'b_fgate', 'mh_norm_gain', 'w_out', 'final_norm_gain']
_OUTS = [(1, SEQ, D), (DB, DS, D), (1, 2, CW), (1, H, P, P), (1, H, P), (1, H),
         (DB, 2, CW), (DB, H, P, P), (DB, H, P), (DB, H)]


def kernel(**inputs):
    import numpy as _np
    import concourse.bacc as _bacc
    from concourse import mybir as _mybir
    from concourse.bass_utils import run_bass_kernel_spmd as _run

    nc = _bacc.Bacc("TRN2", target_bir_lowering=False, num_devices=1)
    arrays, args = {}, []
    for name in _INS:
        a = _np.ascontiguousarray(inputs[name])
        arrays[f"in_{name}"] = a
        args.append(nc.dram_tensor(f"in_{name}", a.shape, _mybir.dt.from_np(a.dtype), kind="ExternalInput").ap())
    for i, shape in enumerate(_OUTS):
        args.append(nc.dram_tensor(f"out_{i}", shape, _mybir.dt.float32, kind="ExternalOutput").ap())
    args.append(nc.dram_tensor("y_mid", (KT, P, 2, NTOK), _mybir.dt.float16, kind="Internal").ap())
    build(nc, *args)
    r = _run(nc, [arrays], core_ids=[0])
    return tuple(r.results[0][f"out_{i}"] for i in range(len(_OUTS)))
```

```python
import concourse.bass as bass
from concourse import mybir
from contextlib import ExitStack

F32 = mybir.dt.float32
F16 = mybir.dt.float16
BF16 = mybir.dt.bfloat16
ALU = mybir.AluOpType
ACT = mybir.ActivationFunctionType

P = 128
D = 1024
KT = D // P
SEQ = 2048
META = 16
DB, DS = 8, 8
MIX = META + DB * DS
H = 4
CW = 512
NB, CH = 4, 4
BT = CH * P
NTOK = MIX + SEQ
EPS = 1e-6
NEG = -1.0e30
WS = 64.0
SK = float(P) ** -0.5
K, V, Q, GC, HC, GB, ZC, O, ZM = range(9)
NT = 9
TILE_COL = {GB: 0, GC: CW, HC: 2 * CW, ZC: 3 * CW, Q: 4 * CW, K: 5 * CW, V: 6 * CW, O: 7 * CW, ZM: 8 * CW}
IG_COL, FG_COL = 9 * CW, 9 * CW + H
GR = 32 + H
A_COL = 40
DV1 = P + 1
STATES_IN = DB * H + DB * 2 * H
STATES_OUT = STATES_IN + 3 * H
PARAMS = KT + 4 * H
STAGES = 3
XBUF = 3
SEGS = [(0, META)] + [(META + DS * i, DS) for i in range(DB)]
SAMPLE_ROUNDS = [(0, 3), (3, 6), (6, 8)]

T0_PRO = 2 + 2 * CH
T1_PRO = 4
X_HALF = {HC: (3,), GB: (5,), ZC: (7,)}
X_END = {V: (0,), Q: (1,), GC: (2,), HC: (4,), GB: (6,)}
X_SQUARE = {K: 0, Q: 1, GC: 2, HC: 3}
SPLIT_AT_HALF = {Q: (4,), GC: (5,), HC: (6,), GB: (7,), ZC: (8,)}
DVE_TURN = 61
ACT_TURN = 37


def t0_uses(b, first):
    names = []
    for t in range(NT):
        names += [("mix", t)] if b == 0 else []
        names += {V: [] if first and b == 0 else ["hT"], Q: ["kT"], GC: ["vT"]}.get(t, [])
        names += [("x", r) for r in X_HALF.get(t, ()) + X_END.get(t, ())] if first else []
    return names


def t1_uses(b, first):
    names = []
    for t in range(NT):
        names += {K: ["mix cols"] if b == 0 else [], Q: ["cols"]}.get(t, []) if first else []
        names += {Q: ["args"], GC: ["kv"], HC: ["score"], GB: ["num"], O: ["hT"]}.get(t, []) if b == 0 else []
        names += [("state", t - V)] if b == 1 and t in (V, Q, GC) else []
        names += {ZC: ["gates"], ZM: ["next cols"] if b == NB - 2 else []}.get(t, []) if first else []
    return names


def ordinal(uses, before, g, b, name, first):
    turn = sum(len(uses(x, False)) for x in range(NB))
    start = before + sum(len(uses(x, True)) for x in range(NB - 1))
    if first:
        return before + sum(len(uses(x, True)) for x in range(b)) + uses(b, True).index(name)
    if b == NB - 1:
        return g * turn + (start + uses(b, False).index(name))
    inside = len(uses(NB - 1, False)) + sum(len(uses(x, False)) for x in range(b))
    return (g - 1) * turn + (start + inside + uses(b, False).index(name))


def t0(g, b, name, first):
    return ordinal(t0_uses, T0_PRO, g, b, name, first)


def t1(g, b, name, first):
    return ordinal(t1_uses, T1_PRO, g, b, name, first)


def tok0(b):
    return MIX + BT * b


def nth(g, b):
    return g * NB + b


class Order:

    def __init__(self, eng, sem, per_turn):
        self.eng, self.sem, self.per_turn, self.n, self.base, self.last = eng, sem, per_turn, 0, 0, None

    def did(self, instruction):
        instruction.then_inc(self.sem, 1)
        self.n += 1
        self.last = (self.sem, self.base + self.n)

    def mark(self, instruction, sem, value):
        self.last = (sem, value)

    def settle(self):
        if self.last:
            self.eng.wait_ge(*self.last)

    def after(self, op):
        def run(*operands, **named):
            self.settle()
            return op(*operands, **named)
        return run

    def enter(self, g):
        self.settle()
        self.start, self.base, self.last = self.n, (g - 1) * self.per_turn, None

    def leave(self, turns):
        assert self.n - self.start == self.per_turn, (self.sem, self.n - self.start, self.per_turn)
        self.base, self.last = (turns - 1) * self.per_turn, None


def build(nc, x_prompt, x_sample, state_conv, state_c, state_n, state_m, meta, norm_gain, w_in, conv_w,
          b_igate, b_fgate, mh_gain, w_out, final_gain, y_prompt, y_sample, conv_p, c_p, n_p, m_p,
          conv_s, c_s, n_s, m_s, y_mid):
    ctx = ExitStack()
    with ctx:
        ctx.enter_context(nc.allow_non_contiguous_dma(reason="small parameters and states"))

        def sb(name, shape, dt=F32):
            return ctx.enter_context(nc.sbuf_tensor(name, shape, dt))

        def sem(name):
            return ctx.enter_context(nc.semaphore(name))

        xTh, xTl = sb("xTh", [P, KT, NTOK], F16), sb("xTl", [P, KT, NTOK], F16)
        Wh, Wl = sb("Wh", [P, NT, KT, P], F16), sb("Wl", [P, NT, KT, P], F16)
        Wg = sb("Wg", [P, KT, 64 + GR], F16)
        mparts = sb("mparts", [64 + H, NTOK], BF16)
        cols = sb("cols", [P, 1 + NB * CH, 5, H])
        decs = sb("decs", [P, DB, H])
        Woh, Wol = xTh[:, :, 0:D], xTl[:, :, 0:D]
        ybuf = [x[:, :, D + META:D + META + BT].rearrange("p k (s t) -> p k s t", s=2) for x in (xTh, xTl)]
        wst = [sb(f"wst{i}", [P, KT, P]) for i in range(STAGES)]
        result = [w[:, :, :].rearrange("p k c -> p (k c)") for w in wst[0:2]]
        wgst = sb("wgst", [P, KT, 2 * H])
        xs = [sb(f"xs{i}", [P, D]) for i in range(XBUF)]
        junk = sb("junk", [P, D], F16)
        xtmp = [sb(f"xtmp{i}", [P, BT]) for i in range(2)]
        fgain = sb("fgain", [P, D])
        ident, ones = sb("ident", [P, P]), sb("ones", [P, P])
        identb, maskb = sb("identb", [P, P], BF16), sb("maskb", [P, P], BF16)
        mixmask = sb("mixmask", [MIX, MIX], BF16)
        segind = sb("segind", [MIX, DB])
        selh, seln = sb("selh", [P, H]), sb("seln", [P, H])
        prow, par = sb("prow", [P, P]), sb("par", [P, STATES_OUT + PARAMS])
        nst = par[:, 0:DB * H].rearrange("p (b h) -> p b h", h=H)
        cst = par[:, DB * H:STATES_IN].rearrange("p (b j h) -> p h (b j)", j=2, h=H)
        npo = par[:, STATES_IN:STATES_IN + H]
        cpo = par[:, STATES_IN + H:STATES_OUT].rearrange("p (j h) -> p h j", h=H)
        gain, mhg = par[:, STATES_OUT:STATES_OUT + KT], par[:, STATES_OUT + KT:STATES_OUT + KT + H]
        cwt = par[:, STATES_OUT + KT + H:].rearrange("p (j h) -> p h j", h=H)
        biasg, halves = sb("biasg", [GR, 1]), sb("halves", [P, CH])
        gwork = sb("gwork", [64 + GR, BT])
        grow, trr = gwork[0:GR, :], gwork[64:64 + GR, :]
        gt, lf = fgain[0:H, 0:BT], fgain[0:H, BT:2 * BT]
        mst = sb("mst", [H, NB * CH + 2])
        sm0, smn = sb("sm0", [H, DB]), sb("smn", [H, DB])
        restart, remix, forget = sb("restart", [H, BT]), sb("remix", [H, MIX]), sb("forget", [H, DB * DS])
        arow, mpart = sb("arow", [H, BT]), sb("mpart", [H, BT], BF16)
        rl, drl = sb("rl", [H, DB]), sb("drl", [H, DB * H])
        selneg = sb("selneg", [64 + H, P], BF16)
        kf, vf, qf = sb("kf", [P, BT]), sb("vf", [P, BT]), sb("qf", [P, BT])
        v1 = sb("v1", [P, CH, DV1])
        dp = sb("dp", [P, BT])
        eh = sb("eh", [P, BT])
        kw = sb("kw", [P, BT])
        u, gcs, yc, zs = sb("u", [P, BT + 2]), sb("gcs", [P, BT]), sb("yc", [P, BT]), sb("zs", [P, BT])
        tz, to, G = sb("tz", [P, BT]), sb("to", [P, BT]), sb("G", [P, BT])
        bcum, mrow = gcs[0:H, :], yc[0:H, :]
        sel, cn = sb("sel", [P, CH, 5]), sb("cn", [P, DV1])
        den, rec, hss, hms, hrs, hf = (sb(n, [P, CH]) for n in ("den", "rec", "hss", "hms", "hrs", "hf"))
        yst = sb("yst", [P, 2, 2, BT], F16)
        rows = sb("rows", [P, MIX])
        rbm = sb("rbm", [64 + H, MIX])
        kfm, vfm, qfm, gcm, ycm, zsm, tzm, tom, Gm, ehm, ymm = (
            sb(n, [P, MIX]) for n in ("kfm", "vfm", "qfm", "gcm", "ycm", "zsm", "tzm", "tom", "Gm", "ehm", "ymm"))
        um = sb("um", [P, META + 2 + DB * (DS + 2)])
        dpm, kwm, hnm = sb("dpm", [MIX, MIX]), sb("kwm", [MIX, P]), sb("hnm", [MIX, P])
        v1m, v1x = sb("v1m", [MIX, DV1]), sb("v1x", [MIX, DB, DV1])
        qm = sb("qm", [P, DB * (MIX + DS)])
        cs = sb("cs", [P, DB, DV1])
        selm, dselm = sb("selm", [MIX, 2]), sb("dselm", [P, DB])
        hm = sb("hm", [MIX, 6])
        ystm = sb("ystm", [P, 2, 2, MIX], F16)
        ssx, msx, rsx = sb("ssx", [P, 17]), sb("msx", [P, 17]), sb("rsx", [P, 17])

        bank = [ctx.enter_context(nc.psum_tensor(f"bank{i}", [P, BT], F32)) for i in range(8)]
        PB, T0, T1, A, S, N = bank[0:2], bank[2], bank[3], bank[4], bank[5], bank[6:8]
        T1_END = t1(H, 0, "args", False) - t1_uses(0, False).index("args")
        OUT = [bank[0:2], bank[4:6]]

        par_in, states_in, bias_in, gate_in, fg_in, cs_in = (sem(n) for n in (
            "par_in", "states_in", "bias_in", "gate_in", "fg_in", "cs_in"))
        x_in = [sem(f"x_in{i}") for i in range(XBUF)]
        w_in_s = [sem(f"w_in{i}") for i in range(STAGES)]
        const, rows_const, const2, bias_clear = (sem(n) for n in ("const", "rows_const", "const2", "bias_clear"))
        w_high, w_low, g_high, g_low = sem("w_high"), sem("w_low"), sem("g_high"), sem("g_low")
        x_sq, x_ms, x_rs, x_scaled = sem("x_sq"), sem("x_ms"), sem("x_rs"), sem("x_scaled")
        x_high, x_low = sem("x_high"), sem("x_low")
        tile_done, p_free = sem("tile_done"), [sem("p0_free"), sem("p1_free")]
        t0_full, t0_free, t1_full, t1_free = sem("t0_full"), sem("t0_free"), sem("t1_full"), sem("t1_free")
        a_full, a_free, s_full, s_free = sem("a_full"), sem("a_free"), sem("s_full"), sem("s_free")
        e_full, e_ready, n_full, n_free = sem("e_full"), sem("e_ready"), sem("n_full"), sem("n_free")
        g_logits, g_abs, g_exp, g_ln, rows_ready = (
            sem(n) for n in ("g_logits", "g_abs", "g_exp", "g_ln", "rows_ready"))
        sel_ready, q_scaled, gc_used = sem("sel_ready"), sem("q_scaled"), sem("gc_used")
        tanh_zc, tanh_zm, g_done = sem("tanh_zc"), sem("tanh_zm"), sem("g_done")
        rec_ready, h_sq, h_ms, h_rs = sem("rec_ready"), sem("h_sq"), sem("h_ms"), sem("h_rs")
        yc_ready, yc_high, yc_low, ym_high, ym_low = (
            sem(n) for n in ("yc_ready", "yc_high", "yc_low", "ym_high", "ym_low"))
        y_out_c, y_out_m = sem("y_out_c"), sem("y_out_m")
        mx_q, mx_tanh_zc, mx_tanh_zm, mx_gc_used, mx_g = (
            sem(n) for n in ("mx_q", "mx_tanh_zc", "mx_tanh_zm", "mx_gc_used", "mx_g"))
        mx_rec, mx_sq, mx_ms, mx_rs, mx_yc, mx_yc_high, mx_yc_low, mx_ym_high, mx_ym_low = (
            sem(n) for n in ("mx_rec", "mx_sq", "mx_ms", "mx_rs", "mx_yc", "mx_yc_high", "mx_yc_low",
                             "mx_ym_high", "mx_ym_low"))
        mx_out_c, mx_out_m, mx_v_wide, mx_n, mx_states, cs_out = (
            sem(n) for n in ("mx_out_c", "mx_out_m", "mx_v_wide", "mx_n", "mx_states", "cs_out"))
        cn_meta, cn_out, dve_step, act_step, pool_step, out_sem = (
            sem(n) for n in ("cn_meta", "cn_out", "dve_step", "act_step", "pool_step", "out_sem"))
        wo_high, wo_low, finals, rows_out = (sem(n) for n in ("wo_high", "wo_low", "finals", "rows_out"))
        y_in, r_in, b_store = ([sem(f"{n}{i}") for i in range(2)] for n in ("y_in", "r_in", "b_store"))
        b_full, b_free, b_sq, b_ms, b_rs, b_out = (
            sem(n) for n in ("b_full", "b_free", "b_sq", "b_ms", "b_rs", "b_out"))

        useg = um[:, META + 2:].rearrange("p (b t) -> p b t", t=DS + 2)
        qdiag = qm[:, :].rearrange("p (b t) -> p b t", t=MIX + DS)[:, :, META:META + DS]

        def samples(ap):
            return ap[:, META:MIX].rearrange("p (b t) -> p b t", t=DS)

        def wide(ap, n):
            return ap.unsqueeze(2).broadcast_to([ap.shape[0], ap.shape[1], n])

        def evacuations(g, b, t):
            j = NT * b + t
            return j % 2, g * (NT * NB // 2) + j // 2

        def x_bank(count):
            return N[1] if count < T0_PRO and count % 2 else T0

        def chunks(ap):
            return ap.rearrange("p (c t) -> p c t", c=CH)

        def load_w(queue, g, t):
            src = w_in[:, bass.ds(g * P + TILE_COL[t], P)].rearrange("(k p) c -> p k c", p=P)
            queue.dma_start(wst[t % STAGES][:, :, :], src).then_inc(w_in_s[t % STAGES], 16)

        def load_states(queue, g):
            src = state_c[:, bass.ds(g, 1), :, :].rearrange("b h d v -> d (b h) v")
            queue.dma_start(cs[:, :, 0:P], src).then_inc(cs_in, 16)

        def load_rows(queue, done, at, *parts):
            for src in parts:
                queue.dma_start(prow[at:at + src.shape[0], :], src).then_inc(done, 16)
                at += src.shape[0]

        block = ctx.enter_context(nc.Block())

        @block.sync
        def _(sp):
            def load_x(unit):
                s = unit % XBUF
                if unit >= XBUF:
                    sp.wait_ge(t0_full, t0_after_x(unit - XBUF))
                if unit == 0:
                    sp.dma_start(xs[0][0:META, :], meta).then_inc(x_in[0], 16)
                    sp.dma_start(xs[0][META:MIX, :], x_sample.rearrange("b t d -> (b t) d")).then_inc(x_in[0], 16)
                else:
                    r = (unit - 1) * P
                    sp.dma_start(xs[s][:, :], x_prompt[0, r:r + P, :]).then_inc(x_in[s], 16)

            def t0_after_x(unit):
                if unit <= CH:
                    return 2 * unit + 2
                b, c = divmod(unit - 1 - CH, CH)
                return t0(0, b, ("x", 2 * c + 1), True) + 1

            load_x(0)
            load_x(1)
            load_x(2)
            load_w(sp, 0, 0)
            load_w(sp, 0, 1)
            load_w(sp, 0, 2)
            load_x(3)
            load_x(4)
            load_rows(sp, states_in, 0, state_n.rearrange("b h p -> (b h) p"), state_conv.rearrange("b j (h p) -> (b j h) p", p=P))
            load_states(sp, 0)
            load_x(5)
            for t in range(STAGES, NT):
                sp.wait_ge(w_low, t - STAGES + 1)
                load_w(sp, 0, t)
                if t - STAGES in (1, 3):
                    load_x(6 + (t - STAGES) // 2)
            for unit in range(2 * CH, 1 + CH * NB):
                load_x(unit)
            for t in range(KT):
                if t < STAGES:
                    sp.wait_ge(w_low, NT * H - STAGES + t + 1)
                else:
                    sp.wait_ge(wo_low, t - STAGES + 1)
                sp.dma_start(wst[t % STAGES][:, :, :],
                             w_out[:, t * P:(t + 1) * P].rearrange("(k p) c -> p k c", p=P)).then_inc(w_in_s[t % STAGES], 16)

            def load_y(slot, tok, n):
                for k in range(KT):
                    sp.dma_start(ybuf[slot][:, k, :, 0:n], y_mid[k, :, :, bass.ds(tok, n)]).then_inc(y_in[slot], 16)

            sp.dma_start(fgain[:, :], final_gain.rearrange("(o d) -> o d", o=1).broadcast_to([P, D])).then_inc(fg_in, 16)
            sp.wait_ge(mx_out_c, 16 * H)
            sp.wait_ge(mx_out_m, 16 * H)
            sp.wait_ge(tile_done, NT * (NB * H - 1) + 1)
            load_y(0, META, DB * DS)
            sp.wait_ge(x_scaled, 17)
            sp.dma_start(xs[0][0:DB * DS, :], x_sample.rearrange("b t d -> (b t) d")).then_inc(r_in[0], 16)
            for j in range(NB):
                sp.wait_ge(y_out_c, (j + (NB * (H - 1) + 1)) * 16)
                sp.wait_ge(y_out_m, (j + (NB * (H - 1) + 1)) * 16)
                for c in range(CH):
                    if c % 2 == 0:
                        slot = 1 - c // 2
                        sp.wait_ge(b_full, j * (2 * CH) + (0 if slot else 2))
                        load_y(slot, j * BT + (MIX + c * P), 2 * P)
                    i = (1 + c) % 2
                    sp.wait_ge(b_out, j * CH + c)
                    sp.dma_start(xs[i][:, :], x_prompt[0, bass.ds(j * BT + c * P, P), :]).then_inc(r_in[i], 16)

        @block.gpsimd
        def _(pool):
            made = [0]

            def step(ins):
                ins.then_inc(pool_step, 1)
                made[0] += 1
                pool.wait_ge(pool_step, made[0])

            pool.memset(biasg[:, :], 0.0).then_inc(bias_clear, 1)
            pool.wait_ge(bias_clear, 1)
            step(pool.memset(ident[:, :], 0.0))
            step(pool.affine_select(out=ident[:, :], in_=ident[:, :], compare_op=ALU.not_equal, fill=1.0, base=0,
                                    pattern=[[-1, P]], channel_multiplier=1))
            step(pool.memset(halves[:, :], -0.5))
            pool.memset(Wg[:, :, :], 0.0).then_inc(const, 1)
            pool.wait_ge(const, 1)

            def x_power(unit):
                n = MIX if unit == 0 else P
                pool.wait_ge(x_sq, unit + 1)
                pool.tensor_scalar(msx[0:n, unit:unit + 1], ssx[0:n, unit:unit + 1], 1.0 / D, EPS, ALU.mult, ALU.add).then_inc(x_ms, 1)
                pool.wait_ge(x_ms, unit + 1)
                pool.tensor_tensor(rsx[0:n, unit:unit + 1], msx[0:n, unit:unit + 1], halves[0:n, 0:1], ALU.pow).then_inc(x_rs, 1)

            x_power(0)
            x_power(1)
            step(pool.memset(ones[:, :], 1.0))
            step(pool.memset(trr, 0.0))
            step(pool.memset(mst[:, :], 0.0))
            for tile, first_of, rest, start in ((restart, chunks(restart[:, :]), 1.0, 0.0), (remix, samples(remix), 1.0, 0.0),
                                               (forget, forget[:, :].rearrange("p (b t) -> p b t", t=DS), 0.0, NEG)):
                step(pool.memset(tile[:, :], rest))
                step(pool.memset(first_of[:, :, 0], start))
            step(pool.memset(rows[0:32, :], 0.0))
            step(pool.memset(rows[32:GR, :], 1.0))
            pool.memset(mparts[:, :], 0.0).then_inc(rows_const, 1)
            pool.wait_ge(rows_const, 1)
            x_power(2)
            step(pool.memset(maskb[:, :], 0.0))
            step(pool.affine_select(out=maskb[:, :], in_=maskb[:, :], compare_op=ALU.is_ge, fill=NEG, base=0,
                                    pattern=[[1, P]], channel_multiplier=-1))
            step(pool.tensor_copy(mixmask[:, :], maskb[0:MIX, 0:MIX]))
            x_power(3)
            step(pool.memset(v1[:, :, P:DV1], 1.0))
            step(pool.memset(um[:, 0:2], 0.0))
            step(pool.memset(v1m[:, P:DV1], 1.0))
            step(pool.memset(rbm[:, :], 0.0))
            x_power(4)
            step(pool.memset(qm[:, :], 0.0))
            for at, n in SEGS[1:]:
                step(pool.affine_select(out=mixmask[:, at:at + n], in_=mixmask[:, at:at + n], compare_op=ALU.is_ge,
                                        fill=NEG, base=-at, pattern=[[0, n]], channel_multiplier=1))
            step(pool.memset(segind[:, :], 1.0))
            step(pool.affine_select(out=segind[:, :], in_=segind[:, :], compare_op=ALU.is_ge, fill=0.0, base=-META,
                                    pattern=[[-DS, DB]], channel_multiplier=1))
            pool.affine_select(out=segind[:, :], in_=segind[:, :], compare_op=ALU.is_ge, fill=0.0, base=META + DS - 1,
                               pattern=[[DS, DB]], channel_multiplier=-1).then_inc(const2, 1)
            pool.wait_ge(const2, 1)

            def store_y(g, b, part):
                done, out = ((yc_low, y_out_c), (ym_low, y_out_m))[part]
                pool.wait_ge(done, nth(g, b) + 1)
                dst = y_mid[bass.ds(g + H * part, 1), :, :, tok0(b):tok0(b) + BT].rearrange("k p s t -> p (k s) t")
                pool.dma_start(dst, yst[:, part, :, :]).then_inc(out, 16)

            def store_mixed(g, part):
                done, out = ((mx_yc_low, mx_out_c), (mx_ym_low, mx_out_m))[part]
                pool.wait_ge(done, g + 1)
                dst = y_mid[bass.ds(g + H * part, 1), :, :, 0:MIX].rearrange("k p s t -> p (k s) t")
                pool.dma_start(dst, ystm[:, part, :, :]).then_inc(out, 16)

            def pool_block(g, b, first):
                if first:
                    x_power(1 + CH * (b + 1))
                if not (first and b == 0):
                    store_y(g if b else g - 1, b - 1 if b else NB - 1, 1)
                if first:
                    for c in range(1, CH):
                        x_power(1 + CH * (b + 1) + c)
                if b == 0:
                    pool.wait_ge(mx_ms, g + 1)
                    pool.tensor_tensor(hm[:, 4:5], hm[:, 3:4], halves[0:MIX, 0:1], ALU.pow).then_inc(mx_rs, 1)
                    store_mixed(g, 0)
                if b == 1:
                    pool.wait_ge(mx_states, g + 1)
                    dst = c_s[:, bass.ds(g, 1), :, :].rearrange("b h d v -> d (b h) v")
                    pool.dma_start(dst, cs[:, :, 0:P]).then_inc(cs_out, 16)
                store_y(g, b, 0)
                pool.wait_ge(h_ms, nth(g, b) + 1)
                pool.tensor_tensor(hrs[:, :], hms[:, :], halves[:, :], ALU.pow).then_inc(h_rs, 1)
                if b == 0:
                    store_mixed(g, 1)
                if b == NB - 1:
                    pool.wait_ge(s_free, nth(g, b) * 3 + 3)
                    pool.dma_start(c_p[0, bass.ds(g, 1), :, :].rearrange("h d v -> d (h v)"), cn[:, 0:P]).then_inc(cn_out, 16)

            for b in range(NB - 1):
                pool_block(0, b, True)
            with pool.Fori(1, H) as g:
                pool_block(g - 1, NB - 1, False)
                for b in range(NB - 1):
                    pool_block(g, b, False)
            pool_block(H - 1, NB - 1, False)
            store_y(H - 1, NB - 1, 1)

            def b_tile(tile, n, c, dst):
                pool.wait_ge(b_ms, tile + 1)
                pool.tensor_tensor(rsx[0:n, c:c + 1], msx[0:n, c:c + 1], halves[0:n, 0:1], ALU.pow).then_inc(b_rs, 1)
                pool.wait_ge(b_out, tile + 1)
                pool.dma_start(dst, result[c % 2][0:n, :]).then_inc(b_store[c % 2], 16)

            pool.wait_ge(finals, 1)
            pool.dma_start(m_p.rearrange("o h -> h o"), mst[:, NB * CH + 1:NB * CH + 2]).then_inc(out_sem, 16)
            pool.dma_start(m_s.rearrange("b h -> h b"), smn[:, :]).then_inc(out_sem, 16)
            b_tile(0, DB * DS, 0, y_sample.rearrange("b t d -> (b t) d"))
            pool.wait_ge(rows_out, 1)
            at = 0
            for dst in (n_s.rearrange("b h p -> (b h) p"), conv_s.rearrange("b j (h p) -> (b j h) p", p=P), n_p[0],
                        conv_p[0].rearrange("j (h p) -> (j h) p", p=P)):
                pool.dma_start(dst, prow[at:at + dst.shape[0], :]).then_inc(out_sem, 16)
                at += dst.shape[0]
            with pool.Fori(0, NB) as j:
                for c in range(CH):
                    b_tile(j * CH + (1 + c), P, 1 + c, y_prompt[0, bass.ds(j * BT + c * P, P), :])
            pool.wait_ge(b_store[0], 16 * 9)
            pool.wait_ge(b_store[1], 16 * 8)
            pool.wait_ge(out_sem, 16 * 6)
            pool.wait_ge(cs_out, 16 * H)
            pool.wait_ge(cn_out, 16 * H)

        @block.tensor
        def _(pe):
            mm = nc.tensor.matmul

            def split_product(out, wh, wl, k0, k1, tok, n):
                for k in range(k0, k1):
                    xh, xl = xTh[:, k, tok:tok + n], xTl[:, k, tok:tok + n]
                    mm(out, wh[:, k, :], xh, start=(k == 0), stop=False)
                    mm(out, wh[:, k, :], xl, start=False, stop=False)
                    last = mm(out, wl[:, k, :], xh, start=False, stop=(k == KT - 1))
                return last

            def use_t0(count):
                pe.wait_ge(t0_free, count)

            def use_t1(count):
                pe.wait_ge(t1_free, count)

            def x_round(unit, r, count):
                n = MIX if unit == 0 else P
                pe.wait_ge(x_scaled, unit + 1)
                bank_ = x_bank(count)
                if count < T0_PRO:
                    if count > 1:
                        pe.wait_ge(t0_free, count - 1)
                else:
                    use_t0(count)
                for k in range(4):
                    last = nc.tensor.transpose(bank_[:, k * n:k * n + n], xs[unit % XBUF][0:n, (4 * r + k) * P:(4 * r + k + 1) * P],
                                               ident[0:n, 0:n])
                last.then_inc(t0_full, 1)

            def gates(rounds, tok, n, count):
                pe.wait_ge(x_low, rounds)
                use_t1(count)
                for k in range(KT):
                    if k:
                        mm(T1[0:GR, 0:n], Wg[:, k - 1, 0:GR], xTl[:, k - 1, tok:tok + n], start=False, stop=False)
                    if k == KT - 1:
                        mm(T1[0:GR, 0:n], Wg[:, k, 0:GR], xTl[:, k, tok:tok + n], start=False, stop=False)
                    last = mm(T1[0:64 + GR, 0:n], Wg[:, k, :], xTh[:, k, tok:tok + n], start=(k == 0), stop=(k == KT - 1))
                last.then_inc(t1_full, 1)

            def columns(units, n, count):
                pe.wait_ge(rows_const, 1)
                pe.wait_ge(rows_ready, units)
                use_t1(count)
                for c in range(0 if n == MIX else CH):
                    nc.tensor.transpose(T1[:, c * 64 + A_COL:c * 64 + A_COL + H], arow[:, c * P:(c + 1) * P], ident[0:H, 0:H])
                for c in range(1 if n == MIX else CH):
                    nc.tensor.transpose(T1[0:min(n, P), c * 64:c * 64 + GR], trr[:, c * P:c * P + min(n, P)], ident[64:64 + GR, 64:64 + GR])
                mm(T1[:, 256:256 + DB * H], ones[0:H, :], drl[:, :], start=True, stop=True).then_inc(t1_full, 1)

            def transposed(src, count):
                use_t0(count)
                for c in range(CH):
                    last = nc.tensor.transpose(T0[:, c * P:(c + 1) * P], src[:, c * P:(c + 1) * P], ident[:, :])
                last.then_inc(t0_full, 1)

            def chunk(g, b, c, first):
                n = nth(g, b)
                out = N[c // 2][:, (c % 2) * DV1:(c % 2 + 1) * DV1]
                if c == 0:
                    pe.wait_ge(s_free, n * 3 + 1)
                    pe.wait_ge(q_scaled, n + 1)
                    pe.wait_ge(t0_free, t0(g, b, "vT", first) + 1)
                    if b == 0:
                        pe.wait_ge(cn_meta, g + 1)
                    else:
                        pe.wait_ge(s_free, n * 3)
                else:
                    pe.wait_ge(a_free if c % 2 else s_free, n * 3 + 2 + (c - 1) // 2)
                mm(out, dp[:, c * P:(c + 1) * P], v1[:, c, :], start=True, stop=False)
                last = mm(out, eh[:, c * P:(c + 1) * P], cn[:, :], start=False, stop=True)
                if c == CH - 1:
                    last.then_inc(n_full, 1)
                kv, full, free = ((S, s_full, s_free), (A, a_full, a_free))[1 - c % 2]
                pe.wait_ge(free, n * 3 + 1 + c // 2)
                mm(kv[:, 0:DV1], kw[:, c * P:(c + 1) * P], v1[:, c, :], start=True, stop=True).then_inc(full, 1)

            def at_half(g, b, t, first):
                n = nth(g, b)
                if t == V and not (first and b == 0):
                    pe.wait_ge(n_free, n)
                    transposed(eh, t0(g, b, "hT", first))
                if t == K and first and b == 0:
                    columns(1, MIX, t1(g, b, "mix cols", first))
                if t == Q:
                    if first:
                        pe.wait_ge(const2, 1)
                        columns(b + 2, BT, t1(g, b, "cols", first))
                    bank_, left = evacuations(g, b, K)
                    pe.wait_ge(p_free[bank_], left + 1)
                    transposed(kf, t0(g, b, "kT", first))
                if t == GC:
                    bank_, left = evacuations(g, b, V)
                    pe.wait_ge(p_free[bank_], left + 1)
                    transposed(vf, t0(g, b, "vT", first))
                if t == ZC:
                    chunk(g, b, 0, first)
                if t == O:
                    chunk(g, b, 2, first)
                if first:
                    for r in X_HALF.get(t, ()):
                        x_round(1 + CH * (b + 1) + r // 2, r % 2, t0(g, b, ("x", r), first))

            def at_end(g, b, t, first):
                n = nth(g, b)
                if first:
                    for r in X_END.get(t, ()):
                        x_round(1 + CH * (b + 1) + r // 2, r % 2, t0(g, b, ("x", r), first))
                if t == Q:
                    pe.wait_ge(sel_ready, n + 1)
                    pe.wait_ge(a_free, n * 3)
                    m = mparts[:, tok0(b):tok0(b) + BT]
                    mm(A[:, :], selneg[:, :], m, start=True, stop=False)
                    mm(A[:, :], identb[:, :], maskb[:, :].unsqueeze(1).broadcast_to([P, CH, P]), start=False, stop=True)\
                        .then_inc(a_full, 1)
                    pe.wait_ge(n_free, n)
                    mm(N[0][:, :], selneg[:, :], m, start=True, stop=True).then_inc(e_full, 1)
                if t == GC:
                    bank_, left = evacuations(g, b, Q)
                    pe.wait_ge(p_free[bank_], left + 1)
                    pe.wait_ge(s_free, n * 3)
                    for c in range(CH):
                        cc = slice(c * P, (c + 1) * P)
                        last = mm(S[:, cc], kf[:, cc], qf[:, cc], start=True, stop=True)
                    last.then_inc(s_full, 1)
                if t == ZC:
                    chunk(g, b, 1, first)
                if t == O:
                    chunk(g, b, 3, first)
                if b == 0:
                    mixed_end(g, b, t, first)
                if b == 1 and t in (V, Q, GC):
                    i0, i1 = SAMPLE_ROUNDS[t - V]
                    pe.wait_ge(mx_v_wide, g + 1)
                    use_t1(t1(g, b, ("state", t - V), first))
                    mm(T1[:, 0:(i1 - i0) * DV1], kwm[:, :], v1x[:, i0:i1, :].rearrange("p b v -> p (b v)"),
                       start=True, stop=True).then_inc(t1_full, 1)
                if first and t == ZC:
                    gates(2 + 2 * CH * (b + 2), tok0(b + 1), BT, t1(g, b, "gates", first))
                if first and b == NB - 2 and t == ZM:
                    columns(b + 3, BT, t1(g, b, "next cols", first))

            def mixed_end(g, b, t, first):
                if t == Q:
                    use_t1(t1(g, b, "args", first))
                    mm(T1[0:MIX, 0:MIX], rows[0:GR, 0:MIX], rbm[0:GR, :], start=True, stop=False)
                    mm(T1[0:MIX, 0:MIX], identb[0:MIX, 0:MIX], mixmask[:, :], start=False, stop=True)
                    mm(T1[:, P:P + MIX], ones[64:64 + H, :], rbm[64:64 + H, :], start=True, stop=True).then_inc(t1_full, 1)
                if t == GC:
                    pe.wait_ge(t0_free, t0(g, b, ("mix", V), first) + 1)
                    use_t1(t1(g, b, "kv", first))
                    nc.tensor.transpose(T1[0:MIX, 0:P], kfm[:, :], ident[:, :])
                    nc.tensor.transpose(T1[0:MIX, P:2 * P], vfm[:, :], ident[:, :]).then_inc(t1_full, 1)
                if t == HC:
                    pe.wait_ge(t0_free, t0(g, b, ("mix", Q), first) + 1)
                    use_t1(t1(g, b, "score", first))
                    mm(T1[0:MIX, 0:MIX], kfm[:, :], qfm[:, :], start=True, stop=True).then_inc(t1_full, 1)
                if t == GB:
                    use_t1(t1(g, b, "num", first))
                    pe.wait_ge(mx_q, g + 1)
                    pe.wait_ge(cs_in, (g + 1) * 16)
                    pe.wait_ge(mx_n, g + 1)
                    o = T1[0:MIX, 0:DV1]
                    mm(o, dpm[:, :], v1m[:, :], start=True, stop=False)
                    for i in range(DB):
                        mm(o, qm[:, i * MIX:(i + 1) * MIX], cs[:, i, :], start=False, stop=(i == DB - 1))
                    mm(T1[:, 2 * P:2 * P + DV1], kwm[0:META, :], v1m[0:META, :], start=True, stop=True).then_inc(t1_full, 1)
                if t == O:
                    use_t1(t1(g, b, "hT", first))
                    nc.tensor.transpose(T1[:, 0:MIX], hnm[:, :], ident[0:MIX, 0:MIX]).then_inc(t1_full, 1)

            def pe_block(g, b, first):
                for t in range(NT):
                    if b == 0:
                        pe.wait_ge(w_low, g * NT + (t + 1))
                    if b == 0:
                        use_t0(t0(g, b, ("mix", t), first))
                        split_product(T0[:, 0:MIX], Wh[:, t, :, :], Wl[:, t, :, :], 0, KT, 0, MIX).then_inc(t0_full, 1)
                    bank_, left = evacuations(g, b, t)
                    pe.wait_ge(p_free[bank_], left)
                    out = PB[bank_][:, :]
                    split_product(out, Wh[:, t, :, :], Wl[:, t, :, :], 0, KT // 2, tok0(b), BT)
                    at_half(g, b, t, first)
                    split_product(out, Wh[:, t, :, :], Wl[:, t, :, :], KT // 2, KT, tok0(b), BT).then_inc(tile_done, 1)
                    at_end(g, b, t, first)

            pe.wait_ge(const, 1)
            pe.wait_ge(par_in, 16 * 3)
            some = slice(STATES_IN, STATES_IN + PARAMS)
            nc.tensor.transpose(T1[:, 0:PARAMS], prow[some, :], ident[some, some]).then_inc(t1_full, 1)
            for unit in range(1 + CH):
                x_round(unit, 0, 2 * unit)
                x_round(unit, 1, 2 * unit + 1)
                if unit == 1:
                    pe.wait_ge(g_low, 1)
                    gates(2, 0, MIX, 1)
            pe.wait_ge(states_in, 16 * 2)
            use_t1(2)
            nc.tensor.transpose(T1[:, 0:STATES_IN], prow[0:STATES_IN, :], ident[0:STATES_IN, 0:STATES_IN]).then_inc(t1_full, 1)
            gates(2 + 2 * CH, MIX, BT, 3)
            for b in range(NB - 1):
                pe_block(0, b, True)
            with pe.Fori(1, H) as g:
                pe_block(g - 1, NB - 1, False)
                for b in range(NB - 1):
                    pe_block(g, b, False)
            pe_block(H - 1, NB - 1, False)
            pe.wait_ge(n_free, NB * H)
            transposed(eh, t0(H, 0, "hT", False) - t0_uses(0, False).index("hT"))

            def b_tile(tile, n, slot, i, at):
                for h in range(2):
                    if not isinstance(tile, int):
                        pe.wait_ge(b_free, tile * 2 + (h - 2))
                    o = OUT[i][h][0:n, :]
                    for k in range(KT):
                        yh, yl = ybuf[slot][:, k, 0, at:at + n], ybuf[slot][:, k, 1, at:at + n]
                        wh, wl = Woh[:, k, h * BT:(h + 1) * BT], Wol[:, k, h * BT:(h + 1) * BT]
                        mm(o, yh, wh, start=(k == 0), stop=False)
                        mm(o, yh, wl, start=False, stop=False)
                        last = mm(o, yl, wh, start=False, stop=(k == KT - 1))
                    last.then_inc(b_full, 1)

            pe.wait_ge(wo_low, KT)
            pe.wait_ge(y_in[0], 16 * KT)
            pe.wait_ge(p_free[0], H * NT * NB // 2)
            pe.wait_ge(p_free[1], H * NT * NB // 2)
            pe.wait_ge(a_free, 3 * NB * H)
            pe.wait_ge(s_free, 3 * NB * H)
            b_tile(0, DB * DS, 0, 0, 0)
            pe.wait_ge(finals, 1)
            use_t1(T1_END)
            nc.tensor.transpose(T1[0:STATES_OUT, 0:P], par[:, 0:STATES_OUT], ident[:, :]).then_inc(t1_full, 1)
            with pe.Fori(0, NB) as j:
                for c in range(CH):
                    if c == 0:
                        pe.wait_ge(y_in[1], (j + 1) * 16 * KT)
                    if c == 2:
                        pe.wait_ge(y_in[0], (j + 2) * 16 * KT)
                    b_tile(j * CH + (1 + c), P, 1 - c // 2, (1 + c) % 2, (c % 2) * P)

        @block.scalar
        def _(act):
            order = Order(act, act_step, ACT_TURN)
            did, mark, fn = order.did, order.mark, order.after(nc.scalar.activation)

            def x_square(unit):
                n, s = (MIX if unit == 0 else P), unit % XBUF
                loads = unit // XBUF + (2 if s == 0 else 1)
                act.wait_ge(x_in[s], 16 * loads)
                mark(fn(junk[0:n, :], xs[s][0:n, :], ACT.Square, accum_out=ssx[0:n, unit:unit + 1]).then_inc(x_sq, 1), x_sq, unit + 1)

            def x_scale(unit):
                n, s = (MIX if unit == 0 else P), unit % XBUF
                act.wait_ge(x_rs, unit + 1)
                mark(fn(xs[s][0:n, :], xs[s][0:n, :], ACT.Copy, scale=rsx[0:n, unit:unit + 1]).then_inc(x_scaled, 1), x_scaled, unit + 1)

            def x_high_part(unit, r, count):
                n, tok = (MIX, 0) if unit == 0 else (P, MIX + (unit - 1) * P)
                i = 2 * unit + r
                act.wait_ge(t0_free, count + 1)
                mark(fn(xTh[:, 4 * r:4 * r + 4, tok:tok + n], xtmp[i % 2][:, 0:4 * n].rearrange("p (k t) -> p k t", k=4),
                   ACT.Copy).then_inc(x_high, 1), x_high, i + 1)

            def gate_logits(unit, n, count):
                act.wait_ge(t1_full, count + 1)
                if unit:
                    act.wait_ge(rows_ready, unit)
                mark(fn(grow[:, 0:n], T1[0:GR, 0:n], ACT.Identity, bias=biasg[:, :], scale=1.0 / WS).then_inc(g_logits, 1), g_logits, unit + 1)

            def gate_logs(unit, n):
                act.wait_ge(g_abs, unit + 1)
                mark(fn(gt[:, 0:n], gt[:, 0:n], ACT.Exp).then_inc(g_exp, 1), g_exp, unit + 1)
                mark(fn(gt[:, 0:n], gt[:, 0:n], ACT.Ln, bias=1.0).then_inc(g_ln, 1), g_ln, unit + 1)

            def columns_part(first_chunk, chunks_, n, count):
                act.wait_ge(t1_full, count + 1)
                src = T1[0:n, 0:64 * chunks_].rearrange("p (c k r) -> p c k r", k=2, r=32)[:, :, :, 0:H]
                for kind in range(2):
                    did(fn(cols[0:n, first_chunk:first_chunk + chunks_, kind, :], src[:, :, kind, :], ACT.Exp))
                if first_chunk == 0:
                    out = decs[:, :, :]
                else:
                    out = cols[:, first_chunk:first_chunk + chunks_, 2, :]
                k = DB if first_chunk == 0 else CH
                if first_chunk:
                    some = slice(first_chunk, first_chunk + chunks_)
                    a = T1[:, 0:64 * CH].rearrange("p (c r) -> p c r", r=64)[:, :, A_COL:A_COL + H]
                    did(fn(cols[:, some, 3, :], a, ACT.Copy))
                    did(fn(cols[:, some, 4, :], T1[:, 256 + CH * H:256 + 2 * CH * H].rearrange("p (c h) -> p c h", h=H), ACT.Copy))
                mark(fn(out, T1[:, 256:256 + k * H].rearrange("p (c h) -> p c h", h=H), ACT.Exp).then_inc(t1_free, 1), t1_free, count + 1)

            def split_w(g, t):
                act.wait_ge(w_in_s[t % STAGES], g * (16 * NT // STAGES) + 16 * (t // STAGES + 1))
                mark(fn(Wh[:, t, :, :], wst[t % STAGES][:, :, :], ACT.Copy, scale=WS).then_inc(w_high, 1), w_high, g * NT + (t + 1))

            def copy(out, src, scale):
                return fn(out, src, ACT.Copy, scale=scale)

            def mixed_start(g, b, t, first):
                count = t0(g, b, ("mix", t), first)
                src = T0[:, 0:MIX]
                if t in (HC, GB):
                    return
                act.wait_ge(t0_full, count + 1)
                if t == K:
                    mark(copy(kfm[:, :], src, SK / WS).then_inc(t0_free, 1), t0_free, count + 1)
                if t == V:
                    mark(copy(vfm[:, :], src, 1 / WS).then_inc(t0_free, 1), t0_free, count + 1)
                if t == Q:
                    act.wait_ge(mx_q, g)
                    mark(copy(qfm[:, :], src, 1 / WS).then_inc(t0_free, 1), t0_free, count + 1)
                if t == GC:
                    act.wait_ge(mx_gc_used, g)
                    mark(copy(gcm[:, :], src, 1 / WS).then_inc(t0_free, 1), t0_free, count + 1)
                if t == ZC:
                    act.wait_ge(mx_g, g)
                    mark(fn(tzm[:, :], src, ACT.Tanh, scale=0.5 / WS).then_inc(mx_tanh_zc, 1), mx_tanh_zc, g + 1)
                if t == O:
                    mark(fn(tom[:, :], src, ACT.Tanh, scale=0.5 / WS).then_inc(t0_free, 1), t0_free, count + 1)
                if t == ZM:
                    mark(fn(tzm[:, :], src, ACT.Tanh, scale=0.5 / WS).then_inc(mx_tanh_zm, 1), mx_tanh_zm, g + 1)

            def heads_high(g, b, count):
                n = nth(g, b)
                act.wait_ge(t0_free, count + 1)
                act.wait_ge(y_out_m, (n - 1) * 16)
                mark(fn(yst[:, 1, 0, :], dp[:, :], ACT.Copy).then_inc(ym_high, 1), ym_high, n)

            def at_half(g, b, t, first):
                if first and b == 0:
                    for tile in SPLIT_AT_HALF.get(t, ()):
                        split_w(0, tile)
                if t == V and not (first and b == 0):
                    heads_high(g, b, t0(g, b, "hT", first))
                if t == GC:
                    act.wait_ge(t0_full, t0(g, b, "vT", first) + 1)
                    mark(fn(v1[:, :, 0:P], chunks(T0[:, :]), ACT.Copy).then_inc(t0_free, 1), t0_free, t0(g, b, "vT", first) + 1)
                if t == GC and b == 0:
                    act.wait_ge(t1_full, t1(g, b, "args", first) + 1)
                    did(fn(dpm[:, :], T1[0:MIX, 0:MIX], ACT.Exp))
                    mark(fn(ehm[:, :], T1[:, P:P + MIX], ACT.Exp).then_inc(t1_free, 1), t1_free, t1(g, b, "args", first) + 1)
                if first:
                    for r in X_HALF.get(t, ()):
                        x_high_part(1 + CH * (b + 1) + r // 2, r % 2, t0(g, b, ("x", r), first))
                    if b == 0 and t == K:
                        columns_part(0, 1, MIX, t1(g, b, "mix cols", first))
                    if t == Q:
                        columns_part(1 + CH * b, CH, P, t1(g, b, "cols", first))
                    if t in X_SQUARE and (b or t != K):
                        x_square(1 + CH * (b + 1) + X_SQUARE[t])

            def evacuate(g, b, t):
                n = nth(g, b)
                i, left = evacuations(g, b, t)
                src, free = PB[i][:, :], p_free[i]
                if t in (HC, GB):
                    return
                act.wait_ge(tile_done, n * NT + (t + 1))
                if t == K:
                    mark(copy(kf[:, :], src, SK / WS).then_inc(free, 1), free, left + 1)
                if t == V:
                    mark(copy(vf[:, :], src, 1 / WS).then_inc(free, 1), free, left + 1)
                if t == Q:
                    act.wait_ge(q_scaled, n)
                    mark(copy(qf[:, :], src, 1 / WS).then_inc(free, 1), free, left + 1)
                if t == GC:
                    act.wait_ge(gc_used, n)
                    mark(copy(gcs[:, :], src, 1 / WS).then_inc(free, 1), free, left + 1)
                if t == ZC:
                    act.wait_ge(g_done, n)
                    mark(fn(tz[:, :], src, ACT.Tanh, scale=0.5 / WS).then_inc(tanh_zc, 1), tanh_zc, n + 1)
                if t == O:
                    mark(fn(to[:, :], src, ACT.Tanh, scale=0.5 / WS).then_inc(free, 1), free, left + 1)
                if t == ZM:
                    act.wait_ge(yc_ready, n + 1)
                    mark(fn(tz[:, :], src, ACT.Tanh, scale=0.5 / WS).then_inc(tanh_zm, 1), tanh_zm, n + 1)

            def at_end(g, b, t, first):
                n = nth(g, b)
                if t == Q:
                    act.wait_ge(ym_low, n)
                    act.wait_ge(sel_ready, n + 1)
                    for out, src, kind, full, free, value in ((dp, A, 3, a_full, a_free, n * 3 + 1),
                                                              (eh, N[0], 4, e_full, e_ready, n + 1)):
                        act.wait_ge(full, value)
                        for c in range(CH):
                            cc = slice(c * P, (c + 1) * P)
                            last = fn(out[:, cc], src[:, cc], ACT.Exp, bias=sel[:, c, kind:kind + 1])
                            if c < CH - 1:
                                did(last)
                        mark(last.then_inc(free, 1), free, value)
                if t == GB and b == 0:
                    act.wait_ge(mx_rec, g + 1)
                    mark(fn(junk[0:MIX, 0:P], T1[0:MIX, 0:P], ACT.Square, scale=hm[:, 1:2], accum_out=hm[:, 2:3]).then_inc(mx_sq, 1), mx_sq, g + 1)
                if t == ZC:
                    act.wait_ge(yc_ready, n + 1)
                    act.wait_ge(y_out_c, n * 16)
                    mark(fn(yst[:, 0, 0, :], yc[:, :], ACT.Copy).then_inc(yc_high, 1), yc_high, n + 1)
                    if b == 0:
                        act.wait_ge(mx_yc, g + 1)
                        act.wait_ge(mx_out_c, g * 16)
                        mark(fn(ystm[:, 0, 0, :], ycm[:, :], ACT.Copy).then_inc(mx_yc_high, 1), mx_yc_high, g + 1)
                if t == O:
                    act.wait_ge(rec_ready, n + 1)
                    for c in range(CH):
                        last = fn(junk[:, 0:P], N[c // 2][:, (c % 2) * DV1:(c % 2) * DV1 + P], ACT.Square,
                                  scale=rec[:, c:c + 1], accum_out=hss[:, c:c + 1])
                        if c < CH - 1:
                            did(last)
                    mark(last.then_inc(h_sq, 1), h_sq, n + 1)
                if first and t in X_SQUARE and (b or t != K):
                    x_scale(1 + CH * (b + 1) + X_SQUARE[t])
                if t == ZM and b == 0:
                    act.wait_ge(t1_free, t1(g, b, "hT", first) + 1)
                    act.wait_ge(mx_out_m, g * 16)
                    mark(fn(ystm[:, 1, 0, :], ymm[:, :], ACT.Copy).then_inc(mx_ym_high, 1), mx_ym_high, g + 1)
                if first:
                    if t == ZC:
                        gate_logits(b + 2, BT, t1(g, b, "gates", first))
                        gate_logs(b + 2, BT)
                    if t == ZM and b == NB - 2:
                        columns_part(1 + CH * (b + 1), CH, P, t1(g, b, "next cols", first))

            def x_end(b, t, first):
                for r in X_END.get(t, ()) if first else ():
                    x_high_part(1 + CH * (b + 1) + r // 2, r % 2, t0(0, b, ("x", r), first))
                if first and b == 0 and t == V:
                    split_w(0, STAGES)

            def act_block(g, b, first, following):
                if following == "weights":
                    act.wait_ge(w_low, (g + 1) * NT - 1)
                    load_w(act, g + 1, 0)
                    load_w(act, g + 1, 1)
                    act.wait_ge(cs_out, (g + 1) * 16)
                    load_states(act, g + 1)
                for t in range(NT):
                    if b == 0:
                        mixed_start(g, b, t, first)
                    at_half(g, b, t, first)
                    if t in (HC, GB):
                        x_end(b, t, first)
                    evacuate(g, b, t)
                    if t not in (HC, GB):
                        x_end(b, t, first)
                    at_end(g, b, t, first)
                    if following == "weights":
                        act.wait_ge(tile_done, nth(g, b) * NT + (t + 1))
                        split_w(g + 1, t)
                        if t < NT - 2:
                            act.wait_ge(w_low, (g + 1) * NT + t)
                            load_w(act, g + 1, t + 2)
                    if following == "output weights" and t < KT:
                        act.wait_ge(w_in_s[t % STAGES], 16 * (NT * H // STAGES + t // STAGES + 1))
                        mark(fn(Woh[:, :, t * P:(t + 1) * P], wst[t % STAGES][:, :, :], ACT.Copy, scale=WS).then_inc(wo_high, 1), wo_high, t + 1)

            load_rows(act, par_in, STATES_IN, norm_gain.rearrange("(k p) -> k p", p=P), mh_gain.rearrange("(h p) -> h p", p=P),
                      conv_w.rearrange("j (h p) -> (j h) p", p=P))
            act.dma_start(wgst[:, :, :], w_in[:, IG_COL:IG_COL + 2 * H].rearrange("(k p) c -> p k c", p=P)).then_inc(gate_in, 16)
            x_square(0)
            x_square(1)
            act.wait_ge(bias_clear, 1)
            act.dma_start(biasg[0:H, :], b_fgate.rearrange("(h o) -> h o", o=1)).then_inc(bias_in, 16)
            act.dma_start(biasg[32:GR, :], b_igate.rearrange("(h o) -> h o", o=1)).then_inc(bias_in, 16)
            act.dma_start(sm0[:, :], state_m.rearrange("b h -> h b")).then_inc(bias_in, 16)
            act.wait_ge(const, 1)
            act.wait_ge(gate_in, 16)
            did(fn(Wg[:, :, 0:H], wgst[:, :, H:2 * H], ACT.Copy, scale=WS))
            mark(fn(Wg[:, :, 32:GR], wgst[:, :, 0:H], ACT.Copy, scale=WS).then_inc(g_high, 1), g_high, 1)
            x_high_part(0, 0, 0)
            x_high_part(0, 1, 1)
            x_square(2)
            x_high_part(1, 0, 2)
            x_high_part(1, 1, 3)
            act.wait_ge(bias_in, 16 * 3)
            gate_logits(0, MIX, 1)
            x_square(3)
            x_high_part(2, 0, 4)
            x_high_part(2, 1, 5)
            x_square(4)
            x_high_part(3, 0, 6)
            x_high_part(3, 1, 7)
            gate_logs(0, MIX)
            x_high_part(4, 0, 8)
            x_high_part(4, 1, 9)
            split_w(0, 0)
            split_w(0, 1)
            split_w(0, 2)
            x_square(1 + CH)
            x_scale(1 + CH)
            gate_logits(1, BT, 3)
            gate_logs(1, BT)
            for b in range(NB - 1):
                act_block(0, b, True, None)
            with act.Fori(1, H) as g:
                order.enter(g)
                act_block(g - 1, NB - 1, False, "weights")
                for b in range(NB - 1):
                    act_block(g, b, False, None)
            order.leave(H - 1)
            act_block(H - 1, NB - 1, False, "output weights")
            heads_high(H, 0, t0(H, 0, "hT", False) - t0_uses(0, False).index("hT"))

            def b_tile(tile, n, i, c):
                act.wait_ge(b_free, tile * 2 + 2)
                mark(fn(junk[0:n, :], xs[i][0:n, :], ACT.Square, accum_out=ssx[0:n, c:c + 1]).then_inc(b_sq, 1), b_sq, tile + 1)

            b_tile(0, DB * DS, 0, 0)
            with act.Fori(0, NB) as j:
                for c in range(CH):
                    b_tile(j * CH + (1 + c), P, (1 + c) % 2, 1 + c)

        @block.vector
        def _(dve):
            order = Order(dve, dve_step, DVE_TURN)
            did, mark = order.did, order.mark
            tt, ts, stt, scan, copy, reciprocal, memset = (order.after(op) for op in (
                nc.vector.tensor_tensor, nc.vector.tensor_scalar, nc.vector.scalar_tensor_tensor,
                nc.vector.tensor_tensor_scan, nc.vector.tensor_copy, nc.vector.reciprocal, nc.vector.memset))

            def pick(out, src):
                return ts(out, src, 1.0, None, ALU.mult)

            def x_scale(unit):
                n, s = (MIX if unit == 0 else P), unit % XBUF
                dve.wait_ge(x_rs, unit + 1)
                mark(ts(xs[s][0:n, :], xs[s][0:n, :], rsx[0:n, unit:unit + 1], None, ALU.mult).then_inc(x_scaled, 1), x_scaled, unit + 1)

            def x_low_part(i):
                unit, r = divmod(i, 2)
                n, tok = (MIX, 0) if unit == 0 else (P, MIX + (unit - 1) * P)
                dve.wait_ge(x_high, i + 1)
                mark(tt(xTl[:, 4 * r:4 * r + 4, tok:tok + n], xtmp[i % 2][:, 0:4 * n].rearrange("p (k t) -> p k t", k=4),
                   xTh[:, 4 * r:4 * r + 4, tok:tok + n], ALU.subtract).then_inc(x_low, 1), x_low, i + 1)

            def x_gain(unit, r, count0):
                n, i = (MIX if unit == 0 else P), 2 * unit + r
                dve.wait_ge(t0_full, count0 + 1)
                mark(tt(xtmp[i % 2][:, 0:4 * n].rearrange("p (k t) -> p k t", k=4), x_bank(count0)[:, 0:4 * n].rearrange("p (k t) -> p k t", k=4),
                   wide(gain[:, 4 * r:4 * r + 4], n), ALU.mult).then_inc(t0_free, 1), t0_free, count0 + 1)

            def gate_abs(unit, n):
                dve.wait_ge(g_logits, unit + 1)
                count = GATE_COUNTS[unit]
                mark(stt(grow[:, 0:n], T1[64:64 + GR, 0:n], 1.0 / WS, grow[:, 0:n], ALU.mult, ALU.add).then_inc(t1_free, 1), t1_free, count + 1)
                f, t = grow[0:H, 0:n], gt[:, 0:n]
                mark(stt(t, f, -1.0, f, ALU.mult, ALU.min).then_inc(g_abs, 1), g_abs, unit + 1)

            def gate_scan(unit, tok, n):
                f, t = grow[0:H, 0:n], gt[:, 0:n]
                a = t if unit else rows[0:H, :]
                dve.wait_ge(g_ln, unit + 1)
                did(stt(lf[:, 0:n], f, 0.0, t, ALU.min, ALU.subtract))
                if unit:
                    did(scan(bcum[:, :], restart[:, :], lf[:, :], 0.0, ALU.mult, ALU.add))
                else:
                    did(scan(bcum[:, 0:MIX], remix[:, :], lf[:, 0:MIX], 0.0, ALU.mult, ALU.add))
                did(copy(t, grow[32:GR, 0:n]))
                did(tt(a, t, bcum[:, 0:n], ALU.subtract))
                for c in range(CH if unit else 1):
                    before, length = CH * (unit - 1) + c + 1 if unit else 0, P if unit else META
                    sl = slice(c * P, c * P + length)
                    did(scan(mrow[:, sl], a[:, sl], a[:, sl], mst[:, before:before + 1], ALU.max, ALU.max))
                    end = c * P + length - 1
                    did(tt(mst[:, before + 1:before + 2], bcum[:, end:end + 1], mrow[:, end:end + 1], ALU.add))

            def gate_turn(unit, tok, n):
                t = gt[:, 0:n]
                a = t if unit else rows[0:H, :]
                ends = (chunks(mrow[:, :])[:, :, P - 1], samples(mrow)[:, :, DS - 1])[unit == 0]
                if unit == 0:
                    did(copy(t, a))
                    did(tt(samples(t)[:, :, 0], samples(t)[:, :, 0], sm0[:, :], ALU.max))
                    did(scan(mrow[:, META:MIX], forget[:, :], t[:, META:MIX], 0.0, ALU.add, ALU.max))
                else:
                    dve.wait_ge(t1_free, COLS_COUNTS[unit - 1] + 1)
                if unit:
                    k = CH
                    before = mst[:, 1 + CH * (unit - 1):1 + CH * unit]
                    did(copy(arow[:, :], a))
                    did(tt(chunks(trr[32:GR, :]), chunks(a), wide(ends, P), ALU.subtract))
                    did(tt(drl[:, k * H:2 * k * H].rearrange("p (c h) -> p c h", h=H), wide(before, H), each_head(k), ALU.mult))
                else:
                    k, before = DB, sm0[:, :]
                    did(ts(rows[96:96 + H, 0:META], mrow[:, 0:META], -1.0, None, ALU.mult))
                    did(tt(samples(rows[96:96 + H, :]), wide(before, DS), samples(mrow), ALU.subtract))
                    did(ts(trr[32:GR, 0:META], a[:, 0:META], mrow[:, META - 1:META], None, ALU.subtract))
                    did(tt(samples(trr[32:GR, :]), samples(a), wide(ends, DS), ALU.subtract))
                    did(copy(rows[64:64 + H, :], mrow[:, 0:n]))
                did(stt(trr[0:H, 0:n], bcum[:, 0:n], -1.0, mrow[:, 0:n], ALU.mult, ALU.subtract))
                did(tt(rl[:, 0:k], before, ends, ALU.subtract))
                if unit == 0:
                    did(tt(smn[:, :], samples(bcum)[:, :, DS - 1], ends, ALU.add))
                mark(tt(drl[:, 0:k * H].rearrange("p (c h) -> p c h", h=H), wide(rl[:, 0:k], H), each_head(k), ALU.mult)
                     .then_inc(rows_ready, 1), rows_ready, unit + 1)

            def gate_parts(tok):
                block_of, rest = slice(tok, tok + BT), lf[:, :]
                did(copy(mparts[0:H, block_of], mrow[:, :]))
                did(tt(rest, mrow[:, :], mparts[0:H, block_of], ALU.subtract))
                did(copy(mpart[:, :], rest))
                did(copy(mparts[32:GR, block_of], mpart[:, :]))
                did(tt(mparts[64:64 + H, block_of], rest, mpart[:, :], ALU.subtract))

            def each_head(segments):
                return selh[0:H, :].unsqueeze(1).broadcast_to([H, segments, H])

            def split_w(g, t):
                dve.wait_ge(w_high, g * NT + (t + 1))
                mark(stt(Wl[:, t, :, :], wst[t % STAGES][:, :, :], WS, Wh[:, t, :, :], ALU.mult, ALU.subtract).then_inc(w_low, 1), w_low, g * NT + (t + 1))

            def mixed_conv(g):
                conv(ycm[:, 0:META], g, lambda j: um[:, j:j + META])
                conv(samples(ycm), g, lambda j: useg[:, :, j:j + DS])
                did(copy(u[:, 0:2], um[:, META:META + 2]))

            def conv(out, g, tap):
                did(ts(out, tap(0), cwt[:, bass.ds(g, 1), 0], None, ALU.mult))
                for j in (1, 2):
                    did(stt(out, tap(j), cwt[:, bass.ds(g, 1), j], out, ALU.mult, ALU.add))

            def mixed_start(g, b, t, first):
                at = t0(g, b, ("mix", t), first)
                src = T0[:, 0:MIX]
                if t == GC:
                    tt_ = pick(cs[:, :, P], nst[:, :, bass.ds(g, 1)].rearrange("p b o -> p (b o)"))
                    mark(tt_.then_inc(mx_n, 1), mx_n, g + 1)
                if t == HC:
                    dve.wait_ge(t0_full, at + 1)
                    dve.wait_ge(t0_free, t0(g, b, ("mix", GC), first) + 1)
                    states = cst[:, bass.ds(g, 1), :].rearrange("p o (b j) -> p (o b) j", j=2)
                    did(pick(useg[:, :, 0:2], states))
                    did(stt(um[:, 2:2 + META], src[:, 0:META], 1 / WS, gcm[:, 0:META], ALU.mult, ALU.mult))
                    mark(stt(useg[:, :, 2:], samples(src), 1 / WS, samples(gcm), ALU.mult, ALU.mult).then_inc(t0_free, 1), t0_free, at + 1)
                    dve.wait_ge(t0_free, at + 1)
                    mark(pick(states, useg[:, :, DS:DS + 2]).then_inc(mx_gc_used, 1), mx_gc_used, g + 1)
                if t == GB:
                    dve.wait_ge(t0_full, at + 1)
                    mark(stt(ycm[:, :], src, 1 / WS, ycm[:, :], ALU.mult, ALU.mult).then_inc(t0_free, 1), t0_free, at + 1)
                if t == ZC:
                    dve.wait_ge(mx_tanh_zc, g + 1)
                    mark(stt(zsm[:, :], tzm[:, :], 1.0, src, ALU.add, ALU.mult).then_inc(t0_free, 1), t0_free, at + 1)
                    dve.wait_ge(t0_free, at + 1)
                    mark(stt(ycm[:, :], ycm[:, :], 0.5 / WS, zsm[:, :], ALU.mult, ALU.mult).then_inc(mx_yc, 1), mx_yc, g + 1)
                if t == ZM:
                    dve.wait_ge(t0_free, t0(g, b, ("mix", O), first) + 1)
                    did(ts(tom[:, :], tom[:, :], 1.0, mhg[:, bass.ds(g, 1)], ALU.add, ALU.mult))
                    dve.wait_ge(mx_tanh_zm, g + 1)
                    mark(stt(zsm[:, :], tzm[:, :], 1.0, src, ALU.add, ALU.mult).then_inc(t0_free, 1), t0_free, at + 1)
                    dve.wait_ge(t0_free, at + 1)
                    mark(stt(Gm[:, :], tom[:, :], 0.25 / WS, zsm[:, :], ALU.mult, ALU.mult).then_inc(mx_g, 1), mx_g, g + 1)
                    dve.wait_ge(mx_g, g + 1)
                    dve.wait_ge(t1_full, t1(g, b, "hT", first) + 1)
                    mark(tt(ymm[:, :], T1[:, 0:MIX], Gm[:, :], ALU.mult).then_inc(t1_free, 1), t1_free, t1(g, b, "hT", first) + 1)

            def heads_out(g, b, at):
                n = nth(g, b)
                dve.wait_ge(t0_full, at + 1)
                dve.wait_ge(g_done, n)
                mark(tt(dp[:, :], T0[:, :], G[:, :], ALU.mult).then_inc(t0_free, 1), t0_free, at + 1)
                dve.wait_ge(ym_high, n)
                mark(tt(yst[:, 1, 1, :], dp[:, :], yst[:, 1, 0, :], ALU.subtract).then_inc(ym_low, 1), ym_low, n)

            def update(g, b, c):
                n = nth(g, b)
                kv, full, free = ((A, a_full, a_free), (S, s_full, s_free))[c % 2]
                dve.wait_ge(full, n * 3 + (2 + c // 2))
                mark(stt(cn[:, :], cn[:, :], sel[:, c, 2:3], kv[:, 0:DV1], ALU.mult, ALU.add).then_inc(free, 1), free, n * 3 + (2 + c // 2))

            def at_half(g, b, t, first):
                n = nth(g, b)
                if first and b == 0:
                    for tile in SPLIT_AT_HALF.get(t, ()):
                        split_w(0, tile)
                if t == V and not (first and b == 0):
                    heads_out(g, b, t0(g, b, "hT", first))
                if t == Q:
                    if first:
                        select(g, b, first)
                    dve.wait_ge(t0_full, t0(g, b, "kT", first) + 1)
                    mark(tt(chunks(kw[:, :]), chunks(T0[:, :]), wide(sel[:, :, 1], P), ALU.mult).then_inc(t0_free, 1), t0_free, t0(g, b, "kT", first) + 1)
                if t == GC and b == 0:
                    dve.wait_ge(t1_free, t1(g, b, "args", first) + 1)
                    mark(tt(qdiag, samples(ehm), samples(qfm), ALU.mult).then_inc(mx_q, 1), mx_q, g + 1)
                if t == ZC:
                    if b == 0:
                        dve.wait_ge(cn_meta, g + 1)
                    else:
                        dve.wait_ge(s_free, n * 3)
                    update(g, b, 0)
                if t == O:
                    dve.wait_ge(s_free, n * 3 + 2)
                    update(g, b, 2)
                    if first:
                        gate_scan(b + 2, tok0(b + 1), BT)
                        if b == NB - 2:
                            gate_turn(b + 2, tok0(b + 1), BT)
                if first:
                    for r in X_HALF.get(t, ()):
                        x_gain(1 + CH * (b + 1) + r // 2, r % 2, t0(g, b, ("x", r), first))
                        x_low_part(2 * (1 + CH * (b + 1)) + r)

            def evacuate(g, b, t):
                n = nth(g, b)
                i, left = evacuations(g, b, t)
                src, free = PB[i][:, :], p_free[i]
                if t == HC:
                    if b:
                        did(copy(u[:, 0:2], u[:, BT:BT + 2]))
                    dve.wait_ge(tile_done, n * NT + (t + 1))
                    j, before = evacuations(g, b, GC)
                    dve.wait_ge(p_free[j], before + 1)
                    mark(stt(u[:, 2:], src, 1 / WS, gcs[:, :], ALU.mult, ALU.mult).then_inc(free, 1), free, left + 1)
                    dve.wait_ge(free, left + 1)
                    mark(ts(yc[:, :], u[:, 0:BT], cwt[:, bass.ds(g, 1), 0], None, ALU.mult).then_inc(gc_used, 1), gc_used, n + 1)
                    dve.wait_ge(gc_used, n + 1)
                    did(stt(yc[:, :], u[:, 1:1 + BT], cwt[:, bass.ds(g, 1), 1], yc[:, :], ALU.mult, ALU.add))
                    did(stt(yc[:, :], u[:, 2:2 + BT], cwt[:, bass.ds(g, 1), 2], yc[:, :], ALU.mult, ALU.add))
                    if b == NB - 1:
                        did(pick(cpo[:, bass.ds(g, 1), :].rearrange("p o j -> p (o j)"), u[:, BT:BT + 2]))
                if t == GB:
                    dve.wait_ge(tile_done, n * NT + (t + 1))
                    mark(stt(yc[:, :], src, 1 / WS, yc[:, :], ALU.mult, ALU.mult).then_inc(free, 1), free, left + 1)
                if t == ZC:
                    j, before = evacuations(g, b, GB)
                    dve.wait_ge(p_free[j], before + 1)
                    dve.wait_ge(tanh_zc, n + 1)
                    mark(stt(zs[:, :], tz[:, :], 1.0, src, ALU.add, ALU.mult).then_inc(free, 1), free, left + 1)
                    dve.wait_ge(free, left + 1)
                    mark(stt(yc[:, :], yc[:, :], 0.5 / WS, zs[:, :], ALU.mult, ALU.mult).then_inc(yc_ready, 1), yc_ready, n + 1)
                if t == ZM:
                    j, before = evacuations(g, b, O)
                    dve.wait_ge(p_free[j], before + 1)
                    did(ts(to[:, :], to[:, :], 1.0, mhg[:, bass.ds(g, 1)], ALU.add, ALU.mult))
                    dve.wait_ge(tanh_zm, n + 1)
                    mark(stt(zs[:, :], tz[:, :], 1.0, src, ALU.add, ALU.mult).then_inc(free, 1), free, left + 1)
                    dve.wait_ge(free, left + 1)
                    mark(stt(G[:, :], to[:, :], 0.25 / WS, zs[:, :], ALU.mult, ALU.mult).then_inc(g_done, 1), g_done, n + 1)

            def select(g, b, first):
                n = nth(g, b)
                if first and b == 0:
                    dve.wait_ge(const2, 1)
                if first or b == NB - 1:
                    dve.wait_ge(t1_free, COLS_COUNTS[b + 1] + 1)
                dve.wait_ge(tile_done, n * NT + 1)
                dve.wait_ge(e_ready, n)
                if b == 0:
                    factors(g)
                mark(pick(sel[:, :, :], cols[:, 1 + CH * b:1 + CH * (b + 1), :, bass.ds(g, 1)].rearrange("p c k o -> p c (k o)"))
                     .then_inc(sel_ready, 1), sel_ready, n + 1)

            def factors(g):
                one = bass.ds(g, 1)
                did(ts(selneg[:, :], ones[0:64 + H, :], seln[0:64 + H, one], None, ALU.mult))
                did(pick(selm[:, :], cols[0:MIX, 0, 0:2, one].rearrange("p k o -> p (k o)")))
                did(pick(dselm[:, :], decs[:, :, one].rearrange("p k o -> p (k o)")))
                ts(rbm[0:H, :], ones[0:H, 0:MIX], selh[0:H, one], None, ALU.mult)
                ts(rbm[32:GR, :], rows[64:64 + H, :], seln[64:64 + H, one], None, ALU.mult)
                did(ts(rbm[64:64 + H, :], rows[96:96 + H, :], selh[96:96 + H, one], None, ALU.mult))

            def at_end(g, b, t, first):
                n = nth(g, b)
                if t == K and not first:
                    select(g, b, first)
                if t == Q:
                    dve.wait_ge(e_ready, n + 1)
                    mark(tt(eh[:, :], eh[:, :], qf[:, :], ALU.mult).then_inc(q_scaled, 1), q_scaled, n + 1)
                if t == GC:
                    dve.wait_ge(s_full, n * 3 + 1)
                    dve.wait_ge(a_free, n * 3 + 1)
                    mark(tt(dp[:, :], dp[:, :], S[:, :], ALU.mult).then_inc(s_free, 1), s_free, n * 3 + 1)
                if t == ZC:
                    dve.wait_ge(a_free, n * 3 + 2)
                    update(g, b, 1)
                    dve.wait_ge(yc_high, n + 1)
                    mark(tt(yst[:, 0, 1, :], yc[:, :], yst[:, 0, 0, :], ALU.subtract).then_inc(yc_low, 1), yc_low, n + 1)
                if t == O:
                    dve.wait_ge(a_free, n * 3 + 3)
                    update(g, b, 3)
                    if b == NB - 1:
                        dve.wait_ge(s_free, n * 3 + 3)
                        did(pick(npo[:, bass.ds(g, 1)], cn[:, P:DV1]))
                    dve.wait_ge(n_full, n + 1)
                    for i in range(2):
                        nv = N[i][:, 0:2 * DV1].rearrange("p (c v) -> p c v", c=2)
                        did(copy(den[:, 2 * i:2 * i + 2], nv[:, :, P]))
                    did(stt(den[:, :], den[:, :], -1.0, den[:, :], ALU.mult, ALU.max))
                    did(tt(den[:, :], den[:, :], sel[:, :, 0], ALU.max))
                    mark(reciprocal(rec[:, :], den[:, :]).then_inc(rec_ready, 1), rec_ready, n + 1)
                    dve.wait_ge(h_sq, n + 1)
                    mark(ts(hms[:, :], hss[:, :], 1.0 / P, EPS, ALU.mult, ALU.add).then_inc(h_ms, 1), h_ms, n + 1)
                    dve.wait_ge(h_rs, n + 1)
                    did(tt(hf[:, :], rec[:, :], hrs[:, :], ALU.mult))
                    for i in range(2):
                        nv = N[i][:, 0:2 * DV1].rearrange("p (c v) -> p c v", c=2)[:, :, 0:P]
                        last = tt(eh[:, 2 * P * i:2 * P * (i + 1)].rearrange("p (c v) -> p c v", c=2), nv,
                                  wide(hf[:, 2 * i:2 * i + 2], P), ALU.mult)
                    mark(last.then_inc(n_free, 1), n_free, n + 1)
                if b == 0:
                    mixed_end(g, b, t, first)
                if b == 1 and t in (V, Q, GC):
                    i0, i1 = SAMPLE_ROUNDS[t - V]
                    at = t1(g, b, ("state", t - V), first)
                    dve.wait_ge(t1_full, at + 1)
                    for i in range(i0, i1):
                        ins = stt(cs[:, i, :], cs[:, i, :], dselm[:, i:i + 1], T1[:, (i - i0) * DV1:(i - i0 + 1) * DV1], ALU.mult, ALU.add)
                        if i == i1 - 1:
                            mark(ins.then_inc(t1_free, 1), t1_free, at + 1)
                        else:
                            did(ins)
                    if t == GC:
                        dve.wait_ge(t1_free, at + 1)
                        mark(pick(nst[:, :, bass.ds(g, 1)].rearrange("p b o -> p (b o)"), cs[:, :, P]).then_inc(mx_states, 1), mx_states, g + 1)
                if first:
                    if t == ZC:
                        gate_abs(b + 2, BT)
                    if t == ZM and b < NB - 2:
                        gate_turn(b + 2, tok0(b + 1), BT)
                    if t == V:
                        gate_parts(tok0(b))
                    if t == ZM and b == NB - 2:
                        gate_parts(tok0(b + 1))

            def mixed_end(g, b, t, first):
                if t == GC:
                    at = t1(g, b, "kv", first)
                    dve.wait_ge(t1_full, at + 1)
                    did(ts(kwm[:, :], T1[0:MIX, 0:P], selm[:, 1:2], None, ALU.mult))
                    mark(copy(v1m[:, 0:P], T1[0:MIX, P:2 * P]).then_inc(t1_free, 1), t1_free, at + 1)
                if t == HC:
                    at = t1(g, b, "score", first)
                    dve.wait_ge(t1_full, at + 1)
                    mark(tt(dpm[:, :], dpm[:, :], T1[0:MIX, 0:MIX], ALU.mult).then_inc(t1_free, 1), t1_free, at + 1)
                if t == O:
                    mark(tt(v1x[:, :, :], v1m[:, :].unsqueeze(1).broadcast_to([MIX, DB, DV1]), wide(segind[:, :], DV1), ALU.mult)
                         .then_inc(mx_v_wide, 1), mx_v_wide, g + 1)
                if t == GB:
                    at = t1(g, b, "num", first)
                    dve.wait_ge(t1_full, at + 1)
                    dve.wait_ge(cn_out, g * 16)
                    mark(copy(cn[:, :], T1[:, 2 * P:2 * P + DV1]).then_inc(cn_meta, 1), cn_meta, g + 1)
                    did(copy(hm[:, 0:1], T1[0:MIX, P:DV1]))
                    did(stt(hm[:, 0:1], hm[:, 0:1], -1.0, hm[:, 0:1], ALU.mult, ALU.max))
                    did(tt(hm[:, 0:1], hm[:, 0:1], selm[:, 0:1], ALU.max))
                    mark(reciprocal(hm[:, 1:2], hm[:, 0:1]).then_inc(mx_rec, 1), mx_rec, g + 1)
                    dve.wait_ge(mx_sq, g + 1)
                    mark(ts(hm[:, 3:4], hm[:, 2:3], 1.0 / P, EPS, ALU.mult, ALU.add).then_inc(mx_ms, 1), mx_ms, g + 1)
                    dve.wait_ge(mx_rs, g + 1)
                    did(tt(hm[:, 5:6], hm[:, 1:2], hm[:, 4:5], ALU.mult))
                    mark(ts(hnm[:, :], T1[0:MIX, 0:P], hm[:, 5:6], None, ALU.mult).then_inc(t1_free, 1), t1_free, at + 1)
                if t == ZC:
                    dve.wait_ge(mx_yc_high, g + 1)
                    mark(tt(ystm[:, 0, 1, :], ycm[:, :], ystm[:, 0, 0, :], ALU.subtract).then_inc(mx_yc_low, 1), mx_yc_low, g + 1)
                if t == ZM:
                    dve.wait_ge(mx_ym_high, g + 1)
                    mark(tt(ystm[:, 1, 1, :], ymm[:, :], ystm[:, 1, 0, :], ALU.subtract).then_inc(mx_ym_low, 1), mx_ym_low, g + 1)

            def dve_block(g, b, first, following):
                for t in range(NT):
                    if b == 0:
                        mixed_start(g, b, t, first)
                    at_half(g, b, t, first)
                    if first:
                        for r in X_END.get(t, ()):
                            x_gain(1 + CH * (b + 1) + r // 2, r % 2, t0(g, b, ("x", r), first))
                        if b == 0 and t == V:
                            split_w(0, STAGES)
                    if b == 0 and t == HC:
                        mixed_conv(g)
                    evacuate(g, b, t)
                    if first:
                        for r in X_END.get(t, ()):
                            x_low_part(2 * (1 + CH * (b + 1)) + r)
                    at_end(g, b, t, first)
                    if following == "weights":
                        split_w(g + 1, t)
                    if following == "output weights" and t < KT:
                        dve.wait_ge(wo_high, t + 1)
                        mark(stt(Wol[:, :, t * P:(t + 1) * P], wst[t % STAGES][:, :, :], WS, Woh[:, :, t * P:(t + 1) * P],
                            ALU.mult, ALU.subtract).then_inc(wo_low, 1), wo_low, t + 1)

            GATE_COUNTS = [1, 3] + [t1(0, b, "gates", True) for b in range(NB - 1)]
            COLS_COUNTS = ([t1(0, 0, "mix cols", True)] + [t1(0, b, "cols", True) for b in range(NB - 1)] +
                           [t1(0, NB - 2, "next cols", True)])

            dve.wait_ge(const, 1)
            x_scale(0)
            dve.wait_ge(t1_full, 1)
            mark(copy(par[:, STATES_OUT:], T1[:, 0:PARAMS]).then_inc(t1_free, 1), t1_free, 1)
            x_gain(0, 0, 0)
            x_gain(0, 1, 1)
            x_scale(1)
            x_low_part(0)
            x_low_part(1)
            dve.wait_ge(g_high, 1)
            did(stt(Wg[:, :, 64:64 + H], wgst[:, :, H:2 * H], WS, Wg[:, :, 0:H], ALU.mult, ALU.subtract))
            mark(stt(Wg[:, :, 96:96 + H], wgst[:, :, 0:H], WS, Wg[:, :, 32:GR], ALU.mult, ALU.subtract).then_inc(g_low, 1), g_low, 1)
            x_gain(1, 0, 2)
            x_gain(1, 1, 3)
            x_scale(2)
            x_low_part(2)
            x_low_part(3)
            x_gain(2, 0, 4)
            x_gain(2, 1, 5)
            x_scale(3)
            x_low_part(4)
            x_low_part(5)
            x_gain(3, 0, 6)
            x_gain(3, 1, 7)
            x_scale(4)
            dve.wait_ge(rows_const, 1)
            dve.wait_ge(bias_in, 16 * 3)
            gate_abs(0, MIX)
            x_low_part(6)
            x_low_part(7)
            x_gain(4, 0, 8)
            x_gain(4, 1, 9)
            did(memset(selh[:, :], 0.0))
            for q in range(4):
                did(copy(selh[32 * q:32 * q + H, :], ident[32 * q:32 * q + H, 32 * q:32 * q + H]))
            x_low_part(8)
            x_low_part(9)
            dve.wait_ge(t1_full, 3)
            mark(copy(par[:, 0:STATES_IN], T1[:, 0:STATES_IN]).then_inc(t1_free, 1), t1_free, 3)
            split_w(0, 0)
            gate_scan(0, 0, MIX)
            gate_turn(0, 0, MIX)
            split_w(0, 1)
            split_w(0, 2)
            did(copy(identb[:, :], ident[:, :]))
            did(ts(seln[:, :], selh[:, :], -1.0, None, ALU.mult))
            gate_abs(1, BT)
            gate_scan(1, MIX, BT)
            gate_turn(1, MIX, BT)
            for b in range(NB - 1):
                dve_block(0, b, True, None)
            with dve.Fori(1, H) as g:
                order.enter(g)
                dve_block(g - 1, NB - 1, False, "weights")
                for b in range(NB - 1):
                    dve_block(g, b, False, None)
            order.leave(H - 1)
            dve_block(H - 1, NB - 1, False, "output weights")
            heads_out(H, 0, t0(H, 0, "hT", False) - t0_uses(0, False).index("hT"))
            mark(memset(den[:, 0:1], 0.0).then_inc(finals, 1), finals, 1)

            def b_tile(tile, n, i, c, half_count):
                dve.wait_ge(r_in[i], half_count * 16 + 16)
                for h in range(2):
                    dve.wait_ge(b_full, tile * 2 + (h + 1))
                    z = xs[i][0:n, h * BT:(h + 1) * BT]
                    mark(stt(z, OUT[i][h][0:n, :], 1 / WS, z, ALU.mult, ALU.add).then_inc(b_free, 1), b_free, tile * 2 + (h + 1))
                dve.wait_ge(b_sq, tile + 1)
                mark(ts(msx[0:n, c:c + 1], ssx[0:n, c:c + 1], 1.0 / D, EPS, ALU.mult, ALU.add).then_inc(b_ms, 1), b_ms, tile + 1)
                dve.wait_ge(b_rs, tile + 1)
                dve.wait_ge(b_store[i], half_count * 16)
                mark(stt(result[i][0:n, :], xs[i][0:n, :], rsx[0:n, c:c + 1], fgain[0:n, :], ALU.mult, ALU.mult).then_inc(b_out, 1), b_out, tile + 1)

            dve.wait_ge(fg_in, 16)
            b_tile(0, DB * DS, 0, 0, 0)
            dve.wait_ge(t1_full, T1_END + 1)
            mark(copy(prow[0:STATES_OUT, :], T1[0:STATES_OUT, 0:P]).then_inc(rows_out, 1), rows_out, 1)
            with dve.Fori(0, NB) as j:
                for c in range(CH):
                    b_tile(j * CH + (1 + c), P, (1 + c) % 2, 1 + c, j * 2 + (1 + c) // 2)


_INS = ['x_prompt', 'x_sample', 'state_conv', 'state_mlstm_c', 'state_mlstm_n', 'state_mlstm_m', 'meta_tokens',
        'norm_gain', 'w_in', 'conv_w', 'b_igate', 'b_fgate', 'mh_norm_gain', 'w_out', 'final_norm_gain']
_OUTS = [(1, SEQ, D), (DB, DS, D), (1, 2, CW), (1, H, P, P), (1, H, P), (1, H),
         (DB, 2, CW), (DB, H, P, P), (DB, H, P), (DB, H)]


def kernel(**inputs):
    import numpy as _np
    import concourse.bacc as _bacc
    from concourse import mybir as _mybir
    from concourse.bass_utils import run_bass_kernel_spmd as _run

    nc = _bacc.Bacc("TRN2", target_bir_lowering=False, num_devices=1)
    arrays, args = {}, []
    for name in _INS:
        a = _np.ascontiguousarray(inputs[name])
        arrays[f"in_{name}"] = a
        args.append(nc.dram_tensor(f"in_{name}", a.shape, _mybir.dt.from_np(a.dtype), kind="ExternalInput").ap())
    for i, shape in enumerate(_OUTS):
        args.append(nc.dram_tensor(f"out_{i}", shape, _mybir.dt.float32, kind="ExternalOutput").ap())
    args.append(nc.dram_tensor("y_mid", (KT, P, 2, NTOK), _mybir.dt.float16, kind="Internal").ap())
    build(nc, *args)
    r = _run(nc, [arrays], core_ids=[0])
    return tuple(r.results[0][f"out_{i}"] for i in range(len(_OUTS)))
```
